# Optimizing a Trainium2 kernel written in Bass

```python
import jax, jax.numpy as jnp
from jax import lax
import numpy as np

D_MODEL = 2048
BATCH = 1
SEQ = 256
DEPTH = 1

MIX_WIDTH = D_MODEL
HEAD_DIM = 128
SB_HEADS = 8
SB_WIDTH = SB_HEADS * HEAD_DIM
SB_BLOCK = 128
GLA_HEADS = 4
GLA_HEAD_V = HEAD_DIM
GLA_HEAD_K = HEAD_DIM // 2
GLA_WIDTH = GLA_HEADS * GLA_HEAD_V
GLA_KEY_WIDTH = GLA_HEADS * GLA_HEAD_K
GLA_GATE_RANK = 16
GLA_GATE_TAU = 16.0
GLA_CHUNK = 64
SGU_GROUPS = 4
SGU_WIDTH = MIX_WIDTH - SB_WIDTH - GLA_WIDTH
SGU_GROUP_DIM = SGU_WIDTH // SGU_GROUPS
SGU_CHUNK = 128
N_MIX_HEADS = MIX_WIDTH // HEAD_DIM
N_MEM = 256
XA_HEADS = 4
XA_HEAD_DIM = 128
XA_WIDTH = XA_HEADS * XA_HEAD_DIM
EPS = 1e-6

IN_SPLITS = [SB_WIDTH, SB_WIDTH, SB_WIDTH, SB_WIDTH,
             GLA_KEY_WIDTH, GLA_KEY_WIDTH, GLA_WIDTH, GLA_GATE_RANK, GLA_WIDTH,
             SGU_WIDTH, SGU_WIDTH, SGU_WIDTH]
IN_WIDTH = sum(IN_SPLITS)
IN_OFFSETS = [int(o) for o in np.cumsum(IN_SPLITS)[:-1]]


def rmsnorm(x, g):
    xf = x.astype(jnp.float32)
    y = xf * lax.rsqrt(jnp.mean(xf * xf, axis=-1, keepdims=True) + EPS)
    return (y * g.astype(jnp.float32)).astype(x.dtype)

def to_heads(t, n_heads):
    b, s, _ = t.shape
    return t.reshape(b, s, n_heads, -1).transpose(0, 2, 1, 3)

def from_heads(t):
    b, h, s, d = t.shape
    return t.transpose(0, 2, 1, 3).reshape(b, s, h * d)

def stick_breaking_attention(q, k, v):
    B, H, S, d = q.shape
    nblk = S // SB_BLOCK
    scale = d ** -0.5
    qb = q.reshape(B, H, nblk, SB_BLOCK, d).transpose(2, 0, 1, 3, 4)
    key_pos = jnp.arange(S)

    def block(args):
        q_blk, i = args
        z = jnp.einsum('bhqd,bhkd->bhqk', q_blk, k).astype(jnp.float32) * scale
        q_pos = i * SB_BLOCK + jnp.arange(SB_BLOCK)
        causal = key_pos[None, :] < q_pos[:, None]
        log_keep = jnp.where(causal, jax.nn.log_sigmoid(-z), 0.0)
        suffix = lax.cumsum(log_keep, axis=3, reverse=True) - log_keep
        a = jnp.where(causal, jnp.exp(jax.nn.log_sigmoid(z) + suffix), 0.0)
        return jnp.einsum('bhqk,bhkd->bhqd', a.astype(v.dtype), v)

    out = lax.map(block, (qb, jnp.arange(nblk)))
    return out.transpose(1, 2, 0, 3, 4).reshape(B, H, S, d)

def gla_chunked(q, k, v, log_alpha):
    B, H, S, dk = q.shape
    dv = v.shape[-1]
    C = GLA_CHUNK
    N = S // C
    qc = q.reshape(B, H, N, C, dk).astype(jnp.float32) * (dk ** -0.5)
    kc = k.reshape(B, H, N, C, dk).astype(jnp.float32)
    vc = v.reshape(B, H, N, C, dv).astype(jnp.float32)
    bcum = jnp.cumsum(log_alpha.reshape(B, H, N, C, dk).astype(jnp.float32), axis=3)
    tril = jnp.tril(jnp.ones((C, C), dtype=bool))
    rel = bcum[:, :, :, :, None, :] - bcum[:, :, :, None, :, :]
    decay = jnp.exp(jnp.where(tril[:, :, None], rel, -jnp.inf))
    attn = jnp.einsum('bhntd,bhnsd,bhntsd->bhnts', qc, kc, decay)
    o_intra = jnp.einsum('bhnts,bhnsv->bhntv', attn, vc)
    q_dec = qc * jnp.exp(bcum)
    b_last = bcum[:, :, :, -1:, :]
    k_dec = kc * jnp.exp(b_last - bcum)
    chunk_decay = jnp.exp(b_last[:, :, :, 0, :])
    xs = (jnp.moveaxis(q_dec, 2, 0), jnp.moveaxis(k_dec, 2, 0),
          jnp.moveaxis(vc, 2, 0), jnp.moveaxis(chunk_decay, 2, 0))

    def step(state, inp):
        qn, kn, vn, dn = inp
        o = jnp.einsum('bhtd,bhdv->bhtv', qn, state)
        state = dn[..., None] * state + jnp.einsum('bhsd,bhsv->bhdv', kn, vn)
        return state, o

    state0 = jnp.zeros((B, H, dk, dv), jnp.float32)
    _, o_inter = lax.scan(step, state0, xs)
    o = o_intra + jnp.moveaxis(o_inter, 0, 2)
    return o.reshape(B, H, S, dv).astype(v.dtype)

def chunked_sgu(u, v, g_norm, w_s, b_s):
    B, S, _ = v.shape
    N = S // SGU_CHUNK
    v = rmsnorm(v, g_norm)
    vb = v.reshape(B, N, SGU_CHUNK, SGU_GROUPS, SGU_GROUP_DIM)
    w = w_s * jnp.tril(jnp.ones((SGU_CHUNK, SGU_CHUNK), w_s.dtype))[None]
    mixed = jnp.einsum('gts,bnsgc->bntgc', w, vb) + b_s.T[None, None, :, :, None]
    return u * mixed.reshape(B, S, SGU_WIDTH)

def memory_cross_attention(h, m, w_q, w_kv, w_o):
    B, S, _ = h.shape
    q = (h @ w_q).reshape(B, S, XA_HEADS, XA_HEAD_DIM)
    k, v = jnp.split(m @ w_kv, 2, axis=-1)
    k = k.reshape(B, -1, XA_HEADS, XA_HEAD_DIM)
    v = v.reshape(B, -1, XA_HEADS, XA_HEAD_DIM)
    s = jnp.einsum('bqhd,bkhd->bhqk', q, k).astype(jnp.float32) * (XA_HEAD_DIM ** -0.5)
    p = jax.nn.softmax(s, axis=-1).astype(v.dtype)
    o = jnp.einsum('bhqk,bkhd->bqhd', p, v).reshape(B, S, XA_WIDTH)
    return o @ w_o

def first_inputs(seed: int = 0) -> dict:
    key = jax.random.key(seed)
    ks = jax.random.split(key, 17)
    f32 = jnp.float32
    nrm = lambda k, shape, s: jax.random.normal(k, shape, f32) * s
    return {
        "x": nrm(ks[0], (BATCH, SEQ, D_MODEL), 1.0),
        "mem": nrm(ks[1], (BATCH, N_MEM, D_MODEL), 1.0),
        "norm_mix": 1.0 + nrm(ks[2], (DEPTH, D_MODEL), 0.02),
        "w_in": nrm(ks[3], (DEPTH, D_MODEL, IN_WIDTH), D_MODEL ** -0.5),
        "w_gla_gate_up": nrm(ks[4], (DEPTH, GLA_GATE_RANK, GLA_KEY_WIDTH), GLA_GATE_RANK ** -0.5),
        "b_gla_gate": nrm(ks[5], (DEPTH, GLA_KEY_WIDTH), 0.1),
        "sgu_norm": 1.0 + nrm(ks[6], (DEPTH, SGU_WIDTH), 0.02),
        "w_sgu": nrm(ks[7], (DEPTH, SGU_GROUPS, SGU_CHUNK, SGU_CHUNK), SGU_CHUNK ** -0.5),
        "b_sgu": 1.0 + nrm(ks[8], (DEPTH, SGU_GROUPS, SGU_CHUNK), 0.1),
        "out_norm": 1.0 + nrm(ks[9], (DEPTH, MIX_WIDTH), 0.02),
        "w_out": nrm(ks[10], (DEPTH, MIX_WIDTH, D_MODEL), MIX_WIDTH ** -0.5),
        "norm_xattn": 1.0 + nrm(ks[11], (DEPTH, D_MODEL), 0.02),
        "norm_mem": 1.0 + nrm(ks[12], (DEPTH, D_MODEL), 0.02),
        "w_xq": nrm(ks[13], (DEPTH, D_MODEL, XA_WIDTH), D_MODEL ** -0.5),
        "w_xkv": nrm(ks[14], (DEPTH, D_MODEL, 2 * XA_WIDTH), D_MODEL ** -0.5),
        "w_xo": nrm(ks[15], (DEPTH, XA_WIDTH, D_MODEL), XA_WIDTH ** -0.5),
        "final_norm": 1.0 + nrm(ks[16], (D_MODEL,), 0.02),
    }

def first_block(x, mem, norm_mix, w_in, w_gla_gate_up, b_gla_gate, sgu_norm, w_sgu, b_sgu,
              out_norm, w_out, norm_xattn, norm_mem, w_xq, w_xkv, w_xo, final_norm):
    B, S, _ = x.shape
    for l in range(DEPTH):
        h = rmsnorm(x, norm_mix[l])
        (sb_q, sb_k, sb_v, sb_g,
         gla_q, gla_k, gla_v, gla_r, gla_g,
         sgu_u, sgu_v, sgu_g) = jnp.split(h @ w_in[l], IN_OFFSETS, axis=-1)

        o_sb = from_heads(stick_breaking_attention(
            to_heads(sb_q, SB_HEADS), to_heads(sb_k, SB_HEADS), to_heads(sb_v, SB_HEADS)))

        gate_logits = (gla_r @ w_gla_gate_up[l] + b_gla_gate[l]).astype(jnp.float32)
        log_alpha = jax.nn.log_sigmoid(gate_logits) / GLA_GATE_TAU
        o_gla = from_heads(gla_chunked(
            to_heads(gla_q, GLA_HEADS), to_heads(gla_k, GLA_HEADS),
            to_heads(gla_v, GLA_HEADS), to_heads(log_alpha, GLA_HEADS)))

        o_sgu = chunked_sgu(jax.nn.gelu(sgu_u), jax.nn.gelu(sgu_v), sgu_norm[l], w_sgu[l], b_sgu[l])

        mix = jnp.concatenate([o_sb, o_gla, o_sgu], axis=-1)
        mix = rmsnorm(mix.reshape(B, S, N_MIX_HEADS, HEAD_DIM),
                      out_norm[l].reshape(N_MIX_HEADS, HEAD_DIM)).reshape(B, S, MIX_WIDTH)
        gate = jax.nn.silu(jnp.concatenate([sb_g, gla_g, sgu_g], axis=-1))
        x = x + (mix * gate) @ w_out[l]
        x = x + memory_cross_attention(rmsnorm(x, norm_xattn[l]), rmsnorm(mem, norm_mem[l]),
                                       w_xq[l], w_xkv[l], w_xo[l])
    return rmsnorm(x, final_norm)


DEPTH_2 = 2

CHUNK = 64
N_A_LAYERS = DEPTH_2 // 2
N_B_LAYERS = DEPTH_2 - N_A_LAYERS
RWKV_HEAD = 64
RWKV_HEADS = D_MODEL // RWKV_HEAD
DECAY_LORA = 96
AAA_LORA = 96
MV_LORA = 64
GATE_LORA = 256
N_MIX = 6
LNX_EPS = 1e-5 * RWKV_HEAD
FOX_HEAD = 128
FOX_HEADS = D_MODEL // FOX_HEAD
Q_BLOCK = 128
D_FF = 4 * D_MODEL
RMS_EPS = 1e-6


def rms_norm(x, gain):
    xf = x.astype(jnp.float32)
    y = xf * lax.rsqrt(jnp.mean(xf * xf, axis=-1, keepdims=True) + RMS_EPS)
    return (y * gain.astype(jnp.float32)).astype(x.dtype)

def squared_relu_mlp(h, w_up, w_down):
    return jnp.square(jax.nn.relu(h @ w_up)) @ w_down

def rwkv7_recurrence(r, decay, k, v, a, b):
    B, S, H, N = r.shape
    n_chunks = S // CHUNK

    def to_chunks(t):
        return t.reshape(B, n_chunks, CHUNK, H, N).transpose(1, 2, 0, 3, 4)

    def step(state, inp):
        r_t, w_t, k_t, v_t, a_t, b_t = inp
        sa = jnp.einsum('bhvk,bhk->bhv', state, a_t)
        state = (state * w_t[:, :, None, :]
                 + sa[..., None] * b_t[:, :, None, :]
                 + v_t[..., None] * k_t[:, :, None, :])
        y_t = jnp.einsum('bhvk,bhk->bhv', state, r_t)
        return state, y_t

    def chunk_step(state, chunk_inp):
        return lax.scan(step, state, chunk_inp)

    state0 = jnp.zeros((B, H, N, N), jnp.float32)
    inputs = (to_chunks(r), to_chunks(decay), to_chunks(k), to_chunks(v), to_chunks(a), to_chunks(b))
    _, y = lax.scan(chunk_step, state0, inputs)
    return y.transpose(2, 0, 1, 3, 4).reshape(B, S, H, N)

def rwkv7_time_mix(h, x_mix, w_rkv, w0, w1, w2, a0, a1, a2, g1, g2, k_k, k_a, r_k,
                   lnx_w, lnx_b, w_o, v_first, v_res):
    B, S, D = h.shape
    H, N = RWKV_HEADS, RWKV_HEAD
    f32 = jnp.float32
    prev = jnp.pad(h, ((0, 0), (1, 0), (0, 0)))[:, :S]
    xs = h[:, :, None, :] + (prev - h)[:, :, None, :] * x_mix
    rkv = jnp.einsum('bsnd,nde->bsne', xs[:, :, :3], w_rkv)
    r, k, v = rkv[:, :, 0], rkv[:, :, 1], rkv[:, :, 2]
    xv, xw, xa, xg = xs[:, :, 2], xs[:, :, 3], xs[:, :, 4], xs[:, :, 5]

    w_log = -jax.nn.softplus(-(w0 + jnp.tanh(xw @ w1) @ w2).astype(f32)) - 0.5
    decay = jnp.exp(-jnp.exp(w_log))
    if v_res is None:
        v_first = v
    else:
        v0, v1, v2 = v_res
        v = v + (v_first - v) * jax.nn.sigmoid(v0 + (xv @ v1) @ v2)
    a = jax.nn.sigmoid((a0 + (xa @ a1) @ a2).astype(f32))
    g = jax.nn.sigmoid(xg @ g1) @ g2

    heads = lambda t: t.astype(f32).reshape(B, S, H, N)
    kk = heads(k * k_k)
    kk = kk / jnp.maximum(jnp.sqrt(jnp.sum(kk * kk, axis=-1, keepdims=True)), 1e-12)
    k = k.astype(f32) * (1.0 + (a - 1.0) * k_a.astype(f32))
    rh, kh, vh, ah, dh = heads(r), heads(k), heads(v), heads(a), heads(decay)

    y = rwkv7_recurrence(rh, dh, kh, vh, -kk, kk * ah)
    mu = jnp.mean(y, axis=-1, keepdims=True)
    var = jnp.mean(jnp.square(y - mu), axis=-1, keepdims=True)
    y = ((y - mu) * lax.rsqrt(var + LNX_EPS)).reshape(B, S, D)
    y = y * lnx_w.astype(f32) + lnx_b.astype(f32)
    bonus = jnp.sum(rh * kh * r_k.astype(f32), axis=-1, keepdims=True) * vh
    y = y + bonus.reshape(B, S, D)
    out = (y * g.astype(f32)).astype(w_o.dtype) @ w_o
    return out.astype(h.dtype), v_first

def shared_kv_forget(x, kv_norm, w_kvf, b_f):
    B, S, D = x.shape
    proj = rms_norm(x, kv_norm) @ w_kvf
    k = proj[..., :D].reshape(B, S, FOX_HEADS, FOX_HEAD).transpose(0, 2, 1, 3)
    v = proj[..., D:2 * D].reshape(B, S, FOX_HEADS, FOX_HEAD).transpose(0, 2, 1, 3)
    log_f = jax.nn.log_sigmoid((proj[..., 2 * D:] + b_f).astype(jnp.float32))
    cum_log_f = jnp.cumsum(log_f.transpose(0, 2, 1), axis=-1)
    return k, v, cum_log_f

def forgetting_attention(h, w_q, w_o, k, v, cum_log_f):
    B, S, D = h.shape
    q = (h @ w_q).reshape(B, S, FOX_HEADS, FOX_HEAD).transpose(0, 2, 1, 3)
    scale = FOX_HEAD ** -0.5
    outs = []
    for blk in range(S // Q_BLOCK):
        q0, q1 = blk * Q_BLOCK, (blk + 1) * Q_BLOCK
        kb, vb = k[:, :, :q1], v[:, :, :q1]
        s = jnp.einsum('bhqd,bhkd->bhqk', q[:, :, q0:q1], kb).astype(jnp.float32) * scale
        s = s + cum_log_f[:, :, q0:q1, None] - cum_log_f[:, :, None, :q1]
        causal = jnp.arange(q0, q1)[:, None] >= jnp.arange(q1)[None, :]
        p = jax.nn.softmax(jnp.where(causal, s, -jnp.inf), axis=-1)
        outs.append(jnp.einsum('bhqk,bhkd->bhqd', p.astype(vb.dtype), vb))
    o = jnp.concatenate(outs, axis=2).transpose(0, 2, 1, 3).reshape(B, S, D)
    return o @ w_o

def second_inputs(seed: int = 0) -> dict:
    key = jax.random.key(seed)
    ks = iter(jax.random.split(key, 40))
    D = D_MODEL
    nrm = lambda shape, scale: jax.random.normal(next(ks), shape, jnp.float32) * scale
    unif = lambda shape, lo, hi: jax.random.uniform(next(ks), shape, jnp.float32, lo, hi)
    na, nb = N_A_LAYERS, N_B_LAYERS
    return {
        "x": nrm((BATCH, SEQ, D), 1.0),
        "mix_norm": 1.0 + nrm((DEPTH_2, D), 0.02),
        "ffn_norm": 1.0 + nrm((DEPTH_2, D), 0.02),
        "final_norm": 1.0 + nrm((D,), 0.02),
        "rwkv_x_mix": unif((na, N_MIX, D), 0.0, 1.0),
        "rwkv_w_rkv": nrm((na, 3, D, D), D ** -0.5),
        "rwkv_w0": unif((na, D), -6.0, -1.0),
        "rwkv_w1": nrm((na, D, DECAY_LORA), D ** -0.5),
        "rwkv_w2": nrm((na, DECAY_LORA, D), 0.5 * DECAY_LORA ** -0.5),
        "rwkv_a0": nrm((na, D), 0.1),
        "rwkv_a1": nrm((na, D, AAA_LORA), D ** -0.5),
        "rwkv_a2": nrm((na, AAA_LORA, D), AAA_LORA ** -0.5),
        "rwkv_v0": nrm((na - 1, D), 0.1),
        "rwkv_v1": nrm((na - 1, D, MV_LORA), D ** -0.5),
        "rwkv_v2": nrm((na - 1, MV_LORA, D), MV_LORA ** -0.5),
        "rwkv_g1": nrm((na, D, GATE_LORA), D ** -0.5),
        "rwkv_g2": nrm((na, GATE_LORA, D), GATE_LORA ** -0.5),
        "rwkv_k_k": 0.85 + nrm((na, D), 0.02),
        "rwkv_k_a": 1.0 + nrm((na, D), 0.02),
        "rwkv_r_k": nrm((na, RWKV_HEADS, RWKV_HEAD), 0.1),
        "rwkv_lnx_w": 1.0 + nrm((na, D), 0.02),
        "rwkv_lnx_b": nrm((na, D), 0.02),
        "rwkv_w_o": nrm((na, D, D), D ** -0.5),
        "kv_norm": 1.0 + nrm((D,), 0.02),
        "w_kvf": nrm((D, 2 * D + FOX_HEADS), D ** -0.5),
        "b_f": nrm((FOX_HEADS,), 0.1),
        "fox_w_q": nrm((nb, D, D), D ** -0.5),
        "fox_w_o": nrm((nb, D, D), D ** -0.5),
        "mlp_w_up": nrm((DEPTH_2, D, D_FF), D ** -0.5),
        "mlp_w_down": nrm((DEPTH_2, D_FF, D), D_FF ** -0.5),
    }

def second_block(x, mix_norm, ffn_norm, final_norm, rwkv_x_mix, rwkv_w_rkv, rwkv_w0, rwkv_w1,
              rwkv_w2, rwkv_a0, rwkv_a1, rwkv_a2, rwkv_v0, rwkv_v1, rwkv_v2, rwkv_g1, rwkv_g2,
              rwkv_k_k, rwkv_k_a, rwkv_r_k, rwkv_lnx_w, rwkv_lnx_b, rwkv_w_o, kv_norm, w_kvf,
              b_f, fox_w_q, fox_w_o, mlp_w_up, mlp_w_down):
    v_first = None
    k_sh = v_sh = c_sh = None
    for layer in range(DEPTH_2):
        if layer < N_A_LAYERS:
            i = layer
            v_res = None if i == 0 else (rwkv_v0[i - 1], rwkv_v1[i - 1], rwkv_v2[i - 1])
            h = rms_norm(x, mix_norm[layer])
            mixed, v_first = rwkv7_time_mix(
                h, rwkv_x_mix[i], rwkv_w_rkv[i], rwkv_w0[i], rwkv_w1[i], rwkv_w2[i],
                rwkv_a0[i], rwkv_a1[i], rwkv_a2[i], rwkv_g1[i], rwkv_g2[i], rwkv_k_k[i],
                rwkv_k_a[i], rwkv_r_k[i], rwkv_lnx_w[i], rwkv_lnx_b[i], rwkv_w_o[i],
                v_first, v_res)
        else:
            if layer == N_A_LAYERS:
                k_sh, v_sh, c_sh = shared_kv_forget(x, kv_norm, w_kvf, b_f)
            j = layer - N_A_LAYERS
            h = rms_norm(x, mix_norm[layer])
            mixed = forgetting_attention(h, fox_w_q[j], fox_w_o[j], k_sh, v_sh, c_sh)
        x = x + mixed
        x = x + squared_relu_mlp(rms_norm(x, ffn_norm[layer]), mlp_w_up[layer], mlp_w_down[layer])
    return rms_norm(x, final_norm)


def setup_inputs(seed=0):
    out = dict(first_inputs(seed))
    for name, value in second_inputs(seed + 1).items():
        if name != "x":
            out[name + "_2"] = value
    return out


def reference(
    x, mem, norm_mix, w_in, w_gla_gate_up, b_gla_gate, sgu_norm, w_sgu, b_sgu, out_norm, w_out,
    norm_xattn, norm_mem, w_xq, w_xkv, w_xo, final_norm, mix_norm_2, ffn_norm_2, final_norm_2,
    rwkv_x_mix_2, rwkv_w_rkv_2, rwkv_w0_2, rwkv_w1_2, rwkv_w2_2, rwkv_a0_2, rwkv_a1_2,
    rwkv_a2_2, rwkv_v0_2, rwkv_v1_2, rwkv_v2_2, rwkv_g1_2, rwkv_g2_2, rwkv_k_k_2, rwkv_k_a_2,
    rwkv_r_k_2, rwkv_lnx_w_2, rwkv_lnx_b_2, rwkv_w_o_2, kv_norm_2, w_kvf_2, b_f_2, fox_w_q_2,
    fox_w_o_2, mlp_w_up_2, mlp_w_down_2,
):
    x = first_block(
        x, mem, norm_mix, w_in, w_gla_gate_up, b_gla_gate, sgu_norm, w_sgu, b_sgu, out_norm,
        w_out, norm_xattn, norm_mem, w_xq, w_xkv, w_xo, final_norm,
    )
    return second_block(
        x, mix_norm_2, ffn_norm_2, final_norm_2, rwkv_x_mix_2, rwkv_w_rkv_2, rwkv_w0_2,
        rwkv_w1_2, rwkv_w2_2, rwkv_a0_2, rwkv_a1_2, rwkv_a2_2, rwkv_v0_2, rwkv_v1_2, rwkv_v2_2,
        rwkv_g1_2, rwkv_g2_2, rwkv_k_k_2, rwkv_k_a_2, rwkv_r_k_2, rwkv_lnx_w_2, rwkv_lnx_b_2,
        rwkv_w_o_2, kv_norm_2, w_kvf_2, b_f_2, fox_w_q_2, fox_w_o_2, mlp_w_up_2, mlp_w_down_2,
    )


_drawn_inputs = setup_inputs


def setup_inputs(seed=0):
    import zlib

    import numpy as np

    out = dict(_drawn_inputs(seed))
    spreads = {}
    factors = {'b_gla_gate': 3.434,
     'sgu_norm': 8.0,
     'b_sgu': 2.91,
     'out_norm': 3.677,
     'norm_xattn': 8.0,
     'norm_mem': 8.0,
     'final_norm_2': 21.704,
     'rwkv_w1_2': 4.114,
     'rwkv_w2_2': 4.175,
     'rwkv_a0_2': 2.694,
     'rwkv_k_k_2': 18.804,
     'rwkv_k_a_2': 4.657,
     'rwkv_lnx_w_2': 4.996,
     'rwkv_lnx_b_2': 4.99,
     'kv_norm_2': 16.824,
     'b_f_2': 4.356,
     'ffn_norm_2': 2.698}
    for name, (base, spread) in spreads.items():
        noise = np.random.default_rng([zlib.crc32(name.encode()), seed]).standard_normal(out[name].shape)
        drawn = base * np.exp(spread * noise) if base else spread * noise
        out[name] = __import__('jax').numpy.asarray(drawn.astype(out[name].dtype))
    for name, factor in factors.items():
        out[name] = (out[name] * factor).astype(out[name].dtype)
    return out
```

```python
from contextlib import ExitStack

import concourse.bass as bass
from concourse import mybir

F32 = mybir.dt.float32
F32R = mybir.dt.float32r
U8 = mybir.dt.uint8
ACT = mybir.ActivationFunctionType
ALU = mybir.AluOpType
AXX = mybir.AxisListType.X

P = 128
D = 2048
KT = D // P
S = 256
HALF = KT // 2
EPS = 1e-6
LNX_EPS = 64e-5
NEG = -1e30
GELU = 1.5957691216057308
EXP_HALF = 0.6065306597126334

PHASES = [
    ("xkv", 8, False), ("in_a", 40, False), ("in_r", 1, False), ("in_b", 16, False),
    ("out", 16, False), ("xq", 4, False), ("xo", 4, True),
    ("rw_r", 16, False), ("rw_k", 16, False), ("rw_v", 16, False), ("rw_w1", 1, False),
    ("rw_a1", 1, False), ("rw_g1", 2, False), ("rw_up", 6, True), ("rw_o", 16, False),
    ("up0", 64, False), ("mlp0", 64, False),
    ("fk", 16, False), ("fv", 16, False), ("ff", 1, False), ("fq", 16, False), ("fo", 16, False),
    ("mlp1", 128, False),
]


def mlp_phases(layer):
    return [(f"{w}{layer}_{q}", 16, False) for q in range(4) for w in ("up", "dn")]


PHASES = [p for p in PHASES if p[0] not in ("up0", "mlp0", "mlp1")]
_at = [p[0] for p in PHASES].index("rw_o") + 1
PHASES = PHASES[:_at] + mlp_phases(0) + PHASES[_at:] + mlp_phases(1)
STOPS = {1: "out", 2: "xo", 3: "rw_o", 4: "dn0_3", 5: "fo", 6: "dn1_3"}


def two_block_kernel(nc, a, out, stop=6):
    phases = PHASES[:[p[0] for p in PHASES].index(STOPS[stop]) + 1]
    N0, M0, COUNT, n, m = {}, {}, {}, 0, 0
    for name, count, special in phases:
        N0[name], M0[name], COUNT[name] = n, m, count
        n += count
        m += 0 if special else count
    TOTAL = n

    with ExitStack() as ctx:
        TILE = S * 4
        arena = ctx.enter_context(nc.sbuf_tensor("arena", [P, 192 * 256], F32))
        base = BASE = 16512

        def at(name, tiles_at, shape, dt=F32):
            return nc.alloc_sbuf_tensor_at(name, shape, dt, offset=BASE + tiles_at * TILE)

        X = at("x_resid", 0, [P, KT, S])
        raw = [at(f"w_raw{i}", 16 + 4 * i, [P, HALF, P]) for i in range(4)]
        wh = [at(f"w_high{i}", 32 + 4 * i, [P, HALF, P], F32R) for i in range(4)]
        wl = [at(f"w_low{i}", 48 + 4 * i, [P, HALF, P], F32R) for i in range(4)]
        AH, AL = at("a_high", 64, [P, KT, S], F32R), at("a_low", 80, [P, KT, S], F32R)
        BH, BL = at("b_high", 96, [P, KT, S], F32R), at("b_low", 112, [P, KT, S], F32R)
        AF, BF = at("a_scratch", 64, [P, 32, S]), at("b_scratch", 96, [P, 32, S])
        G = at("g", 128, [P, 64, S])
        LH, LL = at("lora_high", 184, [P, 4, S], F32R), at("lora_low", 188, [P, 4, S], F32R)

        def sb(name, shape, dt=F32):
            return ctx.enter_context(nc.sbuf_tensor(name, shape, dt))

        ident, ones, bones, kge = (sb(x, [P, P]) for x in ("ident", "ones", "bones", "kge"))
        lowmask, upmask = sb("lowmask", [P, 7, P], U8), sb("upmask", [P, 7, P], U8)
        m_low, m_up, m_upi, m_id = (sb(x, [P, P], U8) for x in ("m_low", "m_up", "m_upi", "m_id"))
        causal = sb("causal", [P, 2, P])
        limit = sb("limit", [P, 2, P])
        NROW = 4
        prm = sb("prm", [P, NROW * P])
        omm = sb("one_minus_mix", [P, 6 * KT])
        neg = sb("negated", [P, 3 * KT])
        eps, eps_ln = sb("eps", [P, 1]), sb("eps_ln", [P, 1])
        rT, gup = sb("gla_r", [16, S]), sb("gate_up", [16, S])
        w_s = G[:, 8:10, :].rearrange("p a (b n) -> p (a b) n", n=P)
        b_s = G[0:1, 10:12, :].rearrange("p a (b n) -> p (a b) n", n=P)
        bf = sb("b_f_sb", [16, 1])
        rstd = sb("rstd", [P, 2, S])
        touched = sb("touched", [P, 16])
        stat = sb("stat", [P, 2, 8])
        ps = [ctx.enter_context(nc.psum_tensor(f"proj{i}", [P, 512], F32)) for i in range(2)]
        q = [ctx.enter_context(nc.psum_tensor(f"side{i}", [P, 512], F32)) for i in range(6)]
        spill = nc.dram_tensor("rwkv_spill", [6, KT, P, S], F32)

        names = {}

        def sem(name):
            if name not in names:
                names[name] = ctx.enter_context(nc.semaphore(name))
            return names[name]

        ONCE = {"tensor": ["prm_t", "gl_z", "gl_vt", "gl_o", "sg_wt", "sg_ss", "sg_vt", "sg_mixed", "f_t"],
                "vector": ["prm2", "gl_x", "gl_vtc", "gl_out", "sg_v", "sg_vtc", "sg_out", "rw_zero", "f_in", "f_c", "f_ready"],
                "scalar": ["prm", "gl_ln", "sg_sq", "sg_std", "sg_wtc", "f_ln"],
                "gpsimd": ["prow_zero", "ident", "gl_zero", "sg_wm"]}
        POSITION = {event: (f"{engine}_once", k + 1) for engine, events in ONCE.items() for k, event in enumerate(events)}

        def once(event):
            return sem(POSITION[event][0]), 1

        def after(event):
            return sem(POSITION[event][0]), POSITION[event][1]

        vec = [("norm_mix", "norm_mix", 16), ("out_norm", "out_norm", 16), ("norm_xattn", "norm_xattn", 16),
               ("norm_mem", "norm_mem", 16), ("final_norm", "final_norm", 16), ("mix_norm", "mix_norm_2", 32),
               ("w0", "rwkv_w0_2", 16),
               ("ffn_norm", "ffn_norm_2", 32), ("final2", "final_norm_2", 16), ("a0", "rwkv_a0_2", 16),
               ("k_k", "rwkv_k_k_2", 16), ("k_a", "rwkv_k_a_2", 16), ("r_k", "rwkv_r_k_2", 16), ("lnx_w", "rwkv_lnx_w_2", 16),
               ("x_mix", "rwkv_x_mix_2", 96), ("lnx_b", "rwkv_lnx_b_2", 16), ("kv_norm", "kv_norm_2", 16),
               ("sgu_norm", "sgu_norm", 4), ("b_gla", "b_gla_gate", 2)]
        COL, row = {}, 0
        rows = []
        for key, src, cnt in vec:
            assert row // P == (row + cnt - 1) // P, key
            COL[key] = row
            rows.append((src, row, cnt))
            row += cnt
        assert row <= NROW * P
        prow = G[:, 48:50, :].rearrange("p a (b c) -> p (a b) c", c=P)

        def col(key, k=0):
            return prm[:, bass.ds(COL[key] + k, 1)] if not isinstance(k, int) else prm[:, COL[key] + k:COL[key] + k + 1]

        def tile(t, k):
            return t[:, bass.ds(k, 1), :].rearrange("p a n -> p (a n)") if not isinstance(k, int) else t[:, k, :]

        def rows_of(w):
            return w.rearrange("(k p) n -> p k n", p=P)

        def cols(w, c0, width=P):
            view = rows_of(w)
            return lambda t, j: (view[:, HALF * j:HALF * j + HALF, bass.ds(t * P + c0, width)], width)

        def xo_src(t, j):
            return rows_of(a["w_xo"][0])[:, :, bass.ds(t * 512 + j * 256, 256)], "xo"

        win = a["w_in"][0]
        SRC = {"xkv": cols(a["w_xkv"][0], 0), "in_a": cols(win, 0), "in_r": cols(win, 5120, 16),
               "in_b": cols(win, 5136), "out": cols(a["w_out"][0], 0), "xq": cols(a["w_xq"][0], 0),
               "xo": xo_src, "rw_r": cols(a["rwkv_w_rkv_2"][0, 0], 0), "rw_k": cols(a["rwkv_w_rkv_2"][0, 1], 0),
               "rw_v": cols(a["rwkv_w_rkv_2"][0, 2], 0), "rw_w1": cols(a["rwkv_w1_2"][0], 0, 96),
               "rw_a1": cols(a["rwkv_a1_2"][0], 0, 96), "rw_g1": cols(a["rwkv_g1_2"][0], 0),
               "rw_o": cols(a["rwkv_w_o_2"][0], 0),
               "fk": cols(a["w_kvf_2"], 0), "fv": cols(a["w_kvf_2"], D), "ff": cols(a["w_kvf_2"], 2 * D, 16),
               "fq": cols(a["fox_w_q_2"][0], 0), "fo": cols(a["fox_w_o_2"][0], 0)}
        for layer in range(2):
            for qq in range(4):
                SRC[f"up{layer}_{qq}"] = cols(a["mlp_w_up_2"][layer], qq * D)
                SRC[f"dn{layer}_{qq}"] = cols(a["mlp_w_down_2"][layer][qq * D:(qq + 1) * D], 0)

        def up_src(t, j):
            which, part = divmod(2 * t + j, 4)
            if which < 2:
                w = a["rwkv_w2_2" if which == 0 else "rwkv_a2_2"][0]
                return w[:, part * 512:part * 512 + 512], "up96"
            return rows_of(a["rwkv_g2_2"][0])[:, :, part * 512:part * 512 + 512], "up256"

        SRC["rw_up"] = up_src

        def over(eng, name, body, peel=0, tail=0):
            cnt, n0, m0 = COUNT[name], N0[name], M0[name]

            def one(t0, i, u):
                t = t0 + 2 * i + u
                nb, mb = n0 + t0 + u, m0 + t0 + u
                body(t, nb + 2 * i, nb // 2 + i, nb % 2, mb // 2 + i, mb % 2)

            for t in range(min(peel, cnt)):
                one(t, 0, 0)
            start, end = min(peel, cnt), cnt - tail
            pairs = max(0, end - start) // 2
            if pairs >= 2:
                with eng.Fori(0, pairs) as i:
                    one(start, i, 0)
                    one(start, i, 1)
                start += 2 * pairs
            for t in range(start, cnt):
                one(t, 0, 0)

        def phase_done(eng, name):
            m_end = M0[name] + COUNT[name]
            eng.wait_ge(sem("proj_out0"), (m_end + 1) // 2)
            eng.wait_ge(sem("proj_out1"), m_end // 2)

        def split_next(eng, n, nh, pair, last):
            if last:
                return
            for j in range(2):
                slot = 2 * pair + j
                if eng is nc.scalar:
                    eng.wait_ge(sem("w_used"), n * 2 + j + 1)
                    eng.wait_ge(sem(f"w_loaded{slot}"), nh * 16 + 32)
                    eng.activation(wh[slot][:], raw[slot][:], ACT.Copy).then_inc(sem("w_hi"), 1)
                else:
                    eng.wait_ge(sem("w_hi"), n * 2 + j + 5)
                    eng.tensor_tensor(wl[slot][:], raw[slot][:], wh[slot][:].bitcast(F32), ALU.subtract)\
                       .then_inc(sem("w_lo"), 1)

        last_phase = phases[-1][0]

        def stream(eng, name, evac=None, peel=0):
            def run(tail_only):
                def body(t, n, nh, pair, mh, bank):
                    split_next(eng, n, nh, pair, tail_only and isinstance(n, int) and n >= TOTAL - 2)
                    if evac:
                        evac(t, n, mh, bank)
                return body
            over(eng, name, run(name == last_phase), peel=peel, tail=2 if name == last_phase else 0)

        def project(pe, name, hi, lo, groups=None, k_of=None):
            def body(t, n, nh, pair, mh, bank):
                if not (isinstance(mh, int) and mh == 0):
                    pe.wait_ge(sem(f"proj_out{bank}"), mh)
                for j in range(2):
                    slot = 2 * pair + j
                    pe.wait_ge(sem("w_lo"), n * 2 + j + 1)
                    for k in range(HALF):
                        kk = HALF * j + k
                        if groups and kk % 4 == 0:
                            pe.wait_ge(sem(groups[0]), groups[1](kk // 4))
                        o = ps[bank][:, 0:S]
                        pe.matmul(o, wh[slot][:, k, :], hi[:, kk, :], start=kk == 0, stop=False)
                        pe.matmul(o, wh[slot][:, k, :], lo[:, kk, :], start=False, stop=False)
                        mm = pe.matmul(o, wl[slot][:, k, :], hi[:, kk, :], start=False, stop=kk == KT - 1)
                    mm.then_inc(sem("w_used"), 1)
            over(pe, name, body, peel=2 if M0[name] == 0 else 0)

        def out_copy(eng, dst, k0, scale=None):
            def evac(t, n, mh, bank):
                eng.wait_ge(sem("w_used"), n * 2 + 2)
                if scale:
                    o = eng.tensor_scalar(tile(dst, k0 + t), ps[bank][:, 0:S], scale, None, ALU.mult)
                else:
                    o = eng.tensor_copy(tile(dst, k0 + t), ps[bank][:, 0:S])
                o.then_inc(sem(f"proj_out{bank}"), 1)
            return evac

        def out_resid(eng):
            def evac(t, n, mh, bank):
                eng.wait_ge(sem("w_used"), n * 2 + 2)
                eng.tensor_tensor(tile(X, t), ps[bank][:, 0:S], tile(X, t), ALU.add).then_inc(sem(f"proj_out{bank}"), 1)
            return evac

        NORMS = {
            "mem": (0, G, 32, "norm_mem", (AH, AL), BF, 0),
            "mix": (1, X, 0, "norm_mix", (BH, BL), G, 0),
            "xattn": (2, X, 0, "norm_xattn", (AH, AL), G, 0),
            "final1": (3, X, 0, "final_norm", None, G, 0),
            "rwkv": (4, X, 0, "mix_norm", G, G, 16),
            "ffn0": (5, X, 0, "ffn_norm", (AH, AL), G, 0),
            "kv": (6, X, 0, "kv_norm", (AH, AL), G, 48),
            "fox": (7, X, 0, ("mix_norm", 16), (BH, BL), G, 48),
            "ffn1": (8, X, 0, ("ffn_norm", 16), (AH, AL), G, 0),
            "final2": (9, X, 0, "final2", None, G, 0),
        }
        run_norms = ["mem", "mix", "xattn", "final1", "rwkv", "ffn0", "kv", "fox", "ffn1", "final2"]
        if stop == 1:
            run_norms = ["mem", "mix"]
        elif stop == 2:
            run_norms = run_norms[:3]
        else:
            run_norms = run_norms[:{3: 5, 4: 6, 5: 8, 6: 9}[stop]]
        run_norms = run_norms + ["final2"]
        NIDX = {x: i for i, x in enumerate(run_norms)}

        def norm_scalar(act, name):
            _, src, k0, gain, dst, scr, s0 = NORMS[name]
            i = NIDX[name]
            if i:
                act.wait_ge(sem("norm_done"), 4 * i)
            for g in range(4):
                act.activation(scr[:, s0 + 4 * g:s0 + 4 * g + 4, :], src[:, k0 + 4 * g:k0 + 4 * g + 4, :], ACT.Square)\
                   .then_inc(sem("norm_sq"), 1)
            act.wait_ge(sem("norm_sum"), i + 1)
            act.activation(rstd[:, 0, :], q[0][:, 0:S], ACT.Sqrt, scale=1.0 / D, bias=eps[:, 0:1]).then_inc(sem("norm_std"), 1)
            if isinstance(dst, tuple):
                for g in range(4):
                    act.wait_ge(sem("norm_val"), 4 * norm_hl(name) + g + 1)
                    act.activation(dst[0][:, 4 * g:4 * g + 4, :], scr[:, s0 + 4 * g:s0 + 4 * g + 4, :], ACT.Copy)\
                       .then_inc(sem("norm_hi"), 1)

        def norm_hl(name):
            return sum(isinstance(NORMS[x][4], tuple) for x in run_norms[:NIDX[name]])

        def norm_tensor(pe, name):
            _, src, k0, gain, dst, scr, s0 = NORMS[name]
            for g in range(4):
                pe.wait_ge(sem("norm_sq"), 4 * NIDX[name] + g + 1)
                for k in range(4):
                    mm = pe.matmul(q[0][:, 0:S], ones[:], scr[:, s0 + 4 * g + k, :], start=g + k == 0, stop=g + k == 6)
            mm.then_inc(sem("norm_sum"), 1)

        def norm_vector(dve, name):
            _, src, k0, gain, dst, scr, s0 = NORMS[name]
            i = NIDX[name]
            gkey, goff = gain if isinstance(gain, tuple) else (gain, 0)
            split = isinstance(dst, tuple)
            to, t0 = (scr, s0) if split else ((X, 0) if dst is None else (dst, 0))
            dve.wait_ge(sem("norm_std"), i + 1)
            dve.reciprocal(rstd[:, 1, :], rstd[:, 0, :]).then_inc(sem("norm_rec"), 1)
            dve.wait_ge(sem("norm_rec"), i + 1)

            def low(g):
                dve.wait_ge(sem("norm_hi"), 4 * norm_hl(name) + g + 1)
                dve.tensor_tensor(dst[1][:, 4 * g:4 * g + 4, :], scr[:, s0 + 4 * g:s0 + 4 * g + 4, :],
                                  dst[0][:, 4 * g:4 * g + 4, :].bitcast(F32), ALU.subtract).then_inc(sem("norm_done"), 1)

            for g in range(4):
                for k in range(4 * g, 4 * g + 4):
                    o = dve.scalar_tensor_tensor(out=to[:, t0 + k, :], in0=src[:, k0 + k, :], scalar=col(gkey, goff + k),
                                                 in1=rstd[:, 1, :], op0=ALU.mult, op1=ALU.mult)
                o.then_inc(sem("norm_val" if split else "norm_done"), 1)
                if split and g:
                    low(g - 1)
            if split:
                low(3)

        def norm_ready(name):
            return ("norm_done", lambda g: 4 * NIDX[name] + g + 1)

        def norm_all(eng, name):
            eng.wait_ge(sem("norm_done"), 4 * NIDX[name] + 4)

        ATT = {"xa": dict(heads=4, hb=0, q0=16, k0=56, v0=60, causal=False, scr=(G, 20), dst=(BH, BL)),
               "fa": dict(heads=16, hb=4, q0=32, k0=0, v0=16, causal=True, scr=(BF, 0), dst=(AH, AL))}
        SCALE = float(P) ** -0.5

        def att_bufs(name, s):
            t, o = ATT[name]["scr"]
            o += 9 * s
            flat = lambda b, k: t[:, o + b:o + b + k, :].rearrange("p a n -> p (a n)")
            return dict(qS=flat(0, 1), vS=flat(1, 1), S=flat(2, 2), P=flat(4, 2), PT=flat(6, 2), vt=flat(8, 1))

        fscr = G[:, 48:64, :]
        cneg, cpos = fscr[0:16, 0, :], fscr[0:16, 1, :]
        cT = fscr[:, 2, 0:32].rearrange("p (a h) -> p a h", a=2)
        selS = [fscr[0:16, 3 + s, 0:P] for s in range(2)]

        def settled(pool):
            pool.wait_ge(sem("masks32"), 1)

        def att_pool(pool, name):
            c = ATT[name]
            with pool.Fori(0, c["heads"] // 2) as i:
                for s in range(2):
                    b = att_bufs(name, s)
                    pool.wait_ge(sem("att_out"), i * 2 + (s + 1 + c["hb"]))
                    settled(pool)
                    pool.tensor_copy(b["qS"], tile(G, i * 2 + (c["q0"] + s))).then_inc(sem("att_staged"), 1)
                    pool.tensor_copy(b["vS"], tile(G, i * 2 + (c["v0"] + s))).then_inc(sem("att_staged"), 1)
                    if c["causal"]:
                        pool.tensor_copy(selS[s], ident[0:16, bass.ds(i * 2 + s, 1)].broadcast_to([16, P]))\
                            .then_inc(sem("att_staged"), 1)

        def att_tensor(pe, name):
            c = ATT[name]
            per = 3 if c["causal"] else 2
            W = (P, S) if c["causal"] else (S, S)
            with pe.Fori(0, c["heads"] // 2) as i:
                for s in range(2):
                    b = att_bufs(name, s)
                    pe.wait_ge(sem("att_staged"), i * (2 * per) + ((s + 1) * per + 2 * c["hb"]))
                    for t in range(2):
                        o = q[s][:, S * t:S * t + W[t]]
                        mm = pe.matmul(o, b["qS"][:, P * t:P * t + P], tile(G, i * 2 + (c["k0"] + s))[:, 0:W[t]],
                                       start=True, stop=not c["causal"])
                        if c["causal"]:
                            mm = pe.matmul(o, selS[s], cneg[:, 0:W[t]], start=False, stop=True)
                    mm.then_inc(sem("att_score"), 1)
                    for t in range(2):
                        mm = pe.transpose(q[4 + s][:, P * t:P * t + P], b["vS"][:, P * t:P * t + P], ident[:])
                    mm.then_inc(sem("att_vt"), 1)
                for s in range(2):
                    b = att_bufs(name, s)
                    pe.wait_ge(sem("att_prob"), i * 2 + (s + 1 + c["hb"]))
                    o = 0
                    for k in range(2):
                        for t in range(2):
                            if P * k < W[t]:
                                mm = pe.transpose(q[2 + s][:, o:o + P], b["P"][:, S * t + P * k:S * t + P * k + P], ident[:])
                                o += P
                    mm.then_inc(sem("att_pt"), 1)
                for s in range(2):
                    b = att_bufs(name, s)
                    pe.wait_ge(sem("att_ptc"), i * 2 + (s + 1 + c["hb"]))
                    pe.wait_ge(sem("att_vtc"), i * 2 + (s + 1 + c["hb"]))
                    pe.matmul(q[4 + s][:, S:2 * S], b["vt"][:, 0:P], b["PT"][:, 0:S], start=True, stop=False)
                    lo = P if c["causal"] else 0
                    pe.matmul(q[4 + s][:, S + lo:2 * S], b["vt"][:, P:2 * P], b["PT"][:, S:2 * S - lo], start=False, stop=True)\
                        .then_inc(sem("att_o"), 1)

        def att_scalar(act, name):
            c = ATT[name]
            W = (P, S) if c["causal"] else (S, S)
            n = 3 * P if c["causal"] else 4 * P
            with act.Fori(0, c["heads"] // 2) as i:
                for s in range(2):
                    b = att_bufs(name, s)
                    act.wait_ge(sem("att_max"), i * 2 + (s + 1 + c["hb"]))
                    src = b["S"] if c["causal"] else q[s]
                    for t in range(2):
                        e = act.activation(b["P"][:, S * t:S * t + W[t]], src[:, S * t:S * t + W[t]], ACT.Exp,
                                           bias=stat[:, s, t:t + 1], accum_out=stat[:, s, 2 + t:3 + t])
                    e.then_inc(sem("att_exp"), 1)
                for s in range(2):
                    b = att_bufs(name, s)
                    act.wait_ge(sem("att_pt"), i * 2 + (s + 1 + c["hb"]))
                    act.activation(b["PT"][:, 0:n], q[2 + s][:, 0:n], ACT.Copy).then_inc(sem("att_ptc"), 1)
                for s in range(2):
                    act.wait_ge(sem("att_o"), i * 2 + (s + 1 + c["hb"]))
                    act.activation(tile(c["dst"][0], i * 2 + s), q[4 + s][:, S:2 * S], ACT.Copy).then_inc(sem("att_ohi"), 1)

        def att_vector(dve, name):
            c = ATT[name]
            W = (P, S) if c["causal"] else (S, S)
            with dve.Fori(0, c["heads"] // 2) as i:
                for s in range(2):
                    b = att_bufs(name, s)
                    dve.wait_ge(sem("att_score"), i * 2 + (s + 1 + c["hb"]))
                    src = q[s]
                    if c["causal"]:
                        cm = causal[:, :, :].rearrange("p a n -> p (a n)")
                        for t in range(2):
                            o = dve.scalar_tensor_tensor(out=b["S"][:, S * t:S * t + W[t]], in0=q[s][:, S * t:S * t + W[t]],
                                                         scalar=cT[:, t, bass.ds(i * 2 + s, 1)], in1=cm[:, S - W[t]:S],
                                                         op0=ALU.add, op1=ALU.add)
                        o.then_inc(sem("att_masked"), 1)
                        dve.wait_ge(sem("att_masked"), i * 2 + (s + 1))
                        src = b["S"]
                    for t in range(2):
                        o = dve.tensor_reduce(stat[:, s, t:t + 1], src[:, S * t:S * t + W[t]], AXX, ALU.max, negate=True)
                    o.then_inc(sem("att_max"), 1)
                    dve.wait_ge(sem("att_vt"), i * 2 + (s + 1 + c["hb"]))
                    dve.tensor_copy(b["vt"], q[4 + s][:, 0:S]).then_inc(sem("att_vtc"), 1)
                for s in range(2):
                    b = att_bufs(name, s)
                    dve.wait_ge(sem("att_exp"), i * 2 + (s + 1 + c["hb"]))
                    dve.reciprocal(stat[:, s, 4:6], stat[:, s, 2:4]).then_inc(sem("att_rec"), 1)
                    dve.wait_ge(sem("att_rec"), i * 2 + (s + 1 + c["hb"]))
                    for t in range(2):
                        p_ = b["P"][:, S * t:S * t + W[t]]
                        o = dve.tensor_scalar(p_, p_, stat[:, s, 4 + t:5 + t], None, ALU.mult)
                    o.then_inc(sem("att_prob"), 1)
                for s in range(2):
                    dve.wait_ge(sem("att_ohi"), i * 2 + (s + 1 + c["hb"]))
                    dve.tensor_tensor(tile(c["dst"][1], i * 2 + s), q[4 + s][:, S:2 * S],
                                      tile(c["dst"][0], i * 2 + s).bitcast(F32), ALU.subtract).then_inc(sem("att_out"), 1)

        class Chain:

            def __init__(self, eng, name):
                self.eng, self.sem, self.n = eng, sem(name), 0

            def after(self, ins):
                self.n += 1
                ins.then_inc(self.sem, 1)
                self.eng.wait_ge(self.sem, self.n)

        def sb_bufs(s):
            flat = lambda b, n=1: AF[:, 10 * s + b:10 * s + b + n, :].rearrange("p a n -> p (a n)")
            return dict(kS=flat(0), vS=flat(1), qS=flat(2), z=flat(3, 2)[:, 0:384], e=flat(5, 2)[:, 0:384],
                        a=flat(7, 2)[:, 0:384], vt=flat(9))

        def diag(t):
            return t.rearrange("p (b n) -> p b n", n=P)[:, 0:3:2, :]

        def sb_pool(pool):
            phase_done(pool, "in_b")
            with pool.Fori(0, 4) as i:
                for s in range(2):
                    b = sb_bufs(s)
                    pool.wait_ge(sem("sb_out"), i * 2 + (s + 1))
                    settled(pool)
                    pool.tensor_copy(b["kS"], tile(G, i * 2 + (8 + s))).then_inc(sem("sb_staged"), 1)
                    pool.tensor_copy(b["vS"], tile(G, i * 2 + (16 + s))).then_inc(sem("sb_staged"), 1)

        def sb_tensor(pe):
            phase_done(pe, "in_b")
            with pe.Fori(0, 4) as i:
                for s in range(2):
                    b = sb_bufs(s)
                    pe.wait_ge(sem("sb_staged"), i * 4 + 2 * (s + 1))
                    query = tile(G, i * 2 + s)
                    pe.matmul(q[s][:, 0:S], b["kS"][:, 0:P], query, start=True, stop=True)
                    pe.matmul(q[s][:, S:384], b["kS"][:, P:S], query[:, P:S], start=True, stop=True).then_inc(sem("sb_z"), 1)
                    pe.transpose(q[2 + s][:, 0:P], b["vS"][:, 0:P], ident[:])
                    pe.transpose(q[2 + s][:, P:S], b["vS"][:, P:S], ident[:]).then_inc(sem("sb_vt"), 1)
                for s in range(2):
                    b = sb_bufs(s)
                    pe.wait_ge(sem("sb_spm"), i * 2 + (s + 1))
                    pe.matmul(q[4 + s][:, 0:S], kge[:], b["e"][:, 0:S], start=True, stop=False)
                    pe.matmul(q[4 + s][:, P:S], ones[:], b["e"][:, S:384], start=False, stop=True)
                    pe.matmul(q[4 + s][:, S:384], kge[:], b["e"][:, S:384], start=True, stop=True).then_inc(sem("sb_sum"), 1)
                for s in range(2):
                    b = sb_bufs(s)
                    pe.wait_ge(sem("sb_vtc"), i * 2 + (s + 1))
                    pe.wait_ge(sem("sb_exp"), i * 2 + (s + 1))
                    pe.matmul(q[s][:, 0:S], b["vt"][:, 0:P], b["a"][:, 0:S], start=True, stop=False)
                    pe.matmul(q[s][:, P:S], b["vt"][:, P:S], b["a"][:, S:384], start=False, stop=True).then_inc(sem("sb_o"), 1)

        def sb_scalar(act):
            with act.Fori(0, 4) as i:
                for s in range(2):
                    b = sb_bufs(s)
                    act.wait_ge(sem("sb_z"), i * 2 + (s + 1))
                    act.activation(b["z"], q[s][:, 0:384], ACT.Copy, scale=SCALE).then_inc(sem("sb_zc"), 1)
                    act.activation(b["e"], q[s][:, 0:384], ACT.Abs, scale=SCALE).then_inc(sem("sb_abs"), 1)
                for s in range(2):
                    b = sb_bufs(s)
                    act.wait_ge(sem("sb_abs"), i * 2 + (s + 1))
                    act.activation(b["e"], b["e"], ACT.Exp, scale=-1.0).then_inc(sem("sb_e"), 1)
                for s in range(2):
                    b = sb_bufs(s)
                    act.wait_ge(sem("sb_e"), i * 2 + (s + 1))
                    act.activation(b["e"], b["e"], ACT.Ln, bias=1.0).then_inc(sem("sb_ln"), 1)
                for s in range(2):
                    b = sb_bufs(s)
                    act.wait_ge(sem("sb_dm"), i * 2 + (s + 1))
                    act.activation(b["a"], b["a"], ACT.Exp).then_inc(sem("sb_exp"), 1)

        def sb_vector(dve):
            with dve.Fori(0, 4) as i:
                for s in range(2):
                    b = sb_bufs(s)
                    dve.wait_ge(sem("sb_vt"), i * 2 + (s + 1))
                    dve.tensor_copy(b["vt"], q[2 + s][:, 0:S]).then_inc(sem("sb_vtc"), 1)
                for s in range(2):
                    b = sb_bufs(s)
                    dve.wait_ge(sem("sb_ln"), i * 2 + (s + 1))
                    dve.scalar_tensor_tensor(out=b["e"], in0=b["z"], scalar=0.0, in1=b["e"], op0=ALU.max, op1=ALU.add)\
                       .then_inc(sem("sb_sp"), 1)
                for s in range(2):
                    b = sb_bufs(s)
                    dve.wait_ge(sem("sb_sp"), i * 2 + (s + 1))
                    dve.tensor_tensor(diag(b["e"]), diag(b["e"]), limit[:, 0, :].unsqueeze(1).broadcast_to([P, 2, P]), ALU.min)\
                       .then_inc(sem("sb_spm"), 1)
                for s in range(2):
                    b = sb_bufs(s)
                    dve.wait_ge(sem("sb_sum"), i * 2 + (s + 1))
                    dve.scalar_tensor_tensor(out=b["a"], in0=q[4 + s][:, 0:384], scalar=-1.0, in1=b["z"], op0=ALU.mult, op1=ALU.add)\
                       .then_inc(sem("sb_d"), 1)
                for s in range(2):
                    b = sb_bufs(s)
                    dve.wait_ge(sem("sb_d"), i * 2 + (s + 1))
                    dve.tensor_tensor(diag(b["a"]), diag(b["a"]), limit[:, 1, :].unsqueeze(1).broadcast_to([P, 2, P]), ALU.min)\
                       .then_inc(sem("sb_dm"), 1)
                for s in range(2):
                    dve.wait_ge(sem("sb_o"), i * 2 + (s + 1))
                    dve.tensor_copy(tile(G, i * 2 + s), q[s][:, 0:S]).then_inc(sem("sb_out"), 1)

        af = lambda o, n: AF[:, o:o + n, :]
        gl_c, gl_x, gl_l = af(0, 2), af(2, 2), af(4, 2)
        gl_E, gl_Q, gl_K = [af(6, 2), af(8, 2)], [af(10, 2), af(12, 2)], [af(14, 2), af(16, 2)]
        gl_AT = af(18, 6).rearrange("p a (b n) -> p (a b) n", n=P).rearrange("p (x h) n -> p x h n", x=3)
        gl_vt = af(24, 4).rearrange("p a (b n) -> p (a b) n", n=P).rearrange("p (x h) n -> p x h n", x=2)
        gl_d, gl_nd = af(28, 2), af(30, 2)

        def level(t, l):
            return t.rearrange("p a (b n) -> p (a b) n", n=2 ** l)

        def bank4(b):
            return q[b][:, :].rearrange("p (h n) -> p h n", h=4)

        def gla_pool(pool):
            pool.wait_ge(sem("sb_out"), 10)
            pool.dma_start(w_s, a["w_sgu"][0].rearrange("g t s -> t g s")).then_inc(sem("sgu_in"), 16)
            pool.dma_start(b_s, a["b_sgu"]).then_inc(sem("sgu_in"), 16)
            pool.memset(gl_AT, 0.0).then_inc(*once("gl_zero"))
            for l in range(1, 9):
                pool.wait_ge(sem("gl_E"), l)
                if l > 2:
                    pool.wait_ge(sem("gl_mm"), l - 2)
                pool.tensor_tensor(gl_K[l % 2], G[:, 34:36, :], gl_E[l % 2], ALU.mult).then_inc(sem("gl_K"), 1)

        def gla_scalar(act, ch):
            act.wait_ge(*after("gl_x"))
            ch.after(act.activation(gl_l, gl_x, ACT.Abs))
            ch.after(act.activation(gl_l, gl_l, ACT.Exp, scale=-1.0))
            act.activation(gl_l, gl_l, ACT.Ln, bias=1.0).then_inc(*once("gl_ln"))
            for l in range(1, 9):
                act.wait_ge(sem("gl_nd"), l)
                if l > 2:
                    act.wait_ge(sem("gl_K"), l - 2)
                    act.wait_ge(sem("gl_Q"), l - 2)
                act.activation(gl_E[l % 2], gl_nd, ACT.Exp).then_inc(sem("gl_E"), 1)

        def gla_vector(dve, ch):
            dve.wait_ge(*after("gl_z"))
            dve.wait_ge(sem("sb_out"), 10)
            for j in range(2):
                o = dve.tensor_scalar(gl_x[:, j, :], q[0][:, S * j:S * j + S], col("b_gla", j), None, ALU.add)
            o.then_inc(*once("gl_x"))
            dve.wait_ge(*after("gl_x"))
            ch.after(dve.tensor_scalar(gl_d, gl_x, -1.0, 0.0, ALU.mult, ALU.max))
            dve.wait_ge(*after("gl_ln"))
            ch.after(dve.tensor_tensor(gl_d, gl_d, gl_l, ALU.add))
            ch.after(dve.tensor_scalar(gl_d, gl_d, -1.0 / 16.0, None, ALU.mult))
            for j in range(2):
                o = dve.tensor_tensor_scan(gl_c[:, j, :], ones[:, 0:1].broadcast_to([P, S]), gl_d[:, j, :], 0.0, ALU.mult, ALU.add)
            ch.after(o)
            ch.after(dve.tensor_scalar(G[:, 32:34, :], G[:, 32:34, :], 0.125, None, ALU.mult))

            def pick(l, lv):
                dve.wait_ge(sem("gl_mm"), lv)
                b0 = 2 * (lv % 2)
                if l == 8:
                    o = dve.tensor_copy(gl_AT[:, 1], bank4(b0))
                else:
                    mask = m_id[:, :] if l == 0 else upmask[:, l - 1, :]
                    for x, b in ((0, b0), (2, b0 + 1)):
                        o = dve.copy_predicated(gl_AT[:, x], mask.unsqueeze(1).broadcast_to([P, 4, P]), bank4(b))
                o.then_inc(sem("gl_pick"), 1)

            dve.wait_ge(*after("gl_zero"))
            for l in range(1, 9):
                c = level(gl_c, l)
                n = 2 ** l
                if l > 1:
                    dve.wait_ge(sem("gl_E"), l - 1)
                ch.after(dve.tensor_tensor(level(gl_d, l), c, c[:, :, n // 2 - 1:n // 2].broadcast_to([P, 512 // n, n]), ALU.subtract))
                dve.scalar_tensor_tensor(out=gl_nd, in0=gl_d, scalar=-1.0, in1=gl_d, op0=ALU.mult, op1=ALU.min).then_inc(sem("gl_nd"), 1)
                if l > 1:
                    pick(l - 1, l - 1)
                dve.wait_ge(sem("gl_E"), l)
                dve.tensor_tensor(gl_Q[l % 2], G[:, 32:34, :], gl_E[l % 2], ALU.mult).then_inc(sem("gl_Q"), 1)
            pick(8, 8)
            pick(0, 9)
            dve.wait_ge(*after("gl_vt"))
            for x in range(2):
                o = dve.tensor_copy(gl_vt[:, x], bank4(4 + x))
            o.then_inc(*once("gl_vtc"))
            dve.wait_ge(*after("gl_o"))
            for x in range(2):
                o = dve.tensor_copy(G[:, 32 + 2 * x:34 + 2 * x, :], q[x][:, :].rearrange("p (a n) -> p a n", a=2))
            o.then_inc(*once("gl_out"))

        def gla_tensor(pe):
            rows_done = Chain(pe, "rows_done")
            pe.wait_ge(sem("sb_out"), 10)
            for j in range(2):
                mm = pe.matmul(q[0][:, S * j:S * j + S], gup[:, P * j:P * j + P], rT[:, :], start=True, stop=True)
            mm.then_inc(*once("gl_z"))
            for h in range(4):
                for x in range(2):
                    mm = pe.transpose(q[4 + x][:, P * h:P * h + P], G[:, 36 + h, P * x:P * x + P], ident[:])
            mm.then_inc(*once("gl_vt"))
            pe.wait_ge(*after("gl_x"))
            for lv, l in enumerate([1, 2, 3, 4, 5, 6, 7, 8, 0], 1):
                if l:
                    pe.wait_ge(sem("gl_Q"), l)
                    pe.wait_ge(sem("gl_K"), l)
                if lv > 2:
                    pe.wait_ge(sem("gl_pick"), lv - 2)
                kk, qq = (gl_K[l % 2], gl_Q[l % 2]) if l else (G[:, 34:36, :], G[:, 32:34, :])
                for h in (0, 2, 1, 3):
                    for x, (ts, tt) in enumerate([(0, 1)] if l == 8 else [(0, 0), (1, 1)]):
                        r = slice(64 * (h % 2), 64 * (h % 2) + 64)
                        mm = pe.matmul(q[2 * (lv % 2) + x][:, P * h:P * h + P], kk[r, h // 2, P * ts:P * ts + P],
                                       qq[r, h // 2, P * tt:P * tt + P], start=True, stop=True)
                    if h == 2:
                        rows_done.after(mm)
                mm.then_inc(sem("gl_mm"), 1)
            pe.wait_ge(sem("gl_pick"), 9)
            pe.wait_ge(*after("gl_vtc"))
            for h in range(4):
                o = q[h // 2][:, S * (h % 2):S * (h % 2) + S]
                pe.matmul(o[:, 0:P], gl_vt[:, 0, h, :], gl_AT[:, 0, h, :], start=True, stop=True)
                pe.matmul(o[:, P:S], gl_vt[:, 0, h, :], gl_AT[:, 1, h, :], start=True, stop=False)
                mm = pe.matmul(o[:, P:S], gl_vt[:, 1, h, :], gl_AT[:, 2, h, :], start=False, stop=True)
            mm.then_inc(*once("gl_o"))

        sg_e, sg_sq = af(0, 8), af(8, 4)
        sg_vt = af(12, 4).rearrange("p a (b n) -> p (a b) n", n=P).rearrange("p (x h) n -> p x h n", x=2)
        sg_w = af(16, 2).rearrange("p a (b n) -> p (a b) n", n=P)

        def sgu_scalar(act, ch):
            act.wait_ge(*after("gl_out"))
            for h, lo in ((0, 4), (1, 0)):
                x, e = G[:, 44 + lo:48 + lo, :], sg_e[:, lo:lo + 4, :]
                act.activation(e, x, ACT.Square).then_inc(sem("sg_x2"), 1)
                act.wait_ge(sem("sg_arg"), h + 1)
                act.activation(e, e, ACT.Exp, scale=-GELU).then_inc(sem("sg_exp"), 1)
            act.wait_ge(sem("sg_gelu"), 1)
            act.activation(sg_sq, G[:, 48:52, :], ACT.Square).then_inc(*once("sg_sq"))
            act.wait_ge(*after("sg_ss"))
            act.activation(rstd[:, 0, :], q[0][:, 0:S], ACT.Sqrt, scale=1.0 / 512, bias=eps[:, 0:1]).then_inc(*once("sg_std"))
            act.wait_ge(*after("sg_wt"))
            act.activation(sg_w, bank4(3), ACT.Copy).then_inc(*once("sg_wtc"))

        def sgu_vector(dve, ch):
            for h, lo in ((0, 4), (1, 0)):
                x, e = G[:, 44 + lo:48 + lo, :], sg_e[:, lo:lo + 4, :]
                dve.wait_ge(sem("sg_x2"), h + 1)
                ch.after(dve.tensor_scalar(e, e, 0.044715, 1.0, ALU.mult, ALU.add))
                dve.tensor_tensor(e, e, x, ALU.mult).then_inc(sem("sg_arg"), 1)
                dve.wait_ge(sem("sg_exp"), h + 1)
                ch.after(dve.tensor_scalar(e, e, 1.0, None, ALU.add))
                ch.after(dve.reciprocal(e, e))
                dve.tensor_tensor(x, x, e, ALU.mult).then_inc(sem("sg_gelu"), 1)
            dve.wait_ge(*after("sg_std"))
            ch.after(dve.reciprocal(rstd[:, 1, :], rstd[:, 0, :]))
            for g in range(4):
                o = dve.scalar_tensor_tensor(out=G[:, 48 + g, :], in0=G[:, 48 + g, :], scalar=col("sgu_norm", g),
                                             in1=rstd[:, 1, :], op0=ALU.mult, op1=ALU.mult)
            o.then_inc(*once("sg_v"))
            dve.wait_ge(*after("sg_vt"))
            for x in range(2):
                o = dve.tensor_copy(sg_vt[:, x], bank4(1 + x))
            o.then_inc(*once("sg_vtc"))
            dve.wait_ge(*after("sg_mixed"))
            for x in range(2):
                u = G[:, 44 + 2 * x:46 + 2 * x, :]
                o = dve.tensor_tensor(u, q[4 + x][:, :].rearrange("p (a n) -> p a n", a=2), u, ALU.mult)
            o.then_inc(*once("sg_out"))

        def sgu_pool(pool):
            pool.wait_ge(*after("sg_wtc"))
            pool.affine_select(out=sg_w, in_=sg_w, compare_op=ALU.is_ge, fill=0.0, base=0,
                               pattern=[[0, 4], [1, P]], channel_multiplier=-1).then_inc(*once("sg_wm"))

        def sgu_tensor(pe):
            pe.wait_ge(*after("gl_out"))
            pe.wait_ge(sem("sgu_in"), 32)
            for g in range(4):
                mm = pe.transpose(q[3][:, P * g:P * g + P], w_s[:, g, :], ident[:])
            mm.then_inc(*once("sg_wt"))
            pe.wait_ge(*after("sg_sq"))
            for g in range(4):
                mm = pe.matmul(q[0][:, 0:S], ones[:], sg_sq[:, g, :], start=g == 0, stop=g == 3)
            mm.then_inc(*once("sg_ss"))
            pe.wait_ge(*after("sg_v"))
            for g in range(4):
                for x in range(2):
                    mm = pe.transpose(q[1 + x][:, P * g:P * g + P], G[:, 48 + g, P * x:P * x + P], ident[:])
            mm.then_inc(*once("sg_vt"))
            pe.wait_ge(*after("sg_vtc"))
            pe.wait_ge(*after("sg_wm"))
            for g in range(4):
                for x in range(2):
                    o = q[4 + g // 2][:, S * (g % 2) + P * x:S * (g % 2) + P * x + P]
                    pe.matmul(o, sg_vt[:, x, g, :], sg_w[:, g, :], start=True, stop=False)
                    mm = pe.matmul(o, ones[0:1, :], b_s[0:1, g, :], start=False, stop=True)
            mm.then_inc(*once("sg_mixed"))

        MIX_O, MIX_G = [0, 4, 32, 44], [24, 28, 40, 52]

        def mix_scalar(act):
            act.wait_ge(*after("sg_out"))
            for g in range(4):
                act.activation(af(4 * g, 4), G[:, MIX_G[g]:MIX_G[g] + 4, :], ACT.Exp, scale=-1.0).then_inc(sem("mix_e"), 1)
            for g in range(4):
                act.activation(af(16 + 4 * g, 4), G[:, MIX_O[g]:MIX_O[g] + 4, :], ACT.Square).then_inc(sem("mix_sq"), 1)
                act.wait_ge(sem("mix_ss"), g + 1)
                for x in range(2):
                    o = act.activation(af(16 + 4 * g + 2 * x, 2), q[2 * (g % 2) + x][:, :].rearrange("p (a n) -> p a n", a=2),
                                       ACT.Sqrt, scale=1.0 / P, bias=eps[:, 0:1])
                o.then_inc(sem("mix_std"), 1)
                if g:
                    act.wait_ge(sem("mix_val"), g)
                    act.activation(BH[:, 4 * g - 4:4 * g, :], af(4 * g - 4, 4), ACT.Copy).then_inc(sem("mix_hi"), 1)
            act.wait_ge(sem("mix_val"), 4)
            act.activation(BH[:, 12:16, :], af(12, 4), ACT.Copy).then_inc(sem("mix_hi"), 1)

        def mix_tensor(pe):
            for g in range(4):
                pe.wait_ge(sem("mix_sq"), g + 1)
                if g > 1:
                    pe.wait_ge(sem("mix_std"), g - 1)
                for k in range(4):
                    mm = pe.matmul(q[2 * (g % 2) + k // 2][:, S * (k % 2):S * (k % 2) + S], ones[:], AF[:, 16 + 4 * g + k, :],
                                   start=True, stop=True)
                mm.then_inc(sem("mix_ss"), 1)

        def mix_vector(dve, ch):
            def low(g):
                dve.wait_ge(sem("mix_hi"), g + 1)
                dve.tensor_tensor(BL[:, 4 * g:4 * g + 4, :], af(4 * g, 4), BH[:, 4 * g:4 * g + 4, :].bitcast(F32), ALU.subtract)\
                   .then_inc(sem("mix_done"), 1)

            for g in range(4):
                e, r, o = af(4 * g, 4), af(16 + 4 * g, 4), MIX_O[g]
                dve.wait_ge(sem("mix_e"), g + 1)
                ch.after(dve.tensor_scalar(e, e, 1.0, None, ALU.add))
                ch.after(dve.reciprocal(e, e))
                ch.after(dve.tensor_tensor(e, e, G[:, MIX_G[g]:MIX_G[g] + 4, :], ALU.mult))
                dve.wait_ge(sem("mix_std"), g + 1)
                ch.after(dve.reciprocal(r, r))
                for k in range(4):
                    i = dve.scalar_tensor_tensor(out=AF[:, 16 + 4 * g + k, :], in0=G[:, o + k, :], scalar=col("out_norm", 4 * g + k),
                                                 in1=AF[:, 16 + 4 * g + k, :], op0=ALU.mult, op1=ALU.mult)
                ch.after(i)
                dve.tensor_tensor(e, e, r, ALU.mult).then_inc(sem("mix_val"), 1)
                if g:
                    low(g - 1)
            low(3)

        class LoopChain:

            def __init__(self, eng, name, i, per):
                self.eng, self.sem, self.i, self.per, self.k = eng, sem(name), i, per, 0

            def do(self, ins):
                ins.then_inc(self.sem, 1)
                self.k += 1
                return self.k

            def need(self, k):
                self.eng.wait_ge(self.sem, self.i * self.per + k)

            def end(self):
                assert self.k == self.per, self.k

        H, XT = G, G[:, 16:32, :]
        MIXES = {"r": (0, 0, (AH, AL)), "k": (1, 1, (BH, BL)), "v": (2, 2, (AH, AL)), "w": (3, 3, (BH, BL)),
                 "a": (4, 4, (AH, AL)), "g": (5, 5, (BH, BL))}

        def xs_scalar_part(act, mix, t):
            m, c, dst = MIXES[mix]
            if m:
                act.wait_ge(sem("xs_done"), t + (16 * m - 15))
            src = omm[:, bass.ds(t + 16 * c, 1)] if not isinstance(t, int) else omm[:, 16 * c + t:16 * c + t + 1]
            act.activation(tile(XT, t), tile(H, t), ACT.Copy, scale=src).then_inc(sem("xs_here"), 1)

        def xs_scalar_high(act, mix, t):
            m, c, dst = MIXES[mix]
            act.wait_ge(sem("xs_val"), t + (16 * m + 1))
            act.activation(tile(dst[0], t), tile(XT, t), ACT.Copy).then_inc(sem("xs_hi"), 1)

        def xs_vector_add(dve, mix, t):
            m, c, dst = MIXES[mix]
            dve.wait_ge(sem("xs_here"), t + (16 * m + 1))
            x = tile(XT, t)
            dve.scalar_tensor_tensor(out=x[:, 1:S], in0=tile(H, t)[:, 0:S - 1], scalar=col("x_mix", t + 16 * c),
                                     in1=x[:, 1:S], op0=ALU.mult, op1=ALU.add).then_inc(sem("xs_val"), 1)

        def xs_vector_low(dve, mix, t):
            m, c, dst = MIXES[mix]
            dve.wait_ge(sem("xs_hi"), t + (16 * m + 1))
            dve.tensor_tensor(tile(dst[1], t), tile(XT, t), tile(dst[0], t).bitcast(F32), ALU.subtract).then_inc(sem("xs_done"), 1)

        def xs_bulk(eng, mix, first, second):
            with eng.Fori(0, 4) as i:
                for u in range(4):
                    first(eng, mix, i * 4 + u)
                for u in range(4):
                    second(eng, mix, i * 4 + u)

        def xs_ready(mix):
            return ("xs_done", lambda g: 16 * MIXES[mix][0] + 4 * g + 4)

        SPILL = {"rw_r": 0, "rw_k": 1, "rw_v": 2}

        def spill_before(name, mh, bank):
            m0 = M0["rw_r"]
            return mh - (m0 // 2 if m0 % 2 == bank else (m0 + 1) // 2)

        def spill_scalar(act, name, nxt):
            def evac(t, n, mh, bank):
                act.wait_ge(sem("w_used"), n * 2 + 2)
                before = spill_before(name, mh, bank)
                if not (isinstance(before, int) and before == 0):
                    act.wait_ge(sem(f"spilled{bank}"), before * 16)
                act.activation(G[:, 40 + bank, :], ps[bank][:, 0:S], ACT.Copy).then_inc(sem(f"proj_out{bank}"), 1)
                xs_scalar_part(act, nxt, t)
                xs_scalar_high(act, nxt, t)
            return evac

        def spill_vector(dve, nxt):
            def evac(t, n, mh, bank):
                xs_vector_add(dve, nxt, t)
                xs_vector_low(dve, nxt, t)
            return evac

        def spill_pool(pool, name):
            def body(t, n, nh, pair, mh, bank):
                pool.wait_ge(sem(f"proj_out{bank}"), mh + 1)
                settled(pool)
                pool.dma_start(spill_ap[SPILL[name], bass.ds(t, 1)].rearrange("a p n -> p (a n)"), G[:, 40 + bank, :])\
                    .then_inc(sem(f"spilled{bank}"), 16)
            over(pool, name, body)

        LORA = {"rw_w1": (0, 96, ACT.Tanh), "rw_a1": (1, 96, ACT.Copy), "rw_g1": (2, P, ACT.Sigmoid)}

        def lora_scalar(act, name):
            k0, parts, func = LORA[name]

            def evac(t, n, mh, bank):
                f = G[0:parts, 36 + k0 + t, :]
                act.wait_ge(sem("w_used"), n * 2 + 2)
                act.activation(f, ps[bank][0:parts, 0:S], func).then_inc(sem(f"proj_out{bank}"), 1)
                act.wait_ge(sem(f"proj_out{bank}"), mh + 1)
                act.activation(LH[0:parts, k0 + t, :], f, ACT.Copy).then_inc(sem("lora_hi"), 1)
            return evac

        def lora_vector(dve, name):
            k0, parts, func = LORA[name]

            def evac(t, n, mh, bank):
                dve.wait_ge(sem("lora_hi"), k0 + t + 1)
                dve.tensor_tensor(LL[0:parts, k0 + t, :], G[0:parts, 36 + k0 + t, :], LH[0:parts, k0 + t, :].bitcast(F32), ALU.subtract)\
                   .then_inc(sem("lora_done"), 1)
            return evac

        def up_tensor(pe):
            n0 = N0["rw_up"]
            for hc in range(12):
                which, part = divmod(hc, 4)
                slot = 2 * ((n0 + hc // 2) % 2) + hc % 2
                pe.wait_ge(sem("w_lo"), 2 * n0 + hc + 1)
                pe.wait_ge(sem("lora_done"), (1, 2, 4)[which])
                if hc > 1:
                    pe.wait_ge(sem("up_out"), hc - 1)
                kn, parts = ((1, 96), (1, 96), (2, P))[which]
                flat = lambda w: w[slot][:, :, :].rearrange("p k n -> p (k n)")
                for o in range(4):
                    dst = q[2 * (hc % 2) + o // 2][:, S * (o % 2):S * (o % 2) + S]
                    for k in range(kn):
                        c = slice(512 * k + P * o, 512 * k + P * o + P)
                        x = which + k
                        pe.matmul(dst, flat(wh)[0:parts, c], LH[0:parts, x, :], start=k == 0, stop=False)
                        pe.matmul(dst, flat(wh)[0:parts, c], LL[0:parts, x, :], start=False, stop=False)
                        mm = pe.matmul(dst, flat(wl)[0:parts, c], LH[0:parts, x, :], start=False, stop=k == kn - 1)
                mm.then_inc(sem("w_used"), 1)

        def up_vector(dve):
            n0 = N0["rw_up"]
            for t in range(6):
                split_next(dve, n0 + t, (n0 + t) // 2, (n0 + t) % 2, n0 + t >= TOTAL - 2)
                for j in range(2):
                    hc = 2 * t + j
                    dve.wait_ge(sem("w_used"), 2 * n0 + hc + 1)
                    if hc > 1:
                        dve.wait_ge(sem(f"up_spilled{hc % 2}"), 16 * (hc // 2))
                    for x in range(2):
                        g = 44 + 4 * (hc % 2) + 2 * x
                        o = dve.tensor_copy(G[:, g:g + 2, :], q[2 * (hc % 2) + x][:, :].rearrange("p (a n) -> p a n", a=2))
                    o.then_inc(sem("up_out"), 1)

        def up_pool(pool):
            for hc in range(12):
                which, part = divmod(hc, 4)
                pool.wait_ge(sem("up_out"), hc + 1)
                pool.dma_start(spill_ap[3 + which, 4 * part:4 * part + 4].rearrange("a p n -> p a n"),
                               G[:, 44 + 4 * (hc % 2):48 + 4 * (hc % 2), :]).then_inc(sem(f"up_spilled{hc % 2}"), 16)

        def rw_bufs(s):
            pieces = [[(G, 0, 44)], [(G, 44, 20), (BF, 0, 24)]][s]
            left = [list(p_) for p_ in pieces]
            out_ = {}
            for key, cnt in (("in", 6), ("e", 2), ("ex", 3), ("M", 2), ("AK", 2), ("RB", 2), ("RK", 2), ("U", 2), ("T", 2),
                             ("PP", 2), ("tok", 2), ("ld", 1), ("c", 1), ("cm", 1), ("cml", 1), ("kk", 1), ("sq", 1),
                             ("b", 1), ("at", 1), ("bt", 1), ("kt", 1), ("rt", 1), ("k1", 1), ("t", 1), ("bon", 1),
                             ("xsa", 1), ("s1", 1)):
                for piece in left:
                    if piece[2] >= cnt:
                        view = piece[0][:, piece[1]:piece[1] + cnt, :]
                        piece[1] += cnt
                        piece[2] -= cnt
                        break
                else:
                    raise AssertionError(key)
                out_[key] = view.rearrange("p a n -> p (a n)") if cnt == 1 else view
                if key in ("M", "AK", "RB", "RK", "U", "T", "PP", "tok"):
                    out_[key] = view.rearrange("p a (b n) -> p (a b) n", n=P)
            out_["y"], out_["yc"], out_["ysq"] = out_["ld"], out_["cml"], out_["sq"]
            return out_

        RB_ = [rw_bufs(s) for s in range(2)]
        chunks = lambda t: t.rearrange("p (c n) -> p c n", n=P)

        def bc4(m):
            return m.unsqueeze(1).broadcast_to([P, 4, P])

        def rw_pool(pool):
            for b in range(2):
                cnt = 24
                pool.wait_ge(sem(f"spilled{b}"), 16 * cnt)
                pool.wait_ge(sem(f"up_spilled{b}"), 16 * 6)
            phase_done(pool, "rw_g1")
            with pool.Fori(0, 8) as i:
                for s in range(2):
                    pool.wait_ge(sem("rw_out"), i * 2 + (s + 1))
                    settled(pool)
                    pool.dma_start(RB_[s]["in"], spill_ap[:, bass.ds(i * 2 + s, 1)].rearrange("x a p n -> p x (a n)"))\
                        .then_inc(sem(f"rw_in{s}"), 16)
                for s in range(2):
                    b = RB_[s]
                    pool.wait_ge(sem("rw_t"), i * 2 + (s + 1))
                    settled(pool)
                    pool.tensor_tensor(b["k1"], b["in"][:, 1, :], b["t"], ALU.mult).then_inc(sem("rw_k1"), 1)
                for s in range(2):
                    b = RB_[s]
                    pool.wait_ge(sem("rw_exp"), i * 2 + (s + 1))
                    settled(pool)
                    pool.tensor_tensor(b["rt"], b["in"][:, 0, :], b["ex"][:, 0, :], ALU.mult).then_inc(sem("rw_rt"), 1)
                    pool.wait_ge(sem("rw_k1"), i * 2 + (s + 1))
                    settled(pool)
                    pool.tensor_tensor(b["kt"], b["k1"], b["ex"][:, 1, :], ALU.mult).then_inc(sem("rw_kt"), 1)

        def omka(j):
            return neg[:, bass.ds(j + 32, 1)]

        def rw_scalar(act):
            with act.Fori(0, 8) as i:
                v = lambda s: i * 2 + (s + 1)
                for s in range(2):
                    b = RB_[s]
                    act.wait_ge(sem(f"rw_in{s}"), i * 16 + 16)
                    for x in range(2):
                        e = act.activation(b["e"][:, x, :], b["in"][:, 3 + x, :], ACT.Exp, scale=-1.0,
                                           bias=neg[:, bass.ds(i * 2 + (s + 16 * x), 1)])
                    e.then_inc(sem("rw_e"), 1)
                    act.activation(b["T"], bc4(ident[:, :]), ACT.Copy).then_inc(sem("rw_start"), 1)
                    act.activation(b["U"], bc4(ident[:, :]), ACT.Copy).then_inc(sem("rw_start"), 1)
                for s in range(2):
                    b = RB_[s]
                    act.wait_ge(sem("rw_sig"), v(s))
                    act.activation(b["t"], b["e"][:, 1, :], ACT.Identity, scale=prm[:, bass.ds(i * 2 + (s + COL["k_a"]), 1)],
                                   bias=omka(i * 2 + s)).then_inc(sem("rw_t"), 1)
                for s in range(2):
                    b = RB_[s]
                    act.wait_ge(sem("rw_cm"), v(s))
                    act.activation(b["ex"][:, 0, :], b["cm"], ACT.Exp)
                    act.activation(b["ex"][:, 1, :], b["cm"], ACT.Exp, scale=-1.0)
                    act.activation(b["ex"][:, 2, :], b["cml"], ACT.Exp)
                    act.activation(b["s1"][:, 64:65], b["c"][:, 191:192], ACT.Exp).then_inc(sem("rw_exp"), 1)
                for s in range(2):
                    b = RB_[s]
                    act.wait_ge(sem("rw_kk0"), v(s))
                    act.activation(b["sq"], b["kk"], ACT.Square).then_inc(sem("rw_sq"), 1)
                for s in range(2):
                    b = RB_[s]
                    act.wait_ge(sem("rw_ss"), v(s))
                    act.activation(b["sq"], q[3 * s][:, 0:S], ACT.Sqrt).then_inc(sem("rw_nrm"), 1)
                for s in range(2):
                    act.wait_ge(sem("rw_m2"), v(s))
                    act.activation(RB_[s]["tok"], bank4(3 * s + 2), ACT.Copy).then_inc(sem("rw_tok"), 1)
                for lv in range(6):
                    for s in range(2):
                        act.wait_ge(sem("rw_p"), i * 12 + (2 * lv + s + 1))
                        act.activation(RB_[s]["PP"], bank4(3 * s + 1), ACT.Copy).then_inc(sem("rw_pc"), 1)
                    if lv < 5:
                        for s in range(2):
                            act.wait_ge(sem("rw_tt"), i * 10 + (2 * lv + s + 1))
                            act.activation(RB_[s]["T"], bank4(3 * s + 2), ACT.Copy).then_inc(sem("rw_tc"), 1)
                for c in range(2):
                    for s in range(2):
                        act.wait_ge(sem("rw_x"), i * 4 + (2 * c + s + 1))
                        act.activation(RB_[s]["xsa"][:, 0:P], q[3 * s + 1 - c][:, 0:P], ACT.Copy).then_inc(sem("rw_xc"), 1)
                    for s in range(2):
                        act.wait_ge(sem("rw_sa"), i * 4 + (2 * c + s + 1))
                        act.activation(RB_[s]["xsa"][:, P:S], q[3 * s + 1 - c][:, P:S], ACT.Copy).then_inc(sem("rw_sac"), 1)
                for s in range(2):
                    act.wait_ge(sem("rw_y"), v(s))
                    act.activation(RB_[s]["y"], q[3 * s + 2][:, 0:S], ACT.Copy).then_inc(sem("rw_yc"), 1)
                for s in range(2):
                    act.wait_ge(sem("rw_yd"), v(s))
                    act.activation(RB_[s]["ysq"], RB_[s]["yc"], ACT.Square).then_inc(sem("rw_ysq"), 1)
                for s in range(2):
                    act.wait_ge(sem("rw_var"), v(s))
                    act.activation(RB_[s]["ysq"], q[3 * s + 1][:, S:2 * S], ACT.Sqrt, scale=1.0 / 64, bias=eps_ln[:, 0:1])\
                       .then_inc(sem("rw_sd"), 1)
                for s in range(2):
                    act.wait_ge(sem("rw_val"), v(s))
                    act.activation(tile(AH, i * 2 + s), RB_[s]["yc"], ACT.Copy).then_inc(sem("rw_hi"), 1)

        def rw_tensor(pe):
            with pe.Fori(0, 8) as i:
                v = lambda s: i * 2 + (s + 1)
                rng = lambda h: slice(64 * h, 64 * h + 64)

                halves = LoopChain(pe, "rw_rows", i, 6)

                def pairs(s, *products):
                    for h in range(2):
                        for bank, l, r in products:
                            for c in range(2):
                                mm = pe.matmul(q[bank][:, P * (2 * h + c):P * (2 * h + c) + P], RB_[s][l][rng(h), P * c:P * c + P],
                                               RB_[s][r][rng(h), P * c:P * c + P], start=True, stop=True)
                        if h == 0:
                            halves.need(halves.do(mm))
                    return mm

                for s in range(2):
                    pe.wait_ge(sem("rw_sq"), v(s))
                    pe.matmul(q[3 * s][:, 0:S], bones[:], RB_[s]["sq"], start=True, stop=True).then_inc(sem("rw_ss"), 1)
                for s in range(2):
                    pe.wait_ge(sem("rw_bt"), v(s))
                    pe.wait_ge(sem("rw_kt"), v(s))
                    pe.wait_ge(sem("rw_rt"), v(s))
                    pairs(s, (3 * s, "at", "bt"), (3 * s + 1, "bt", "at"), (3 * s + 2, "kt", "at")).then_inc(sem("rw_m1"), 1)
                for s in range(2):
                    b = RB_[s]
                    pe.wait_ge(sem("rw_m1e"), v(s))
                    pairs(s, (3 * s, "bt", "rt"), (3 * s + 1, "kt", "rt"))
                    for x, src in enumerate((b["bt"][:, 0:P], b["kt"][:, 0:P], b["in"][:, 2, 0:P], b["in"][:, 2, P:S])):
                        mm = pe.transpose(q[3 * s + 2][:, P * x:P * x + P], src, ident[:])
                    mm.then_inc(sem("rw_m2"), 1)
                for s in range(2):
                    pe.wait_ge(sem("rw_m2e"), v(s))
                    pe.wait_ge(sem("rw_rk"), v(s))
                    pe.matmul(q[3 * s][:, 0:S], bones[:], RB_[s]["t"], start=True, stop=True).then_inc(sem("rw_bs"), 1)
                pe.wait_ge(sem("rw_bon"), v(1))
                pe.wait_ge(sem("rw_tok"), v(1))
                for lv in range(6):
                    for s in range(2):
                        b = RB_[s]
                        if lv:
                            pe.wait_ge(sem("rw_tc"), i * 10 + (2 * lv - 2 + s + 1))
                        for x in range(4):
                            mm = pe.matmul(q[3 * s + 1][:, P * x:P * x + P], b["M"][:, x, :], b["U"][:, x, :], start=True, stop=True)
                        mm.then_inc(sem("rw_p"), 1)
                    for s in range(2):
                        b = RB_[s]
                        pe.wait_ge(sem("rw_pc"), i * 12 + (2 * lv + s + 1))
                        for x in range(4):
                            mm = pe.matmul(q[3 * s][:, P * x:P * x + P], b["T"][:, x, :], b["PP"][:, x, :], start=True, stop=True)
                        mm.then_inc(sem("rw_g"), 1)
                    if lv < 5:
                        for s in range(2):
                            b = RB_[s]
                            pe.wait_ge(sem("rw_u"), i * 12 + (2 * lv + s + 1))
                            for x in range(4):
                                mm = pe.transpose(q[3 * s + 2][:, P * x:P * x + P], b["U"][:, x, :], ident[:])
                            mm.then_inc(sem("rw_tt"), 1)
                for c in range(2):
                    for s in range(2):
                        b = RB_[s]
                        bank = 3 * s + 1 - c
                        pe.wait_ge(sem("rw_u"), i * 12 + (10 + s + 1))
                        if c:
                            pe.wait_ge(sem("rw_s1c"), v(s))
                        for h in range(2):
                            o = q[bank][:, 64 * h:64 * h + 64]
                            mm = pe.matmul(o, b["AK"][:, 2 * h + c, :], b["tok"][:, 2 + c, rng(h)], start=True, stop=c == 0)
                            if c:
                                mm = pe.matmul(o, b["at"][rng(h), P:S], b["s1"][rng(h), 0:64], start=False, stop=True)
                            if c and h == 0:
                                halves.need(halves.do(mm))
                        mm.then_inc(sem("rw_x"), 1)
                    for s in range(2):
                        b = RB_[s]
                        bank = 3 * s + 1 - c
                        pe.wait_ge(sem("rw_xc"), i * 4 + (2 * c + s + 1))
                        for h in range(2):
                            mm = pe.matmul(q[bank][:, P + 64 * h:P + 64 * h + 64], b["U"][:, 2 * h + c, :], b["xsa"][:, rng(h)],
                                           start=True, stop=True)
                        mm.then_inc(sem("rw_sa"), 1)
                    for s in range(2):
                        b = RB_[s]
                        pe.wait_ge(sem("rw_sac"), i * 4 + (2 * c + s + 1))
                        for h in range(2):
                            sa = b["xsa"][:, P + 64 * h:P + 64 * h + 64]
                            vt = b["tok"][:, 2 + c, rng(h)]
                            if c == 0:
                                o = q[3 * s + 1][rng(h), S:S + 64]
                                pe.matmul(o, b["tok"][:, 0, rng(h)], sa, start=True, stop=False)
                                mm = pe.matmul(o, b["tok"][:, 1, rng(h)], vt, start=False, stop=True)
                        if c == 0:
                            mm.then_inc(sem("rw_s1"), 1)
                        for h in range(2):
                            sa = b["xsa"][:, P + 64 * h:P + 64 * h + 64]
                            vt = b["tok"][:, 2 + c, rng(h)]
                            o = q[3 * s + 2][rng(h), P * c:P * c + P]
                            pe.matmul(o, sa, b["RB"][:, 2 * h + c, :], start=True, stop=False)
                            mm = pe.matmul(o, vt, b["RK"][:, 2 * h + c, :], start=False, stop=c == 0)
                            if c:
                                mm = pe.matmul(o, b["s1"][rng(h), 0:64], b["rt"][rng(h), P:S], start=False, stop=True)
                        mm.then_inc(sem("rw_y0" if c == 0 else "rw_y"), 1)
                for s in range(2):
                    pe.wait_ge(sem("rw_yc"), v(s))
                    pe.matmul(q[3 * s + 1][:, 0:S], bones[:], RB_[s]["y"], start=True, stop=True).then_inc(sem("rw_mu"), 1)
                for s in range(2):
                    pe.wait_ge(sem("rw_ysq"), v(s))
                    pe.matmul(q[3 * s + 1][:, S:2 * S], bones[:], RB_[s]["ysq"], start=True, stop=True).then_inc(sem("rw_var"), 1)
                halves.end()

        def touch(dve, k):
            dve.tensor_copy(touched[:, k:k + 1], eps[:, 0:1])

        def pred(dve, out_, mask, data):
            return dve.copy_predicated(out_, bc4(mask), data)

        def rw_vector(dve):
            for s in range(2):
                for key in ("M", "AK", "RB", "RK"):
                    o = dve.memset(RB_[s][key], 0.0)
            o.then_inc(*once("rw_zero"))
            dve.wait_ge(*after("rw_zero"))
            with dve.Fori(0, 8) as i:
                v = lambda s: i * 2 + (s + 1)
                ch = LoopChain(dve, "rw_dve", i, 32)
                def scan(s, b):
                    for c in range(2):
                        o = dve.tensor_tensor_scan(b["c"][:, P * c:P * c + P], ones[:, :], b["ld"][:, P * c:P * c + P], 0.0, ALU.mult, ALU.add)
                    return ch.do(o)

                def e_plus(s, b):
                    dve.wait_ge(sem("rw_e"), v(s))
                    return ch.do(dve.tensor_scalar(b["e"], b["e"], 1.0, None, ALU.add))

                for s in range(2):
                    dve.wait_ge(sem(f"rw_in{s}"), i * 16 + 16)
                    dve.tensor_scalar(RB_[s]["kk"], RB_[s]["in"][:, 1, :], col("k_k", i * 2 + s), None, ALU.mult).then_inc(sem("rw_kk0"), 1)
                k1 = [e_plus(s, RB_[s]) for s in range(2)]
                for s in range(2):
                    ch.need(k1[s])
                    dve.reciprocal(RB_[s]["e"], RB_[s]["e"]).then_inc(sem("rw_sig"), 1)
                k2 = []
                for s in range(2):
                    dve.wait_ge(sem("rw_sig"), v(s))
                    k2.append(ch.do(dve.tensor_scalar(RB_[s]["ld"], RB_[s]["e"][:, 0, :], -EXP_HALF, None, ALU.mult)))
                k3 = []
                for s in range(2):
                    ch.need(k2[s])
                    k3.append(scan(s, RB_[s]))
                k4 = []
                for s in range(2):
                    b = RB_[s]
                    ch.need(k3[s])
                    k4.append(ch.do(dve.tensor_tensor(chunks(b["cm"]), chunks(b["c"]), chunks(b["c"])[:, :, 63:64].broadcast_to([P, 2, P]), ALU.subtract)))
                for s in range(2):
                    b = RB_[s]
                    ch.need(k4[s])
                    dve.tensor_tensor(b["cml"], b["cm"], b["ld"], ALU.subtract).then_inc(sem("rw_cm"), 1)
                k5 = []
                for s in range(2):
                    dve.wait_ge(sem("rw_nrm"), v(s))
                    k5.append(ch.do(dve.tensor_scalar(RB_[s]["sq"], RB_[s]["sq"], 1e-12, None, ALU.max)))
                k6 = []
                for s in range(2):
                    ch.need(k5[s])
                    k6.append(ch.do(dve.reciprocal(RB_[s]["sq"], RB_[s]["sq"])))
                k7 = []
                for s in range(2):
                    ch.need(k6[s])
                    k7.append(ch.do(dve.tensor_tensor(RB_[s]["kk"], RB_[s]["kk"], RB_[s]["sq"], ALU.mult)))
                k8 = []
                for s in range(2):
                    b = RB_[s]
                    ch.need(k7[s])
                    k8.append(ch.do(dve.tensor_tensor(b["b"], b["kk"], b["e"][:, 1, :], ALU.mult)))
                for s in range(2):
                    b = RB_[s]
                    dve.wait_ge(sem("rw_exp"), v(s))
                    ch.do(dve.scalar_tensor_tensor(out=b["at"], in0=b["kk"], scalar=-1.0, in1=b["ex"][:, 2, :], op0=ALU.mult, op1=ALU.mult))
                    ch.need(k8[s])
                    dve.tensor_tensor(b["bt"], b["b"], b["ex"][:, 1, :], ALU.mult).then_inc(sem("rw_bt"), 1)
                for s in range(2):
                    b = RB_[s]
                    dve.wait_ge(sem("rw_k1"), v(s))
                    dve.scalar_tensor_tensor(out=b["t"], in0=b["in"][:, 0, :], scalar=col("r_k", i * 2 + s), in1=b["k1"],
                                             op0=ALU.mult, op1=ALU.mult).then_inc(sem("rw_rk"), 1)
                k9 = []
                for s in range(2):
                    b = RB_[s]
                    dve.wait_ge(sem("rw_start"), i * 4 + (2 * s + 2))
                    dve.wait_ge(sem("rw_m1"), v(s))
                    touch(dve, s)
                    ch.do(pred(dve, b["M"], m_low[:, :], bank4(3 * s)))
                    ch.do(pred(dve, b["T"], lowmask[:, 0, :], bank4(3 * s)))
                    ch.do(pred(dve, b["U"], upmask[:, 0, :], bank4(3 * s + 1)))
                    pred(dve, b["AK"], m_up[:, :], bank4(3 * s + 2)).then_inc(sem("rw_m1e"), 1)
                for s in range(2):
                    b = RB_[s]
                    dve.wait_ge(sem("rw_m2"), v(s))
                    touch(dve, 2 + s)
                    pred(dve, b["RB"], m_upi[:, :], bank4(3 * s))
                    pred(dve, b["RK"], m_upi[:, :], bank4(3 * s + 1)).then_inc(sem("rw_m2e"), 1)
                for s in range(2):
                    b = RB_[s]
                    dve.wait_ge(sem("rw_bs"), v(s))
                    dve.tensor_tensor(b["bon"], q[3 * s][:, 0:S], b["in"][:, 2, :], ALU.mult).then_inc(sem("rw_bon"), 1)
                for lv in range(6):
                    for s in range(2):
                        dve.wait_ge(sem("rw_g"), i * 12 + (2 * lv + s + 1))
                        touch(dve, 4 + 2 * lv + s)
                        pred(dve, RB_[s]["U"], upmask[:, lv + 1, :], bank4(3 * s)).then_inc(sem("rw_u"), 1)
                for s in range(2):
                    b = RB_[s]
                    dve.wait_ge(sem("rw_s1"), v(s))
                    dve.tensor_scalar(b["s1"][:, 0:64], q[3 * s + 1][:, S:S + 64], b["ex"][:, 0, P - 1:P], b["s1"][:, 64:65],
                                      ALU.mult, ALU.mult).then_inc(sem("rw_s1c"), 1)
                for s in range(2):
                    b = RB_[s]
                    dve.wait_ge(sem("rw_mu"), v(s))
                    dve.scalar_tensor_tensor(out=b["yc"], in0=q[3 * s + 1][:, 0:S], scalar=-1.0 / 64, in1=b["y"], op0=ALU.mult, op1=ALU.add)\
                       .then_inc(sem("rw_yd"), 1)
                k10 = []
                for s in range(2):
                    dve.wait_ge(sem("rw_sd"), v(s))
                    k10.append(ch.do(dve.reciprocal(RB_[s]["ysq"], RB_[s]["ysq"])))
                k = k10
                for f in (lambda s, b: dve.tensor_tensor(b["yc"], b["yc"], b["ysq"], ALU.mult),
                          lambda s, b: dve.tensor_scalar(b["yc"], b["yc"], col("lnx_w", i * 2 + s), col("lnx_b", i * 2 + s), ALU.mult, ALU.add),
                          lambda s, b: dve.tensor_tensor(b["yc"], b["yc"], b["bon"], ALU.add)):
                    nk = []
                    for s in range(2):
                        ch.need(k[s])
                        nk.append(ch.do(f(s, RB_[s])))
                    k = nk
                for s in range(2):
                    ch.need(k[s])
                    dve.tensor_tensor(RB_[s]["yc"], RB_[s]["yc"], RB_[s]["in"][:, 5, :], ALU.mult).then_inc(sem("rw_val"), 1)
                for s in range(2):
                    dve.wait_ge(sem("rw_hi"), v(s))
                    dve.tensor_tensor(tile(AL, i * 2 + s), RB_[s]["yc"], tile(AH, i * 2 + s).bitcast(F32), ALU.subtract)\
                       .then_inc(sem("rw_out"), 1)
                ch.end()


        def relu_scalar(act, idx):
            def evac(t, n, mh, bank):
                r, sqr = G[:, 16 + bank, :], G[:, 18 + bank, :]
                act.wait_ge(sem("w_used"), n * 2 + 2)
                if not (isinstance(t, int) and t < 2 and idx == 0):
                    act.wait_ge(sem("hid_done"), t + (idx - 1))
                act.activation(r, ps[bank][:, 0:S], ACT.Relu).then_inc(sem(f"proj_out{bank}"), 1)
                act.wait_ge(sem("hid_sq"), t + (idx + 1))
                act.activation(tile(BH, t), sqr, ACT.Copy).then_inc(sem("hid_hi"), 1)
            return evac

        def relu_vector(dve, idx):
            def evac(t, n, mh, bank):
                r, sqr = G[:, 16 + bank, :], G[:, 18 + bank, :]
                dve.wait_ge(sem(f"proj_out{bank}"), mh + 1)
                dve.tensor_tensor(sqr, r, r, ALU.mult).then_inc(sem("hid_sq"), 1)
                dve.wait_ge(sem("hid_hi"), t + (idx + 1))
                dve.tensor_tensor(tile(BL, t), sqr, tile(BH, t).bitcast(F32), ALU.subtract).then_inc(sem("hid_done"), 1)
            return evac

        block = ctx.enter_context(nc.Block())
        done2 = stop >= 2

        xtok = G[:, 0:16, :].rearrange("p (b k) n -> p b (k n)", b=2)
        mtok = G[:, 16:32, :].rearrange("p (b k) n -> p b (k n)", b=2)
        otok = xtok
        m32 = G[:, 50:60, :].rearrange("p a (b n) -> p (a b) n", n=P)
        spill_ap = spill.ap()

        def mlp(layer):
            return [(f"up{layer}_{x}", f"dn{layer}_{x}", 64 * layer + 16 * x) for x in range(4)]

        @block.sync
        def _(sp):
            sp.dma_start(mtok, a["mem"][0].rearrange("(b p) d -> p b d", p=P)).then_inc(sem("mem_in"), 16)
            sp.dma_start(xtok, a["x"][0].rearrange("(b p) d -> p b d", p=P)).then_inc(sem("x_in"), 16)
            for name, _c, special in phases:
                def body(t, n, nh, pair, mh, bank):
                    for j in range(2):
                        slot = 2 * pair + j
                        if not (isinstance(n, int) and n < 2):
                            sp.wait_ge(sem("w_lo"), n * 2 + (j - 3))
                        src, kind = SRC[name](t, j)
                        flat = raw[slot][:, :, :].rearrange("p k n -> p (k n)")
                        if kind == "xo":
                            dst = flat.rearrange("p (k n) -> p k n", k=4)
                        elif kind == "up96":
                            dst = flat[0:96, 0:512]
                        elif kind == "up256":
                            dst = flat.rearrange("p (k n) -> p k n", k=2)
                        else:
                            dst = raw[slot][:, :, 0:kind]
                        sp.dma_start(dst, src).then_inc(sem(f"w_loaded{slot}"), 16)
                if special:
                    for t in range(COUNT[name]):
                        n_ = N0[name] + t
                        body(t, n_, n_ // 2, n_ % 2, 0, 0)
                else:
                    over(sp, name, body, peel=2 if N0[name] == 0 else 0)
            for b in range(2):
                sp.wait_ge(sem("fin_d"), 4)
                sp.wait_ge(sem("fin_a"), 4)
                sp.dma_start(out[0, P * b:P * b + P, :], otok[:, b, :]).then_inc(sem("stored"), 16)
            sp.wait_ge(sem("stored"), 32)

        @block.gpsimd
        def _(pool):
            ch = Chain(pool, "pool_chain")
            pool.memset(prow, 0.0).then_inc(*once("prow_zero"))
            pool.memset(ident[:], 0.0)
            pool.memset(ones[:], 1.0)
            pool.memset(bones[:], 1.0)
            pool.memset(kge[:], 1.0)
            pool.memset(causal[:], 0.0)
            pool.memset(limit[:], 3e38)
            pool.memset(m32[:, 0:14, :], 0.0)
            ch.after(pool.memset(m32[:, 14:17, :], 1.0))
            pool.affine_select(out=ident[:], in_=ident[:], compare_op=ALU.not_equal, fill=1.0, base=0,
                               pattern=[[-1, P]], channel_multiplier=1).then_inc(*once("ident"))
            keep = lambda t, pattern, base, fill=0.0, op=ALU.is_ge, cm=1: pool.affine_select(
                out=t, in_=t, compare_op=op, fill=fill, base=base, pattern=pattern, channel_multiplier=cm)
            bo = bones[:, :].rearrange("p (b n) -> p b n", n=64)
            ch.after(keep(bo, [[-64, 2], [0, 64]], 0))
            keep(bo, [[64, 2], [0, 64]], 63, cm=-1)
            keep(kge[:], [[-1, P]], 0)
            keep(causal[:, 1, :], [[-1, P]], 0, NEG)
            for x, f in enumerate((0.0, NEG)):
                keep(limit[:, x, :], [[1, P]], 0, f, ALU.is_gt, -1)
            keep(m32[:, 14, :], [[-1, P]], 0, op=ALU.is_gt)
            keep(m32[:, 15, :], [[1, P]], 0, op=ALU.is_gt, cm=-1)
            keep(m32[:, 16, :], [[1, P]], 0, cm=-1)
            pool.memset(eps[:], EPS).then_inc(sem("sb_out"), 2)
            pool.memset(eps_ln[:], LNX_EPS).then_inc(sem("rw_out"), 2)
            pool.memset(stat[:], 0.0).then_inc(sem("att_out"), 2)
            lows, ups = [], []
            for l in range(1, 8):
                n = 2 ** l
                view = lambda x: m32[:, x, :].rearrange("p (b n) -> p b n", n=n)
                lows.append((view(l - 1)[:, :, 0:n // 2], n))
                ups.append((view(6 + l)[:, :, n // 2:n], n))
            for t, n in lows + ups:
                o = pool.memset(t, 1.0)
            ch.after(o)
            for (t, n), (u, _n) in zip(lows, ups):
                keep(t, [[-n, P // n], [0, n // 2]], -n // 2)
                o = keep(u, [[-n, P // n], [0, n // 2]], 0)
            ch.after(o)
            for (t, n), (u, _n) in zip(lows, ups):
                keep(t, [[n, P // n], [0, n // 2]], n - 1, cm=-1)
                o = keep(u, [[n, P // n], [0, n // 2]], n // 2 - 1, cm=-1)
            o.then_inc(sem("masks32"), 1)
            sb_pool(pool)
            gla_pool(pool)
            sgu_pool(pool)
            if stop >= 2:
                phase_done(pool, "xq")
                att_pool(pool, "xa")
            if stop >= 3:
                for name in SPILL:
                    spill_pool(pool, name)
                up_pool(pool)
                rw_pool(pool)
            if stop >= 5:
                phase_done(pool, "fq")
                pool.wait_ge(*after("f_ready"))
                att_pool(pool, "fa")

        @block.scalar
        def _(act):
            act.wait_ge(*after("prow_zero"))
            for src, r, cnt in rows:
                v = a[src]
                while len(v.shape) > 1:
                    v = v.rearrange("a b c -> (a b) c") if len(v.shape) == 3 else v.rearrange("a b -> (a b)")
                act.dma_start(prow[r % P:r % P + cnt, r // P, :], v.rearrange("(r c) -> r c", c=P)).then_inc(sem("prow_in"), 16)
            act.dma_start(gup[:], a["w_gla_gate_up"][0]).then_inc(sem("small_in"), 16)
            act.dma_start(bf[:], a["b_f_2"].rearrange("(n o) -> n o", o=1)).then_inc(sem("small_in"), 16)
            ch = Chain(act, "act_chain")
            for u in range(1, 16, 2):
                act.wait_ge(sem("tr"), u + 1)
                dst = G[:, 32 + 2 * u:34 + 2 * u, :] if u < 8 else X[:, 2 * u - 16:2 * u - 14, :]
                act.activation(dst, q[u % 4][:, :].rearrange("p (a n) -> p a n", a=2), ACT.Copy).then_inc(sem("tr_a"), 1)
            act.wait_ge(*after("prm_t"))
            act.activation(prm[:], q[4][:, :], ACT.Copy).then_inc(*once("prm"))
            for h in range(4):
                act.wait_ge(sem(f"w_loaded{h}"), 16)
                act.activation(wh[h][:], raw[h][:], ACT.Copy).then_inc(sem("w_hi"), 1)
            act.wait_ge(sem("masks32"), 1)
            act.wait_ge(sem("tr_a"), 8)
            act.wait_ge(sem("tr_d"), 8)
            norm_scalar(act, "mem")
            norm_scalar(act, "mix")
            for name in ("xkv", "in_a", "in_r", "in_b"):
                stream(act, name, peel=2 if name == "xkv" else 0)
            sb_scalar(act)
            gla_scalar(act, ch)
            sgu_scalar(act, ch)
            mix_scalar(act)
            stream(act, "out")
            phase_done(act, "out")
            if stop >= 2:
                norm_scalar(act, "xattn")
                stream(act, "xq")
                att_scalar(act, "xa")
                for t in range(4):
                    split_next(act, N0["xo"] + t, (N0["xo"] + t) // 2, (N0["xo"] + t) % 2, N0["xo"] + t >= TOTAL - 2)
                act.wait_ge(sem("xo_out"), 8)
            if stop >= 3:
                norm_scalar(act, "final1")
                act.wait_ge(sem("norm_done"), 4 * NIDX["final1"] + 4)
                norm_scalar(act, "rwkv")
                act.wait_ge(sem("norm_done"), 4 * NIDX["rwkv"] + 4)
                xs_bulk(act, "r", xs_scalar_part, xs_scalar_high)
                for name, nxt in (("rw_r", "k"), ("rw_k", "v"), ("rw_v", "w")):
                    stream(act, name, spill_scalar(act, name, nxt), peel=2 if name == "rw_r" else 0)
                stream(act, "rw_w1", lora_scalar(act, "rw_w1"))
                xs_bulk(act, "a", xs_scalar_part, xs_scalar_high)
                stream(act, "rw_a1", lora_scalar(act, "rw_a1"))
                xs_bulk(act, "g", xs_scalar_part, xs_scalar_high)
                stream(act, "rw_g1", lora_scalar(act, "rw_g1"))
                for t in range(6):
                    n = N0["rw_up"] + t
                    split_next(act, n, n // 2, n % 2, False)
                rw_scalar(act)
                stream(act, "rw_o")
                phase_done(act, "rw_o")
            for layer, lim in ((0, 4), (1, 6)):
                if layer == 1 and stop >= 5:
                    norm_scalar(act, "kv")
                    norm_scalar(act, "fox")
                    for name in ("fk", "fv", "ff"):
                        stream(act, name)
                    act.wait_ge(*after("f_in"))
                    ch.after(act.activation(fscr[0:16, 6, :], fscr[0:16, 5, :], ACT.Abs))
                    ch.after(act.activation(fscr[0:16, 6, :], fscr[0:16, 6, :], ACT.Exp, scale=-1.0))
                    act.activation(fscr[0:16, 6, :], fscr[0:16, 6, :], ACT.Ln, bias=1.0).then_inc(*once("f_ln"))
                    stream(act, "fq")
                    att_scalar(act, "fa")
                    stream(act, "fo")
                    phase_done(act, "fo")
                if stop >= lim:
                    norm_scalar(act, f"ffn{layer}")
                    for up, dn, idx in mlp(layer):
                        stream(act, up, relu_scalar(act, idx), peel=2 if idx == 0 else 0)
                        stream(act, dn)
                    phase_done(act, f"dn{layer}_3")
            norm_scalar(act, "final2")
            for u in range(1, 8, 2):
                act.wait_ge(sem("fin_t"), u + 1)
                act.activation(otok[:, u // 4, 512 * (u % 4):512 * (u % 4) + 512], q[u % 4][:, :], ACT.Copy).then_inc(sem("fin_a"), 1)

        @block.vector
        def _(dve):
            ch = Chain(dve, "dve_chain")
            for u in range(0, 16, 2):
                dve.wait_ge(sem("tr"), u + 1)
                dst = G[:, 32 + 2 * u:34 + 2 * u, :] if u < 8 else X[:, 2 * u - 16:2 * u - 14, :]
                dve.tensor_copy(dst, q[u % 4][:, :].rearrange("p (a n) -> p a n", a=2)).then_inc(sem("tr_d"), 1)
            dve.wait_ge(sem("masks32"), 1)
            dve.wait_ge(*after("ident"))
            dve.tensor_copy(lowmask[:], m32[:, 0:7, :])
            dve.tensor_copy(upmask[:], m32[:, 7:14, :])
            dve.tensor_copy(m_low[:], m32[:, 14, :])
            dve.tensor_copy(m_up[:], m32[:, 15, :])
            dve.tensor_copy(m_upi[:], m32[:, 16, :])
            dve.tensor_copy(m_id[:], ident[:]).then_inc(sem("masks"), 1)
            dve.wait_ge(sem("masks"), 1)
            dve.wait_ge(*after("prm"))
            pc = lambda key, n: prm[:, COL[key]:COL[key] + n]
            dve.tensor_scalar(omm[:], pc("x_mix", 96), -1.0, 1.0, ALU.mult, ALU.add)
            dve.tensor_scalar(neg[:, 0:16], pc("w0", 16), -1.0, None, ALU.mult)
            dve.tensor_scalar(neg[:, 16:32], pc("a0", 16), -1.0, None, ALU.mult)
            dve.tensor_scalar(neg[:, 32:48], pc("k_a", 16), -1.0, 1.0, ALU.mult, ALU.add).then_inc(*once("prm2"))
            for h in range(4):
                dve.wait_ge(sem("w_hi"), h + 1)
                dve.tensor_tensor(wl[h][:], raw[h][:], wh[h][:].bitcast(F32), ALU.subtract).then_inc(sem("w_lo"), 1)
            norm_vector(dve, "mem")
            norm_vector(dve, "mix")
            stream(dve, "xkv", out_copy(dve, G, 56), peel=2)
            stream(dve, "in_a", out_copy(dve, G, 0))
            stream(dve, "in_r", lambda t, n, mh, bank: (
                dve.wait_ge(sem("w_used"), n * 2 + 2),
                dve.tensor_copy(rT[:], ps[bank][0:16, 0:S]).then_inc(sem(f"proj_out{bank}"), 1)))
            stream(dve, "in_b", out_copy(dve, G, 40))
            sb_vector(dve)
            gla_vector(dve, ch)
            sgu_vector(dve, ch)
            mix_vector(dve, ch)
            stream(dve, "out", out_resid(dve))
            if stop >= 2:
                norm_vector(dve, "xattn")
                stream(dve, "xq", out_copy(dve, G, 16, SCALE))
                att_vector(dve, "xa")
                for t in range(4):
                    n = N0["xo"] + t
                    split_next(dve, n, n // 2, n % 2, n >= TOTAL - 2)
                    for j in range(2):
                        hc = 2 * t + j
                        dve.wait_ge(sem("w_used"), 2 * n + j + 1)
                        x = X[:, 2 * hc:2 * hc + 2, :]
                        dve.tensor_tensor(x, q[hc % 2][:, :].rearrange("p (a n) -> p a n", a=2), x, ALU.add).then_inc(sem("xo_out"), 1)
            if stop >= 3:
                norm_vector(dve, "final1")
                norm_vector(dve, "rwkv")
                xs_bulk(dve, "r", xs_vector_add, xs_vector_low)
                for name, nxt in (("rw_r", "k"), ("rw_k", "v"), ("rw_v", "w")):
                    stream(dve, name, spill_vector(dve, nxt))
                stream(dve, "rw_w1", lora_vector(dve, "rw_w1"))
                xs_bulk(dve, "a", xs_vector_add, xs_vector_low)
                stream(dve, "rw_a1", lora_vector(dve, "rw_a1"))
                xs_bulk(dve, "g", xs_vector_add, xs_vector_low)
                stream(dve, "rw_g1", lora_vector(dve, "rw_g1"))
                up_vector(dve)
                for b in range(2):
                    dve.wait_ge(sem(f"up_spilled{b}"), 16 * 6)
                rw_vector(dve)
                stream(dve, "rw_o", out_resid(dve))
            for layer, lim in ((0, 4), (1, 6)):
                if layer == 1 and stop >= 5:
                    norm_vector(dve, "kv")
                    norm_vector(dve, "fox")
                    stream(dve, "fk", out_copy(dve, G, 0))
                    stream(dve, "fv", out_copy(dve, G, 16))
                    stream(dve, "ff", lambda t, n, mh, bank: (
                        dve.wait_ge(sem("w_used"), n * 2 + 2),
                        dve.tensor_scalar(fscr[0:16, 5, :], ps[bank][0:16, 0:S], bf[:, 0:1], None, ALU.add).then_inc(sem(f"proj_out{bank}"), 1)))
                    phase_done(dve, "ff")
                    ch.after(dve.tensor_scalar(fscr[0:16, 7, :], fscr[0:16, 5, :], -1.0, 0.0, ALU.mult, ALU.max))
                    dve.tensor_copy(fscr[0:16, 8, :], fscr[0:16, 7, :]).then_inc(*once("f_in"))
                    dve.wait_ge(*after("f_ln"))
                    ch.after(dve.tensor_tensor(fscr[0:16, 7, :], fscr[0:16, 7, :], fscr[0:16, 6, :], ALU.add))
                    ch.after(dve.tensor_tensor_scan(cneg, ones[0:16, 0:1].broadcast_to([16, S]), fscr[0:16, 7, :], 0.0, ALU.mult, ALU.add))
                    dve.tensor_scalar(cpos, cneg, -1.0, None, ALU.mult).then_inc(*once("f_c"))
                    stream(dve, "fq", out_copy(dve, G, 32, SCALE))
                    dve.wait_ge(*after("f_t"))
                    dve.tensor_copy(fscr[:, 2, 0:32], q[0][:, 0:32]).then_inc(*once("f_ready"))
                    dve.wait_ge(*after("f_ready"))
                    att_vector(dve, "fa")
                    stream(dve, "fo", out_resid(dve))
                if stop >= lim:
                    norm_vector(dve, f"ffn{layer}")
                    for up, dn, idx in mlp(layer):
                        stream(dve, up, relu_vector(dve, idx))
                        stream(dve, dn, out_resid(dve))
            norm_vector(dve, "final2")
            for u in range(0, 8, 2):
                dve.wait_ge(sem("fin_t"), u + 1)
                dve.tensor_copy(otok[:, u // 4, 512 * (u % 4):512 * (u % 4) + 512], q[u % 4][:, :]).then_inc(sem("fin_d"), 1)

        @block.tensor
        def _(pe):
            pe.wait_ge(*after("ident"))
            for u in range(16):
                pe.wait_ge(sem("mem_in" if u < 8 else "x_in"), 16)
                if u > 3:
                    pe.wait_ge(sem("tr_a" if u % 2 else "tr_d"), (u - 4) // 2 + 1)
                tok = mtok if u < 8 else xtok
                for x in range(4):
                    k, b = 2 * (u % 8) + x // 2, x % 2
                    mm = pe.transpose(q[u % 4][:, P * x:P * x + P], tok[:, b, P * k:P * k + P], ident[:])
                mm.then_inc(sem("tr"), 1)
            pe.wait_ge(sem("prow_in"), 16 * len(rows))
            for x in range(NROW):
                mm = pe.transpose(q[4][:, P * x:P * x + P], prow[:, x, :], ident[:])
            mm.then_inc(*once("prm_t"))
            norm_tensor(pe, "mem")
            norm_tensor(pe, "mix")
            project(pe, "xkv", AH, AL, norm_ready("mem"))
            for name in ("in_a", "in_r", "in_b"):
                project(pe, name, BH, BL, norm_ready("mix"))
            pe.wait_ge(sem("small_in"), 32)
            sb_tensor(pe)
            gla_tensor(pe)
            sgu_tensor(pe)
            mix_tensor(pe)
            project(pe, "out", BH, BL, ("mix_done", lambda g: g + 1))
            if stop >= 2:
                norm_tensor(pe, "xattn")
                project(pe, "xq", AH, AL, norm_ready("xattn"))
                phase_done(pe, "xq")
                att_tensor(pe, "xa")
                pe.wait_ge(sem("att_out"), 6)
                for hc in range(8):
                    n = N0["xo"] + hc // 2
                    slot = 2 * (n % 2) + hc % 2
                    pe.wait_ge(sem("w_lo"), 2 * N0["xo"] + hc + 1)
                    if hc > 1:
                        pe.wait_ge(sem("xo_out"), hc - 1)
                    for o in range(2):
                        dst = q[hc % 2][:, S * o:S * o + S]
                        for k in range(4):
                            h_, l_ = (w[slot][:, :, :].rearrange("p k n -> p (k n)")[:, S * k + P * o:S * k + P * o + P] for w in (wh, wl))
                            pe.matmul(dst, h_, BH[:, k, :], start=k == 0, stop=False)
                            pe.matmul(dst, h_, BL[:, k, :], start=False, stop=False)
                            mm = pe.matmul(dst, l_, BH[:, k, :], start=False, stop=k == 3)
                    mm.then_inc(sem("w_used"), 1)
                pe.wait_ge(sem("xo_out"), 8)
            if stop >= 3:
                norm_tensor(pe, "final1")
                norm_tensor(pe, "rwkv")
                for name, mix in (("rw_r", "r"), ("rw_k", "k"), ("rw_v", "v"), ("rw_w1", "w"), ("rw_a1", "a"), ("rw_g1", "g")):
                    d = MIXES[mix][2]
                    project(pe, name, d[0], d[1], xs_ready(mix))
                up_tensor(pe)
                pe.wait_ge(sem("up_out"), 12)
                rw_tensor(pe)
                pe.wait_ge(sem("rw_out"), 18)
                project(pe, "rw_o", AH, AL)
            for layer, lim in ((0, 4), (1, 6)):
                if layer == 1 and stop >= 5:
                    norm_tensor(pe, "kv")
                    norm_tensor(pe, "fox")
                    for name in ("fk", "fv", "ff"):
                        project(pe, name, AH, AL, norm_ready("kv"))
                    project(pe, "fq", BH, BL, norm_ready("fox"))
                    pe.wait_ge(*after("f_c"))
                    for b in range(2):
                        mm = pe.transpose(q[0][:, 16 * b:16 * b + 16], cpos[:, P * b:P * b + P], ident[0:16, 0:16])
                    mm.then_inc(*once("f_t"))
                    pe.wait_ge(*after("f_ready"))
                    phase_done(pe, "fq")
                    att_tensor(pe, "fa")
                    pe.wait_ge(sem("att_out"), 22)
                    project(pe, "fo", AH, AL)
                if stop >= lim:
                    norm_tensor(pe, f"ffn{layer}")
                    for up, dn, idx in mlp(layer):
                        project(pe, up, AH, AL, norm_ready(f"ffn{layer}"))
                        project(pe, dn, BH, BL, ("hid_done", lambda g, idx=idx: idx + 4 * g + 4))
            norm_tensor(pe, "final2")
            norm_all(pe, "final2")
            for u in range(8):
                if u > 3:
                    pe.wait_ge(sem("fin_a" if u % 2 else "fin_d"), (u - 4) // 2 + 1)
                for x in range(4):
                    mm = pe.transpose(q[u % 4][:, P * x:P * x + P], X[:, 4 * (u % 4) + x, P * (u // 4):P * (u // 4) + P], ident[:])
                mm.then_inc(sem("fin_t"), 1)


def kernel(**inputs):
    import numpy as _np
    import concourse.bacc as _bacc
    from concourse import mybir as _mybir
    from concourse.bass_utils import run_bass_kernel_spmd as _run

    nc = _bacc.Bacc("TRN2", target_bir_lowering=False, num_devices=1)
    arrays, args = {}, {}
    for name, value in inputs.items():
        value = _np.ascontiguousarray(value)
        if value.size == 0:
            continue
        arrays[f"in_{name}_dram"] = value
        args[name] = nc.dram_tensor(f"in_{name}_dram", value.shape, _mybir.dt.from_np(value.dtype), kind="ExternalInput").ap()
    out = nc.dram_tensor("out_0_dram", (1, S, D), F32, kind="ExternalOutput").ap()
    two_block_kernel(nc, args, out, 6)
    r = _run(nc, [arrays], core_ids=[0])
    return r.results[0]["out_0_dram"]
```

```python
from contextlib import ExitStack

import concourse.bass as bass
from concourse import mybir

F32 = mybir.dt.float32
F32R = mybir.dt.float32r
U8 = mybir.dt.uint8
ACT = mybir.ActivationFunctionType
ALU = mybir.AluOpType
AXX = mybir.AxisListType.X

P = 128
D = 2048
KT = D // P
S = 256
HALF = KT // 2
EPS = 1e-6
LNX_EPS = 64e-5
NEG = -1e30
GELU = 1.5957691216057308
EXP_HALF = 0.6065306597126334

PHASES = [
    ("xkv", 8, False), ("in_a", 40, False), ("in_r", 1, False), ("in_b", 16, False),
    ("out", 16, False), ("xq", 4, False), ("xo", 4, True),
    ("rw_r", 16, False), ("rw_k", 16, False), ("rw_v", 16, False), ("rw_w1", 1, False),
    ("rw_a1", 1, False), ("rw_g1", 2, False), ("rw_up", 6, True), ("rw_o", 16, False),
    ("up0", 64, False), ("mlp0", 64, False),
    ("fk", 16, False), ("fv", 16, False), ("ff", 1, False), ("fq", 16, False), ("fo", 16, False),
    ("mlp1", 128, False),
]


def mlp_phases(layer):
    return [(f"{w}{layer}_{q}", 16, False) for q in range(4) for w in ("up", "dn")]


PHASES = [p for p in PHASES if p[0] not in ("up0", "mlp0", "mlp1")]
_at = [p[0] for p in PHASES].index("rw_o") + 1
PHASES = PHASES[:_at] + mlp_phases(0) + PHASES[_at:] + mlp_phases(1)
STOPS = {1: "out", 2: "xo", 3: "rw_o", 4: "dn0_3", 5: "fo", 6: "dn1_3"}


def two_block_kernel(nc, a, out, stop=6):
    phases = PHASES[:[p[0] for p in PHASES].index(STOPS[stop]) + 1]
    N0, M0, COUNT, n, m = {}, {}, {}, 0, 0
    for name, count, special in phases:
        N0[name], M0[name], COUNT[name] = n, m, count
        n += count
        m += 0 if special else count
    TOTAL = n

    with ExitStack() as ctx:
        TILE = S * 4
        arena = ctx.enter_context(nc.sbuf_tensor("arena", [P, 192 * 256], F32))
        base = BASE = 16512

        def at(name, tiles_at, shape, dt=F32):
            return nc.alloc_sbuf_tensor_at(name, shape, dt, offset=BASE + tiles_at * TILE)

        X = at("x_resid", 0, [P, KT, S])
        raw = [at(f"w_raw{i}", 16 + 4 * i, [P, HALF, P]) for i in range(4)]
        wh = [at(f"w_high{i}", 32 + 4 * i, [P, HALF, P], F32R) for i in range(4)]
        wl = [at(f"w_low{i}", 48 + 4 * i, [P, HALF, P], F32R) for i in range(4)]
        AH, AL = at("a_high", 64, [P, KT, S], F32R), at("a_low", 80, [P, KT, S], F32R)
        BH, BL = at("b_high", 96, [P, KT, S], F32R), at("b_low", 112, [P, KT, S], F32R)
        AF, BF = at("a_scratch", 64, [P, 32, S]), at("b_scratch", 96, [P, 32, S])
        G = at("g", 128, [P, 64, S])
        LH, LL = at("lora_high", 184, [P, 4, S], F32R), at("lora_low", 188, [P, 4, S], F32R)

        def sb(name, shape, dt=F32):
            return ctx.enter_context(nc.sbuf_tensor(name, shape, dt))

        ident, ones, bones, kge = (sb(x, [P, P]) for x in ("ident", "ones", "bones", "kge"))
        lowmask, upmask = sb("lowmask", [P, 7, P], U8), sb("upmask", [P, 7, P], U8)
        m_low, m_up, m_upi, m_id = (sb(x, [P, P], U8) for x in ("m_low", "m_up", "m_upi", "m_id"))
        causal = sb("causal", [P, 2, P])
        limit = sb("limit", [P, 2, P])
        NROW = 4
        prm = sb("prm", [P, NROW * P])
        omm = sb("one_minus_mix", [P, 6 * KT])
        neg = sb("negated", [P, 3 * KT])
        eps, eps_ln = sb("eps", [P, 1]), sb("eps_ln", [P, 1])
        rT, gup = sb("gla_r", [16, S]), sb("gate_up", [16, S])
        w_s = G[:, 8:10, :].rearrange("p a (b n) -> p (a b) n", n=P)
        b_s = G[0:1, 10:12, :].rearrange("p a (b n) -> p (a b) n", n=P)
        bf = sb("b_f_sb", [16, 1])
        rstd = sb("rstd", [P, 2, S])
        touched = sb("touched", [P, 20])
        s1_all = sb("rw_states", [P, 4, 66])
        stat = sb("stat", [P, 2, 8])
        ps = [ctx.enter_context(nc.psum_tensor(f"proj{i}", [P, 512], F32)) for i in range(2)]
        q = [ctx.enter_context(nc.psum_tensor(f"side{i}", [P, 512], F32)) for i in range(6)]
        spill = nc.dram_tensor("rwkv_spill", [6, KT, P, S], F32)

        names = {}

        def sem(name):
            if name not in names:
                names[name] = ctx.enter_context(nc.semaphore(name))
            return names[name]

        ONCE = {"tensor": ["prm_t", "gl_z", "gl_vt", "gl_o", "sg_wt", "sg_ss", "sg_vt", "sg_mixed", "f_t"],
                "vector": ["prm2", "gl_x", "gl_vtc", "gl_out", "sg_v", "sg_vtc", "sg_out", "rw_zero", "f_in", "f_c", "f_ready"],
                "scalar": ["prm", "gl_ln", "sg_sq", "sg_std", "sg_wtc", "f_ln"],
                "gpsimd": ["prow_zero", "ident", "gl_zero", "sg_wm"]}
        POSITION = {event: (f"{engine}_once", k + 1) for engine, events in ONCE.items() for k, event in enumerate(events)}

        def once(event):
            return sem(POSITION[event][0]), 1

        def after(event):
            return sem(POSITION[event][0]), POSITION[event][1]

        vec = [("norm_mix", "norm_mix", 16), ("out_norm", "out_norm", 16), ("norm_xattn", "norm_xattn", 16),
               ("norm_mem", "norm_mem", 16), ("final_norm", "final_norm", 16), ("mix_norm", "mix_norm_2", 32),
               ("w0", "rwkv_w0_2", 16),
               ("ffn_norm", "ffn_norm_2", 32), ("final2", "final_norm_2", 16), ("a0", "rwkv_a0_2", 16),
               ("k_k", "rwkv_k_k_2", 16), ("k_a", "rwkv_k_a_2", 16), ("r_k", "rwkv_r_k_2", 16), ("lnx_w", "rwkv_lnx_w_2", 16),
               ("x_mix", "rwkv_x_mix_2", 96), ("lnx_b", "rwkv_lnx_b_2", 16), ("kv_norm", "kv_norm_2", 16),
               ("sgu_norm", "sgu_norm", 4), ("b_gla", "b_gla_gate", 2)]
        COL, row = {}, 0
        rows = []
        for key, src, cnt in vec:
            assert row // P == (row + cnt - 1) // P, key
            COL[key] = row
            rows.append((src, row, cnt))
            row += cnt
        assert row <= NROW * P
        prow = G[:, 48:50, :].rearrange("p a (b c) -> p (a b) c", c=P)

        def col(key, k=0):
            return prm[:, bass.ds(COL[key] + k, 1)] if not isinstance(k, int) else prm[:, COL[key] + k:COL[key] + k + 1]

        def tile(t, k):
            return t[:, bass.ds(k, 1), :].rearrange("p a n -> p (a n)") if not isinstance(k, int) else t[:, k, :]

        def rows_of(w):
            return w.rearrange("(k p) n -> p k n", p=P)

        def cols(w, c0, width=P):
            view = rows_of(w)
            return lambda t, j: (view[:, HALF * j:HALF * j + HALF, bass.ds(t * P + c0, width)], width)

        def xo_src(t, j):
            return rows_of(a["w_xo"][0])[:, :, bass.ds(t * 512 + j * 256, 256)], "xo"

        win = a["w_in"][0]
        SRC = {"xkv": cols(a["w_xkv"][0], 0), "in_a": cols(win, 0), "in_r": cols(win, 5120, 16),
               "in_b": cols(win, 5136), "out": cols(a["w_out"][0], 0), "xq": cols(a["w_xq"][0], 0),
               "xo": xo_src, "rw_r": cols(a["rwkv_w_rkv_2"][0, 0], 0), "rw_k": cols(a["rwkv_w_rkv_2"][0, 1], 0),
               "rw_v": cols(a["rwkv_w_rkv_2"][0, 2], 0), "rw_w1": cols(a["rwkv_w1_2"][0], 0, 96),
               "rw_a1": cols(a["rwkv_a1_2"][0], 0, 96), "rw_g1": cols(a["rwkv_g1_2"][0], 0),
               "rw_o": cols(a["rwkv_w_o_2"][0], 0),
               "fk": cols(a["w_kvf_2"], 0), "fv": cols(a["w_kvf_2"], D), "ff": cols(a["w_kvf_2"], 2 * D, 16),
               "fq": cols(a["fox_w_q_2"][0], 0), "fo": cols(a["fox_w_o_2"][0], 0)}
        for layer in range(2):
            for qq in range(4):
                SRC[f"up{layer}_{qq}"] = cols(a["mlp_w_up_2"][layer], qq * D)
                SRC[f"dn{layer}_{qq}"] = cols(a["mlp_w_down_2"][layer][qq * D:(qq + 1) * D], 0)

        def up_src(t, j):
            which, part = divmod(2 * t + j, 4)
            if which < 2:
                w = a["rwkv_w2_2" if which == 0 else "rwkv_a2_2"][0]
                return w[:, part * 512:part * 512 + 512], "up96"
            return rows_of(a["rwkv_g2_2"][0])[:, :, part * 512:part * 512 + 512], "up256"

        SRC["rw_up"] = up_src

        def over(eng, name, body, peel=0, tail=0):
            cnt, n0, m0 = COUNT[name], N0[name], M0[name]

            def one(t0, i, u):
                t = t0 + 2 * i + u
                nb, mb = n0 + t0 + u, m0 + t0 + u
                body(t, nb + 2 * i, nb // 2 + i, nb % 2, mb // 2 + i, mb % 2)

            for t in range(min(peel, cnt)):
                one(t, 0, 0)
            start, end = min(peel, cnt), cnt - tail
            pairs = max(0, end - start) // 2
            if pairs >= 2:
                with eng.Fori(0, pairs) as i:
                    one(start, i, 0)
                    one(start, i, 1)
                start += 2 * pairs
            for t in range(start, cnt):
                one(t, 0, 0)

        def phase_done(eng, name):
            m_end = M0[name] + COUNT[name]
            eng.wait_ge(sem("proj_out0"), (m_end + 1) // 2)
            eng.wait_ge(sem("proj_out1"), m_end // 2)

        def split_next(eng, n, nh, pair, last):
            if last:
                return
            for j in range(2):
                slot = 2 * pair + j
                if eng is nc.scalar:
                    eng.wait_ge(sem("w_used"), n * 2 + j + 1)
                    eng.wait_ge(sem(f"w_loaded{slot}"), nh * 16 + 32)
                    eng.activation(wh[slot][:], raw[slot][:], ACT.Copy).then_inc(sem("w_hi"), 1)
                else:
                    eng.wait_ge(sem("w_hi"), n * 2 + j + 5)
                    eng.tensor_tensor(wl[slot][:], raw[slot][:], wh[slot][:].bitcast(F32), ALU.subtract)\
                       .then_inc(sem("w_lo"), 1)

        last_phase = phases[-1][0]

        def stream(eng, name, evac=None, peel=0):
            def run(tail_only):
                def body(t, n, nh, pair, mh, bank):
                    split_next(eng, n, nh, pair, tail_only and isinstance(n, int) and n >= TOTAL - 2)
                    if evac:
                        evac(t, n, mh, bank)
                return body
            over(eng, name, run(name == last_phase), peel=peel, tail=2 if name == last_phase else 0)

        def project(pe, name, hi, lo, groups=None, k_of=None):
            def body(t, n, nh, pair, mh, bank):
                if not (isinstance(mh, int) and mh == 0):
                    pe.wait_ge(sem(f"proj_out{bank}"), mh)
                for j in range(2):
                    slot = 2 * pair + j
                    pe.wait_ge(sem("w_lo"), n * 2 + j + 1)
                    for k in range(HALF):
                        kk = HALF * j + k
                        if groups and kk % 4 == 0:
                            pe.wait_ge(sem(groups[0]), groups[1](kk // 4))
                        o = ps[bank][:, 0:S]
                        pe.matmul(o, wh[slot][:, k, :], hi[:, kk, :], start=kk == 0, stop=False)
                        pe.matmul(o, wh[slot][:, k, :], lo[:, kk, :], start=False, stop=False)
                        mm = pe.matmul(o, wl[slot][:, k, :], hi[:, kk, :], start=False, stop=kk == KT - 1)
                    mm.then_inc(sem("w_used"), 1)
            over(pe, name, body, peel=2 if M0[name] == 0 else 0)

        def out_copy(eng, dst, k0, scale=None):
            def evac(t, n, mh, bank):
                eng.wait_ge(sem("w_used"), n * 2 + 2)
                if scale:
                    o = eng.tensor_scalar(tile(dst, k0 + t), ps[bank][:, 0:S], scale, None, ALU.mult)
                else:
                    o = eng.tensor_copy(tile(dst, k0 + t), ps[bank][:, 0:S])
                o.then_inc(sem(f"proj_out{bank}"), 1)
            return evac

        def out_resid(eng):
            def evac(t, n, mh, bank):
                eng.wait_ge(sem("w_used"), n * 2 + 2)
                eng.tensor_tensor(tile(X, t), ps[bank][:, 0:S], tile(X, t), ALU.add).then_inc(sem(f"proj_out{bank}"), 1)
            return evac

        NORMS = {
            "mem": (0, G, 32, "norm_mem", (AH, AL), BF, 0),
            "mix": (1, X, 0, "norm_mix", (BH, BL), G, 0),
            "xattn": (2, X, 0, "norm_xattn", (AH, AL), G, 0),
            "final1": (3, X, 0, "final_norm", None, G, 0),
            "rwkv": (4, X, 0, "mix_norm", G, G, 16),
            "ffn0": (5, X, 0, "ffn_norm", (AH, AL), G, 0),
            "kv": (6, X, 0, "kv_norm", (AH, AL), G, 48),
            "fox": (7, X, 0, ("mix_norm", 16), (BH, BL), G, 48),
            "ffn1": (8, X, 0, ("ffn_norm", 16), (AH, AL), G, 0),
            "final2": (9, X, 0, "final2", None, G, 0),
        }
        run_norms = ["mem", "mix", "xattn", "final1", "rwkv", "ffn0", "kv", "fox", "ffn1", "final2"]
        if stop == 1:
            run_norms = ["mem", "mix"]
        elif stop == 2:
            run_norms = run_norms[:3]
        else:
            run_norms = run_norms[:{3: 5, 4: 6, 5: 8, 6: 9}[stop]]
        run_norms = run_norms + ["final2"]
        NIDX = {x: i for i, x in enumerate(run_norms)}

        def norm_scalar(act, name):
            _, src, k0, gain, dst, scr, s0 = NORMS[name]
            i = NIDX[name]
            if i:
                act.wait_ge(sem("norm_done"), 4 * i)
            for g in range(4):
                act.activation(scr[:, s0 + 4 * g:s0 + 4 * g + 4, :], src[:, k0 + 4 * g:k0 + 4 * g + 4, :], ACT.Square)\
                   .then_inc(sem("norm_sq"), 1)
            act.wait_ge(sem("norm_sum"), i + 1)
            act.activation(rstd[:, 0, :], q[0][:, 0:S], ACT.Sqrt, scale=1.0 / D, bias=eps[:, 0:1]).then_inc(sem("norm_std"), 1)
            if isinstance(dst, tuple):
                for g in range(4):
                    act.wait_ge(sem("norm_val"), 4 * norm_hl(name) + g + 1)
                    act.activation(dst[0][:, 4 * g:4 * g + 4, :], scr[:, s0 + 4 * g:s0 + 4 * g + 4, :], ACT.Copy)\
                       .then_inc(sem("norm_hi"), 1)

        def norm_hl(name):
            return sum(isinstance(NORMS[x][4], tuple) for x in run_norms[:NIDX[name]])

        def norm_tensor(pe, name):
            _, src, k0, gain, dst, scr, s0 = NORMS[name]
            for g in range(4):
                pe.wait_ge(sem("norm_sq"), 4 * NIDX[name] + g + 1)
                for k in range(4):
                    mm = pe.matmul(q[0][:, 0:S], ones[:], scr[:, s0 + 4 * g + k, :], start=g + k == 0, stop=g + k == 6)
            mm.then_inc(sem("norm_sum"), 1)

        def norm_vector(dve, name):
            _, src, k0, gain, dst, scr, s0 = NORMS[name]
            i = NIDX[name]
            gkey, goff = gain if isinstance(gain, tuple) else (gain, 0)
            split = isinstance(dst, tuple)
            to, t0 = (scr, s0) if split else ((X, 0) if dst is None else (dst, 0))
            dve.wait_ge(sem("norm_std"), i + 1)
            dve.reciprocal(rstd[:, 1, :], rstd[:, 0, :]).then_inc(sem("norm_rec"), 1)
            dve.wait_ge(sem("norm_rec"), i + 1)

            def low(g):
                dve.wait_ge(sem("norm_hi"), 4 * norm_hl(name) + g + 1)
                dve.tensor_tensor(dst[1][:, 4 * g:4 * g + 4, :], scr[:, s0 + 4 * g:s0 + 4 * g + 4, :],
                                  dst[0][:, 4 * g:4 * g + 4, :].bitcast(F32), ALU.subtract).then_inc(sem("norm_done"), 1)

            for g in range(4):
                for k in range(4 * g, 4 * g + 4):
                    o = dve.scalar_tensor_tensor(out=to[:, t0 + k, :], in0=src[:, k0 + k, :], scalar=col(gkey, goff + k),
                                                 in1=rstd[:, 1, :], op0=ALU.mult, op1=ALU.mult)
                o.then_inc(sem("norm_val" if split else "norm_done"), 1)
                if split and g:
                    low(g - 1)
            if split:
                low(3)

        def norm_ready(name):
            return ("norm_done", lambda g: 4 * NIDX[name] + g + 1)

        def norm_all(eng, name):
            eng.wait_ge(sem("norm_done"), 4 * NIDX[name] + 4)

        ATT = {"xa": dict(heads=4, hb=0, q0=16, k0=56, v0=60, causal=False, scr=(G, 20), dst=(BH, BL)),
               "fa": dict(heads=16, hb=4, q0=32, k0=0, v0=16, causal=True, scr=(BF, 0), dst=(AH, AL))}
        SCALE = float(P) ** -0.5

        def att_bufs(name, s):
            t, o = ATT[name]["scr"]
            o += 9 * s
            flat = lambda b, k: t[:, o + b:o + b + k, :].rearrange("p a n -> p (a n)")
            return dict(qS=flat(0, 1), vS=flat(1, 1), S=flat(2, 2), P=flat(4, 2), PT=flat(6, 2), vt=flat(8, 1))

        fscr = G[:, 48:64, :]
        cneg, cpos = fscr[0:16, 0, :], fscr[0:16, 1, :]
        cT = fscr[:, 2, 0:32].rearrange("p (a h) -> p a h", a=2)
        selS = [fscr[0:16, 3 + s, 0:P] for s in range(2)]

        def settled(pool):
            pool.wait_ge(sem("masks32"), 1)

        def att_pool(pool, name):
            c = ATT[name]
            with pool.Fori(0, c["heads"] // 2) as i:
                for s in range(2):
                    b = att_bufs(name, s)
                    pool.wait_ge(sem("att_out"), i * 2 + (s + 1 + c["hb"]))
                    settled(pool)
                    pool.tensor_copy(b["qS"], tile(G, i * 2 + (c["q0"] + s))).then_inc(sem("att_staged"), 1)
                    pool.tensor_copy(b["vS"], tile(G, i * 2 + (c["v0"] + s))).then_inc(sem("att_staged"), 1)
                    if c["causal"]:
                        pool.tensor_copy(selS[s], ident[0:16, bass.ds(i * 2 + s, 1)].broadcast_to([16, P]))\
                            .then_inc(sem("att_staged"), 1)

        def att_tensor(pe, name):
            c = ATT[name]
            per = 3 if c["causal"] else 2
            W = (P, S) if c["causal"] else (S, S)
            with pe.Fori(0, c["heads"] // 2) as i:
                for s in range(2):
                    b = att_bufs(name, s)
                    pe.wait_ge(sem("att_staged"), i * (2 * per) + ((s + 1) * per + 2 * c["hb"]))
                    for t in range(2):
                        o = q[s][:, S * t:S * t + W[t]]
                        mm = pe.matmul(o, b["qS"][:, P * t:P * t + P], tile(G, i * 2 + (c["k0"] + s))[:, 0:W[t]],
                                       start=True, stop=not c["causal"])
                        if c["causal"]:
                            mm = pe.matmul(o, selS[s], cneg[:, 0:W[t]], start=False, stop=True)
                    mm.then_inc(sem("att_score"), 1)
                    for t in range(2):
                        mm = pe.transpose(q[4 + s][:, P * t:P * t + P], b["vS"][:, P * t:P * t + P], ident[:])
                    mm.then_inc(sem("att_vt"), 1)
                for s in range(2):
                    b = att_bufs(name, s)
                    pe.wait_ge(sem("att_prob"), i * 2 + (s + 1 + c["hb"]))
                    o = 0
                    for k in range(2):
                        for t in range(2):
                            if P * k < W[t]:
                                mm = pe.transpose(q[2 + s][:, o:o + P], b["P"][:, S * t + P * k:S * t + P * k + P], ident[:])
                                o += P
                    mm.then_inc(sem("att_pt"), 1)
                for s in range(2):
                    b = att_bufs(name, s)
                    pe.wait_ge(sem("att_ptc"), i * 2 + (s + 1 + c["hb"]))
                    pe.wait_ge(sem("att_vtc"), i * 2 + (s + 1 + c["hb"]))
                    pe.matmul(q[4 + s][:, S:2 * S], b["vt"][:, 0:P], b["PT"][:, 0:S], start=True, stop=False)
                    lo = P if c["causal"] else 0
                    pe.matmul(q[4 + s][:, S + lo:2 * S], b["vt"][:, P:2 * P], b["PT"][:, S:2 * S - lo], start=False, stop=True)\
                        .then_inc(sem("att_o"), 1)

        def att_scalar(act, name):
            c = ATT[name]
            W = (P, S) if c["causal"] else (S, S)
            n = 3 * P if c["causal"] else 4 * P
            with act.Fori(0, c["heads"] // 2) as i:
                for s in range(2):
                    b = att_bufs(name, s)
                    act.wait_ge(sem("att_max"), i * 2 + (s + 1 + c["hb"]))
                    src = b["S"] if c["causal"] else q[s]
                    for t in range(2):
                        e = act.activation(b["P"][:, S * t:S * t + W[t]], src[:, S * t:S * t + W[t]], ACT.Exp,
                                           bias=stat[:, s, t:t + 1], accum_out=stat[:, s, 2 + t:3 + t])
                    e.then_inc(sem("att_exp"), 1)
                for s in range(2):
                    b = att_bufs(name, s)
                    act.wait_ge(sem("att_pt"), i * 2 + (s + 1 + c["hb"]))
                    act.activation(b["PT"][:, 0:n], q[2 + s][:, 0:n], ACT.Copy).then_inc(sem("att_ptc"), 1)
                for s in range(2):
                    act.wait_ge(sem("att_o"), i * 2 + (s + 1 + c["hb"]))
                    act.activation(tile(c["dst"][0], i * 2 + s), q[4 + s][:, S:2 * S], ACT.Copy).then_inc(sem("att_ohi"), 1)

        def att_vector(dve, name):
            c = ATT[name]
            W = (P, S) if c["causal"] else (S, S)
            with dve.Fori(0, c["heads"] // 2) as i:
                for s in range(2):
                    b = att_bufs(name, s)
                    dve.wait_ge(sem("att_score"), i * 2 + (s + 1 + c["hb"]))
                    src = q[s]
                    if c["causal"]:
                        cm = causal[:, :, :].rearrange("p a n -> p (a n)")
                        for t in range(2):
                            o = dve.scalar_tensor_tensor(out=b["S"][:, S * t:S * t + W[t]], in0=q[s][:, S * t:S * t + W[t]],
                                                         scalar=cT[:, t, bass.ds(i * 2 + s, 1)], in1=cm[:, S - W[t]:S],
                                                         op0=ALU.add, op1=ALU.add)
                        o.then_inc(sem("att_masked"), 1)
                        dve.wait_ge(sem("att_masked"), i * 2 + (s + 1))
                        src = b["S"]
                    for t in range(2):
                        o = dve.tensor_reduce(stat[:, s, t:t + 1], src[:, S * t:S * t + W[t]], AXX, ALU.max, negate=True)
                    o.then_inc(sem("att_max"), 1)
                    dve.wait_ge(sem("att_vt"), i * 2 + (s + 1 + c["hb"]))
                    dve.tensor_copy(b["vt"], q[4 + s][:, 0:S]).then_inc(sem("att_vtc"), 1)
                for s in range(2):
                    b = att_bufs(name, s)
                    dve.wait_ge(sem("att_exp"), i * 2 + (s + 1 + c["hb"]))
                    dve.reciprocal(stat[:, s, 4:6], stat[:, s, 2:4]).then_inc(sem("att_rec"), 1)
                    dve.wait_ge(sem("att_rec"), i * 2 + (s + 1 + c["hb"]))
                    for t in range(2):
                        p_ = b["P"][:, S * t:S * t + W[t]]
                        o = dve.tensor_scalar(p_, p_, stat[:, s, 4 + t:5 + t], None, ALU.mult)
                    o.then_inc(sem("att_prob"), 1)
                for s in range(2):
                    dve.wait_ge(sem("att_ohi"), i * 2 + (s + 1 + c["hb"]))
                    dve.tensor_tensor(tile(c["dst"][1], i * 2 + s), q[4 + s][:, S:2 * S],
                                      tile(c["dst"][0], i * 2 + s).bitcast(F32), ALU.subtract).then_inc(sem("att_out"), 1)

        class Chain:

            def __init__(self, eng, name):
                self.eng, self.sem, self.n = eng, sem(name), 0

            def after(self, ins):
                self.n += 1
                ins.then_inc(self.sem, 1)
                self.eng.wait_ge(self.sem, self.n)

        def sb_bufs(s):
            flat = lambda b, n=1: AF[:, 10 * s + b:10 * s + b + n, :].rearrange("p a n -> p (a n)")
            return dict(kS=flat(0), vS=flat(1), qS=flat(2), z=flat(3, 2)[:, 0:384], e=flat(5, 2)[:, 0:384],
                        a=flat(7, 2)[:, 0:384], vt=flat(9))

        def diag(t):
            return t.rearrange("p (b n) -> p b n", n=P)[:, 0:3:2, :]

        def sb_pool(pool):
            phase_done(pool, "in_b")
            with pool.Fori(0, 4) as i:
                for s in range(2):
                    b = sb_bufs(s)
                    pool.wait_ge(sem("sb_out"), i * 2 + (s + 1))
                    settled(pool)
                    pool.tensor_copy(b["kS"], tile(G, i * 2 + (8 + s))).then_inc(sem("sb_staged"), 1)
                    pool.tensor_copy(b["vS"], tile(G, i * 2 + (16 + s))).then_inc(sem("sb_staged"), 1)

        def sb_tensor(pe):
            phase_done(pe, "in_b")
            with pe.Fori(0, 4) as i:
                for s in range(2):
                    b = sb_bufs(s)
                    pe.wait_ge(sem("sb_staged"), i * 4 + 2 * (s + 1))
                    query = tile(G, i * 2 + s)
                    pe.matmul(q[s][:, 0:S], b["kS"][:, 0:P], query, start=True, stop=True)
                    pe.matmul(q[s][:, S:384], b["kS"][:, P:S], query[:, P:S], start=True, stop=True).then_inc(sem("sb_z"), 1)
                    pe.transpose(q[2 + s][:, 0:P], b["vS"][:, 0:P], ident[:])
                    pe.transpose(q[2 + s][:, P:S], b["vS"][:, P:S], ident[:]).then_inc(sem("sb_vt"), 1)
                for s in range(2):
                    b = sb_bufs(s)
                    pe.wait_ge(sem("sb_spm"), i * 2 + (s + 1))
                    pe.matmul(q[4 + s][:, 0:S], kge[:], b["e"][:, 0:S], start=True, stop=False)
                    pe.matmul(q[4 + s][:, P:S], ones[:], b["e"][:, S:384], start=False, stop=True)
                    pe.matmul(q[4 + s][:, S:384], kge[:], b["e"][:, S:384], start=True, stop=True).then_inc(sem("sb_sum"), 1)
                for s in range(2):
                    b = sb_bufs(s)
                    pe.wait_ge(sem("sb_vtc"), i * 2 + (s + 1))
                    pe.wait_ge(sem("sb_exp"), i * 2 + (s + 1))
                    pe.matmul(q[s][:, 0:S], b["vt"][:, 0:P], b["a"][:, 0:S], start=True, stop=False)
                    pe.matmul(q[s][:, P:S], b["vt"][:, P:S], b["a"][:, S:384], start=False, stop=True).then_inc(sem("sb_o"), 1)

        def sb_scalar(act):
            with act.Fori(0, 4) as i:
                for s in range(2):
                    b = sb_bufs(s)
                    act.wait_ge(sem("sb_z"), i * 2 + (s + 1))
                    act.activation(b["z"], q[s][:, 0:384], ACT.Copy, scale=SCALE).then_inc(sem("sb_zc"), 1)
                    act.activation(b["e"], q[s][:, 0:384], ACT.Abs, scale=SCALE).then_inc(sem("sb_abs"), 1)
                for s in range(2):
                    b = sb_bufs(s)
                    act.wait_ge(sem("sb_abs"), i * 2 + (s + 1))
                    act.activation(b["e"], b["e"], ACT.Exp, scale=-1.0).then_inc(sem("sb_e"), 1)
                for s in range(2):
                    b = sb_bufs(s)
                    act.wait_ge(sem("sb_e"), i * 2 + (s + 1))
                    act.activation(b["e"], b["e"], ACT.Ln, bias=1.0).then_inc(sem("sb_ln"), 1)
                for s in range(2):
                    b = sb_bufs(s)
                    act.wait_ge(sem("sb_dm"), i * 2 + (s + 1))
                    act.activation(b["a"], b["a"], ACT.Exp).then_inc(sem("sb_exp"), 1)

        def sb_vector(dve):
            with dve.Fori(0, 4) as i:
                for s in range(2):
                    b = sb_bufs(s)
                    dve.wait_ge(sem("sb_vt"), i * 2 + (s + 1))
                    dve.tensor_copy(b["vt"], q[2 + s][:, 0:S]).then_inc(sem("sb_vtc"), 1)
                for s in range(2):
                    b = sb_bufs(s)
                    dve.wait_ge(sem("sb_ln"), i * 2 + (s + 1))
                    dve.scalar_tensor_tensor(out=b["e"], in0=b["z"], scalar=0.0, in1=b["e"], op0=ALU.max, op1=ALU.add)\
                       .then_inc(sem("sb_sp"), 1)
                for s in range(2):
                    b = sb_bufs(s)
                    dve.wait_ge(sem("sb_sp"), i * 2 + (s + 1))
                    dve.tensor_tensor(diag(b["e"]), diag(b["e"]), limit[:, 0, :].unsqueeze(1).broadcast_to([P, 2, P]), ALU.min)\
                       .then_inc(sem("sb_spm"), 1)
                for s in range(2):
                    b = sb_bufs(s)
                    dve.wait_ge(sem("sb_sum"), i * 2 + (s + 1))
                    dve.scalar_tensor_tensor(out=b["a"], in0=q[4 + s][:, 0:384], scalar=-1.0, in1=b["z"], op0=ALU.mult, op1=ALU.add)\
                       .then_inc(sem("sb_d"), 1)
                for s in range(2):
                    b = sb_bufs(s)
                    dve.wait_ge(sem("sb_d"), i * 2 + (s + 1))
                    dve.tensor_tensor(diag(b["a"]), diag(b["a"]), limit[:, 1, :].unsqueeze(1).broadcast_to([P, 2, P]), ALU.min)\
                       .then_inc(sem("sb_dm"), 1)
                for s in range(2):
                    dve.wait_ge(sem("sb_o"), i * 2 + (s + 1))
                    dve.tensor_copy(tile(G, i * 2 + s), q[s][:, 0:S]).then_inc(sem("sb_out"), 1)

        af = lambda o, n: AF[:, o:o + n, :]
        gl_c, gl_x, gl_l = af(0, 2), af(2, 2), af(4, 2)
        gl_E, gl_Q, gl_K = [af(6, 2), af(8, 2)], [af(10, 2), af(12, 2)], [af(14, 2), af(16, 2)]
        gl_AT = af(18, 6).rearrange("p a (b n) -> p (a b) n", n=P).rearrange("p (x h) n -> p x h n", x=3)
        gl_vt = af(24, 4).rearrange("p a (b n) -> p (a b) n", n=P).rearrange("p (x h) n -> p x h n", x=2)
        gl_d, gl_nd = af(28, 2), af(30, 2)

        def level(t, l):
            return t.rearrange("p a (b n) -> p (a b) n", n=2 ** l)

        def bank4(b):
            return q[b][:, :].rearrange("p (h n) -> p h n", h=4)

        def gla_pool(pool):
            pool.wait_ge(sem("sb_out"), 10)
            pool.dma_start(w_s, a["w_sgu"][0].rearrange("g t s -> t g s")).then_inc(sem("sgu_in"), 16)
            pool.dma_start(b_s, a["b_sgu"]).then_inc(sem("sgu_in"), 16)
            pool.memset(gl_AT, 0.0).then_inc(*once("gl_zero"))
            for l in range(1, 9):
                pool.wait_ge(sem("gl_E"), l)
                if l > 2:
                    pool.wait_ge(sem("gl_mm"), l - 2)
                pool.tensor_tensor(gl_K[l % 2], G[:, 34:36, :], gl_E[l % 2], ALU.mult).then_inc(sem("gl_K"), 1)

        def gla_scalar(act, ch):
            act.wait_ge(*after("gl_x"))
            ch.after(act.activation(gl_l, gl_x, ACT.Abs))
            ch.after(act.activation(gl_l, gl_l, ACT.Exp, scale=-1.0))
            act.activation(gl_l, gl_l, ACT.Ln, bias=1.0).then_inc(*once("gl_ln"))
            for l in range(1, 9):
                act.wait_ge(sem("gl_nd"), l)
                if l > 2:
                    act.wait_ge(sem("gl_K"), l - 2)
                    act.wait_ge(sem("gl_Q"), l - 2)
                act.activation(gl_E[l % 2], gl_nd, ACT.Exp).then_inc(sem("gl_E"), 1)

        def gla_vector(dve, ch):
            dve.wait_ge(*after("gl_z"))
            dve.wait_ge(sem("sb_out"), 10)
            for j in range(2):
                o = dve.tensor_scalar(gl_x[:, j, :], q[0][:, S * j:S * j + S], col("b_gla", j), None, ALU.add)
            o.then_inc(*once("gl_x"))
            dve.wait_ge(*after("gl_x"))
            ch.after(dve.tensor_scalar(gl_d, gl_x, -1.0, 0.0, ALU.mult, ALU.max))
            dve.wait_ge(*after("gl_ln"))
            ch.after(dve.tensor_tensor(gl_d, gl_d, gl_l, ALU.add))
            ch.after(dve.tensor_scalar(gl_d, gl_d, -1.0 / 16.0, None, ALU.mult))
            for j in range(2):
                o = dve.tensor_tensor_scan(gl_c[:, j, :], ones[:, 0:1].broadcast_to([P, S]), gl_d[:, j, :], 0.0, ALU.mult, ALU.add)
            ch.after(o)
            ch.after(dve.tensor_scalar(G[:, 32:34, :], G[:, 32:34, :], 0.125, None, ALU.mult))

            def pick(l, lv):
                dve.wait_ge(sem("gl_mm"), lv)
                b0 = 2 * (lv % 2)
                if l == 8:
                    o = dve.tensor_copy(gl_AT[:, 1], bank4(b0))
                else:
                    mask = m_id[:, :] if l == 0 else upmask[:, l - 1, :]
                    for x, b in ((0, b0), (2, b0 + 1)):
                        o = dve.copy_predicated(gl_AT[:, x], mask.unsqueeze(1).broadcast_to([P, 4, P]), bank4(b))
                o.then_inc(sem("gl_pick"), 1)

            dve.wait_ge(*after("gl_zero"))
            for l in range(1, 9):
                c = level(gl_c, l)
                n = 2 ** l
                if l > 1:
                    dve.wait_ge(sem("gl_E"), l - 1)
                ch.after(dve.tensor_tensor(level(gl_d, l), c, c[:, :, n // 2 - 1:n // 2].broadcast_to([P, 512 // n, n]), ALU.subtract))
                dve.scalar_tensor_tensor(out=gl_nd, in0=gl_d, scalar=-1.0, in1=gl_d, op0=ALU.mult, op1=ALU.min).then_inc(sem("gl_nd"), 1)
                if l > 1:
                    pick(l - 1, l - 1)
                dve.wait_ge(sem("gl_E"), l)
                dve.tensor_tensor(gl_Q[l % 2], G[:, 32:34, :], gl_E[l % 2], ALU.mult).then_inc(sem("gl_Q"), 1)
            pick(8, 8)
            pick(0, 9)
            dve.wait_ge(*after("gl_vt"))
            for x in range(2):
                o = dve.tensor_copy(gl_vt[:, x], bank4(4 + x))
            o.then_inc(*once("gl_vtc"))
            dve.wait_ge(*after("gl_o"))
            for x in range(2):
                o = dve.tensor_copy(G[:, 32 + 2 * x:34 + 2 * x, :], q[x][:, :].rearrange("p (a n) -> p a n", a=2))
            o.then_inc(*once("gl_out"))

        def gla_tensor(pe):
            rows_done = Chain(pe, "rows_done")
            pe.wait_ge(sem("sb_out"), 10)
            for j in range(2):
                mm = pe.matmul(q[0][:, S * j:S * j + S], gup[:, P * j:P * j + P], rT[:, :], start=True, stop=True)
            mm.then_inc(*once("gl_z"))
            for h in range(4):
                for x in range(2):
                    mm = pe.transpose(q[4 + x][:, P * h:P * h + P], G[:, 36 + h, P * x:P * x + P], ident[:])
            mm.then_inc(*once("gl_vt"))
            pe.wait_ge(*after("gl_x"))
            for lv, l in enumerate([1, 2, 3, 4, 5, 6, 7, 8, 0], 1):
                if l:
                    pe.wait_ge(sem("gl_Q"), l)
                    pe.wait_ge(sem("gl_K"), l)
                if lv > 2:
                    pe.wait_ge(sem("gl_pick"), lv - 2)
                kk, qq = (gl_K[l % 2], gl_Q[l % 2]) if l else (G[:, 34:36, :], G[:, 32:34, :])
                for h in (0, 2, 1, 3):
                    for x, (ts, tt) in enumerate([(0, 1)] if l == 8 else [(0, 0), (1, 1)]):
                        r = slice(64 * (h % 2), 64 * (h % 2) + 64)
                        mm = pe.matmul(q[2 * (lv % 2) + x][:, P * h:P * h + P], kk[r, h // 2, P * ts:P * ts + P],
                                       qq[r, h // 2, P * tt:P * tt + P], start=True, stop=True)
                    if h == 2:
                        rows_done.after(mm)
                mm.then_inc(sem("gl_mm"), 1)
            pe.wait_ge(sem("gl_pick"), 9)
            pe.wait_ge(*after("gl_vtc"))
            for h in range(4):
                o = q[h // 2][:, S * (h % 2):S * (h % 2) + S]
                pe.matmul(o[:, 0:P], gl_vt[:, 0, h, :], gl_AT[:, 0, h, :], start=True, stop=True)
                pe.matmul(o[:, P:S], gl_vt[:, 0, h, :], gl_AT[:, 1, h, :], start=True, stop=False)
                mm = pe.matmul(o[:, P:S], gl_vt[:, 1, h, :], gl_AT[:, 2, h, :], start=False, stop=True)
            mm.then_inc(*once("gl_o"))

        sg_e, sg_sq = af(0, 8), af(8, 4)
        sg_vt = af(12, 4).rearrange("p a (b n) -> p (a b) n", n=P).rearrange("p (x h) n -> p x h n", x=2)
        sg_w = af(16, 2).rearrange("p a (b n) -> p (a b) n", n=P)

        def sgu_scalar(act, ch):
            act.wait_ge(*after("gl_out"))
            for h, lo in ((0, 4), (1, 0)):
                x, e = G[:, 44 + lo:48 + lo, :], sg_e[:, lo:lo + 4, :]
                act.activation(e, x, ACT.Square).then_inc(sem("sg_x2"), 1)
                act.wait_ge(sem("sg_arg"), h + 1)
                act.activation(e, e, ACT.Exp, scale=-GELU).then_inc(sem("sg_exp"), 1)
            act.wait_ge(sem("sg_gelu"), 1)
            act.activation(sg_sq, G[:, 48:52, :], ACT.Square).then_inc(*once("sg_sq"))
            act.wait_ge(*after("sg_ss"))
            act.activation(rstd[:, 0, :], q[0][:, 0:S], ACT.Sqrt, scale=1.0 / 512, bias=eps[:, 0:1]).then_inc(*once("sg_std"))
            act.wait_ge(*after("sg_wt"))
            act.activation(sg_w, bank4(3), ACT.Copy).then_inc(*once("sg_wtc"))

        def sgu_vector(dve, ch):
            for h, lo in ((0, 4), (1, 0)):
                x, e = G[:, 44 + lo:48 + lo, :], sg_e[:, lo:lo + 4, :]
                dve.wait_ge(sem("sg_x2"), h + 1)
                ch.after(dve.tensor_scalar(e, e, 0.044715, 1.0, ALU.mult, ALU.add))
                dve.tensor_tensor(e, e, x, ALU.mult).then_inc(sem("sg_arg"), 1)
                dve.wait_ge(sem("sg_exp"), h + 1)
                ch.after(dve.tensor_scalar(e, e, 1.0, None, ALU.add))
                ch.after(dve.reciprocal(e, e))
                dve.tensor_tensor(x, x, e, ALU.mult).then_inc(sem("sg_gelu"), 1)
            dve.wait_ge(*after("sg_std"))
            ch.after(dve.reciprocal(rstd[:, 1, :], rstd[:, 0, :]))
            for g in range(4):
                o = dve.scalar_tensor_tensor(out=G[:, 48 + g, :], in0=G[:, 48 + g, :], scalar=col("sgu_norm", g),
                                             in1=rstd[:, 1, :], op0=ALU.mult, op1=ALU.mult)
            o.then_inc(*once("sg_v"))
            dve.wait_ge(*after("sg_vt"))
            for x in range(2):
                o = dve.tensor_copy(sg_vt[:, x], bank4(1 + x))
            o.then_inc(*once("sg_vtc"))
            dve.wait_ge(*after("sg_mixed"))
            for x in range(2):
                u = G[:, 44 + 2 * x:46 + 2 * x, :]
                o = dve.tensor_tensor(u, q[4 + x][:, :].rearrange("p (a n) -> p a n", a=2), u, ALU.mult)
            o.then_inc(*once("sg_out"))

        def sgu_pool(pool):
            pool.wait_ge(*after("sg_wtc"))
            pool.affine_select(out=sg_w, in_=sg_w, compare_op=ALU.is_ge, fill=0.0, base=0,
                               pattern=[[0, 4], [1, P]], channel_multiplier=-1).then_inc(*once("sg_wm"))

        def sgu_tensor(pe):
            pe.wait_ge(*after("gl_out"))
            pe.wait_ge(sem("sgu_in"), 32)
            for g in range(4):
                mm = pe.transpose(q[3][:, P * g:P * g + P], w_s[:, g, :], ident[:])
            mm.then_inc(*once("sg_wt"))
            pe.wait_ge(*after("sg_sq"))
            for g in range(4):
                mm = pe.matmul(q[0][:, 0:S], ones[:], sg_sq[:, g, :], start=g == 0, stop=g == 3)
            mm.then_inc(*once("sg_ss"))
            pe.wait_ge(*after("sg_v"))
            for g in range(4):
                for x in range(2):
                    mm = pe.transpose(q[1 + x][:, P * g:P * g + P], G[:, 48 + g, P * x:P * x + P], ident[:])
            mm.then_inc(*once("sg_vt"))
            pe.wait_ge(*after("sg_vtc"))
            pe.wait_ge(*after("sg_wm"))
            for g in range(4):
                for x in range(2):
                    o = q[4 + g // 2][:, S * (g % 2) + P * x:S * (g % 2) + P * x + P]
                    pe.matmul(o, sg_vt[:, x, g, :], sg_w[:, g, :], start=True, stop=False)
                    mm = pe.matmul(o, ones[0:1, :], b_s[0:1, g, :], start=False, stop=True)
            mm.then_inc(*once("sg_mixed"))

        MIX_O, MIX_G = [0, 4, 32, 44], [24, 28, 40, 52]

        def mix_scalar(act):
            act.wait_ge(*after("sg_out"))
            for g in range(4):
                act.activation(af(4 * g, 4), G[:, MIX_G[g]:MIX_G[g] + 4, :], ACT.Exp, scale=-1.0).then_inc(sem("mix_e"), 1)
            for g in range(4):
                act.activation(af(16 + 4 * g, 4), G[:, MIX_O[g]:MIX_O[g] + 4, :], ACT.Square).then_inc(sem("mix_sq"), 1)
                act.wait_ge(sem("mix_ss"), g + 1)
                for x in range(2):
                    o = act.activation(af(16 + 4 * g + 2 * x, 2), q[2 * (g % 2) + x][:, :].rearrange("p (a n) -> p a n", a=2),
                                       ACT.Sqrt, scale=1.0 / P, bias=eps[:, 0:1])
                o.then_inc(sem("mix_std"), 1)
                if g:
                    act.wait_ge(sem("mix_val"), g)
                    act.activation(BH[:, 4 * g - 4:4 * g, :], af(4 * g - 4, 4), ACT.Copy).then_inc(sem("mix_hi"), 1)
            act.wait_ge(sem("mix_val"), 4)
            act.activation(BH[:, 12:16, :], af(12, 4), ACT.Copy).then_inc(sem("mix_hi"), 1)

        def mix_tensor(pe):
            for g in range(4):
                pe.wait_ge(sem("mix_sq"), g + 1)
                if g > 1:
                    pe.wait_ge(sem("mix_std"), g - 1)
                for k in range(4):
                    mm = pe.matmul(q[2 * (g % 2) + k // 2][:, S * (k % 2):S * (k % 2) + S], ones[:], AF[:, 16 + 4 * g + k, :],
                                   start=True, stop=True)
                mm.then_inc(sem("mix_ss"), 1)

        def mix_vector(dve, ch):
            def low(g):
                dve.wait_ge(sem("mix_hi"), g + 1)
                dve.tensor_tensor(BL[:, 4 * g:4 * g + 4, :], af(4 * g, 4), BH[:, 4 * g:4 * g + 4, :].bitcast(F32), ALU.subtract)\
                   .then_inc(sem("mix_done"), 1)

            for g in range(4):
                e, r, o = af(4 * g, 4), af(16 + 4 * g, 4), MIX_O[g]
                dve.wait_ge(sem("mix_e"), g + 1)
                ch.after(dve.tensor_scalar(e, e, 1.0, None, ALU.add))
                ch.after(dve.reciprocal(e, e))
                ch.after(dve.tensor_tensor(e, e, G[:, MIX_G[g]:MIX_G[g] + 4, :], ALU.mult))
                dve.wait_ge(sem("mix_std"), g + 1)
                ch.after(dve.reciprocal(r, r))
                for k in range(4):
                    i = dve.scalar_tensor_tensor(out=AF[:, 16 + 4 * g + k, :], in0=G[:, o + k, :], scalar=col("out_norm", 4 * g + k),
                                                 in1=AF[:, 16 + 4 * g + k, :], op0=ALU.mult, op1=ALU.mult)
                ch.after(i)
                dve.tensor_tensor(e, e, r, ALU.mult).then_inc(sem("mix_val"), 1)
                if g:
                    low(g - 1)
            low(3)

        class LoopChain:

            def __init__(self, eng, name, i, per):
                self.eng, self.sem, self.i, self.per, self.k = eng, sem(name), i, per, 0

            def do(self, ins):
                ins.then_inc(self.sem, 1)
                self.k += 1
                return self.k

            def need(self, k):
                self.eng.wait_ge(self.sem, self.i * self.per + k)

            def end(self):
                assert self.k == self.per, self.k

        H, XT = G, G[:, 16:32, :]
        MIXES = {"r": (0, 0, (AH, AL)), "k": (1, 1, (BH, BL)), "v": (2, 2, (AH, AL)), "w": (3, 3, (BH, BL)),
                 "a": (4, 4, (AH, AL)), "g": (5, 5, (BH, BL))}

        def xs_scalar_part(act, mix, t):
            m, c, dst = MIXES[mix]
            if m:
                act.wait_ge(sem("xs_done"), t + (16 * m - 15))
            src = omm[:, bass.ds(t + 16 * c, 1)] if not isinstance(t, int) else omm[:, 16 * c + t:16 * c + t + 1]
            act.activation(tile(XT, t), tile(H, t), ACT.Copy, scale=src).then_inc(sem("xs_here"), 1)

        def xs_scalar_high(act, mix, t):
            m, c, dst = MIXES[mix]
            act.wait_ge(sem("xs_val"), t + (16 * m + 1))
            act.activation(tile(dst[0], t), tile(XT, t), ACT.Copy).then_inc(sem("xs_hi"), 1)

        def xs_vector_add(dve, mix, t):
            m, c, dst = MIXES[mix]
            dve.wait_ge(sem("xs_here"), t + (16 * m + 1))
            x = tile(XT, t)
            dve.scalar_tensor_tensor(out=x[:, 1:S], in0=tile(H, t)[:, 0:S - 1], scalar=col("x_mix", t + 16 * c),
                                     in1=x[:, 1:S], op0=ALU.mult, op1=ALU.add).then_inc(sem("xs_val"), 1)

        def xs_vector_low(dve, mix, t):
            m, c, dst = MIXES[mix]
            dve.wait_ge(sem("xs_hi"), t + (16 * m + 1))
            dve.tensor_tensor(tile(dst[1], t), tile(XT, t), tile(dst[0], t).bitcast(F32), ALU.subtract).then_inc(sem("xs_done"), 1)

        def xs_bulk(eng, mix, first, second):
            with eng.Fori(0, 4) as i:
                for u in range(4):
                    first(eng, mix, i * 4 + u)
                for u in range(4):
                    second(eng, mix, i * 4 + u)

        def xs_ready(mix):
            return ("xs_done", lambda g: 16 * MIXES[mix][0] + 4 * g + 4)

        SPILL = {"rw_r": 0, "rw_k": 1, "rw_v": 2}

        def spill_before(name, mh, bank):
            m0 = M0["rw_r"]
            return mh - (m0 // 2 if m0 % 2 == bank else (m0 + 1) // 2)

        def spill_scalar(act, name, nxt):
            def evac(t, n, mh, bank):
                act.wait_ge(sem("w_used"), n * 2 + 2)
                before = spill_before(name, mh, bank)
                if not (isinstance(before, int) and before == 0):
                    act.wait_ge(sem(f"spilled{bank}"), before * 16)
                act.activation(G[:, 40 + bank, :], ps[bank][:, 0:S], ACT.Copy).then_inc(sem(f"proj_out{bank}"), 1)
                xs_scalar_part(act, nxt, t)
                xs_scalar_high(act, nxt, t)
            return evac

        def spill_vector(dve, nxt):
            def evac(t, n, mh, bank):
                xs_vector_add(dve, nxt, t)
                xs_vector_low(dve, nxt, t)
            return evac

        def spill_pool(pool, name):
            def body(t, n, nh, pair, mh, bank):
                pool.wait_ge(sem(f"proj_out{bank}"), mh + 1)
                settled(pool)
                pool.dma_start(spill_ap[SPILL[name], bass.ds(t, 1)].rearrange("a p n -> p (a n)"), G[:, 40 + bank, :])\
                    .then_inc(sem(f"spilled{bank}"), 16)
            over(pool, name, body)

        LORA = {"rw_w1": (0, 96, ACT.Tanh), "rw_a1": (1, 96, ACT.Copy), "rw_g1": (2, P, ACT.Sigmoid)}

        def lora_scalar(act, name):
            k0, parts, func = LORA[name]

            def evac(t, n, mh, bank):
                f = G[0:parts, 36 + k0 + t, :]
                act.wait_ge(sem("w_used"), n * 2 + 2)
                act.activation(f, ps[bank][0:parts, 0:S], func).then_inc(sem(f"proj_out{bank}"), 1)
                act.wait_ge(sem(f"proj_out{bank}"), mh + 1)
                act.activation(LH[0:parts, k0 + t, :], f, ACT.Copy).then_inc(sem("lora_hi"), 1)
            return evac

        def lora_vector(dve, name):
            k0, parts, func = LORA[name]

            def evac(t, n, mh, bank):
                dve.wait_ge(sem("lora_hi"), k0 + t + 1)
                dve.tensor_tensor(LL[0:parts, k0 + t, :], G[0:parts, 36 + k0 + t, :], LH[0:parts, k0 + t, :].bitcast(F32), ALU.subtract)\
                   .then_inc(sem("lora_done"), 1)
            return evac

        def up_tensor(pe):
            n0 = N0["rw_up"]
            for hc in range(12):
                which, part = divmod(hc, 4)
                slot = 2 * ((n0 + hc // 2) % 2) + hc % 2
                pe.wait_ge(sem("w_lo"), 2 * n0 + hc + 1)
                pe.wait_ge(sem("lora_done"), (1, 2, 4)[which])
                if hc > 1:
                    pe.wait_ge(sem("up_out"), hc - 1)
                kn, parts = ((1, 96), (1, 96), (2, P))[which]
                flat = lambda w: w[slot][:, :, :].rearrange("p k n -> p (k n)")
                for o in range(4):
                    dst = q[2 * (hc % 2) + o // 2][:, S * (o % 2):S * (o % 2) + S]
                    for k in range(kn):
                        c = slice(512 * k + P * o, 512 * k + P * o + P)
                        x = which + k
                        pe.matmul(dst, flat(wh)[0:parts, c], LH[0:parts, x, :], start=k == 0, stop=False)
                        pe.matmul(dst, flat(wh)[0:parts, c], LL[0:parts, x, :], start=False, stop=False)
                        mm = pe.matmul(dst, flat(wl)[0:parts, c], LH[0:parts, x, :], start=False, stop=k == kn - 1)
                mm.then_inc(sem("w_used"), 1)

        def up_vector(dve):
            n0 = N0["rw_up"]
            for t in range(6):
                split_next(dve, n0 + t, (n0 + t) // 2, (n0 + t) % 2, n0 + t >= TOTAL - 2)
                for j in range(2):
                    hc = 2 * t + j
                    dve.wait_ge(sem("w_used"), 2 * n0 + hc + 1)
                    if hc > 1:
                        dve.wait_ge(sem(f"up_spilled{hc % 2}"), 16 * (hc // 2))
                    for x in range(2):
                        g = 44 + 4 * (hc % 2) + 2 * x
                        o = dve.tensor_copy(G[:, g:g + 2, :], q[2 * (hc % 2) + x][:, :].rearrange("p (a n) -> p a n", a=2))
                    o.then_inc(sem("up_out"), 1)

        def up_pool(pool):
            for hc in range(12):
                which, part = divmod(hc, 4)
                pool.wait_ge(sem("up_out"), hc + 1)
                pool.dma_start(spill_ap[3 + which, 4 * part:4 * part + 4].rearrange("a p n -> p a n"),
                               G[:, 44 + 4 * (hc % 2):48 + 4 * (hc % 2), :]).then_inc(sem(f"up_spilled{hc % 2}"), 16)

        def rw_layout():
            left = [[G, 0, 64], [BF, 0, 32]]

            def take(cnt, blocks=False):
                for piece in left:
                    if piece[2] >= cnt:
                        view = piece[0][:, piece[1]:piece[1] + cnt, :]
                        piece[1] += cnt
                        piece[2] -= cnt
                        if blocks:
                            return view.rearrange("p a (b n) -> p (a b) n", n=P)
                        return view.rearrange("p a n -> p (a n)") if cnt == 1 else view
                raise AssertionError(cnt)

            temps, cores = [], []
            for s in range(2):
                t = dict(zip(("in", "ex"), (take(4), take(3))))
                t.update((key, take(1)) for key in ("ld", "c", "cm", "kk", "sq", "t"))
                temps.append(t)
                b = {key: take(2, True) for key in ("M", "AK", "RB", "RK", "U", "T", "PP", "tok")}
                b.update((key, take(1)) for key in ("xsa", "y", "yc", "ysq"))
                cores.append(b)
            sets = []
            for par in range(2):
                sets.append([])
                for s in range(2):
                    t = {key: take(1) for key in ("at", "bt", "kt", "rt", "bon")}
                    t["vg"] = take(2)
                    sets[par].append(t)
            for par in range(2):
                for s in range(2):
                    sets[par][s]["s1"] = s1_all[:, 2 * par + s, :]
            return temps, cores, sets

        RW_T, RW_C, RW_S = rw_layout()
        chunks = lambda t: t.rearrange("p (c n) -> p c n", n=P)
        rng = lambda h: slice(64 * h, 64 * h + 64)

        def bc4(m):
            return m.unsqueeze(1).broadcast_to([P, 4, P])

        def omka(j):
            return neg[:, bass.ds(j + 32, 1)] if not isinstance(j, int) else neg[:, j + 32:j + 33]

        def ncol(j):
            return neg[:, bass.ds(j, 1)] if not isinstance(j, int) else neg[:, j:j + 1]

        def turns(eng, start, turn):
            start(0, 0)
            with eng.Fori(0, 3) as ii:
                turn(ii * 2, 0, ii * 2 + 1)
                turn(ii * 2 + 1, 1, ii * 2 + 2)
            turn(6, 0, 7)
            turn(7, 1, None)

        def rw_pool(pool):
            for b in range(2):
                pool.wait_ge(sem(f"spilled{b}"), 16 * 24)
                pool.wait_ge(sem(f"up_spilled{b}"), 16 * 6)
            phase_done(pool, "rw_g1")
            pool.wait_ge(*after("rw_zero"))

            def load(j, par):
                for s in range(2):
                    pool.wait_ge(sem("rw_out"), j * 2 + (s + 1))
                    pool.wait_ge(sem("rw_bon"), j * 2 + (s + 1))
                    settled(pool)
                    pair = bass.ds(j * 2 + s, 1) if not isinstance(j, int) else slice(j * 2 + s, j * 2 + s + 1)
                    part = lambda x: spill_ap[x, pair].rearrange("x a p n -> p x (a n)")
                    pool.dma_start(RW_T[s]["in"][:, 2:4, :], part(slice(3, 5))).then_inc(sem(f"rw_in{s}"), 16)
                    pool.dma_start(RW_T[s]["in"][:, 0:2, :], part(slice(0, 2))).then_inc(sem(f"rw_in{s}"), 16)
                    pool.dma_start(RW_S[par][s]["vg"], part(slice(2, 6, 3))).then_inc(sem(f"rw_in{s}"), 16)

            def ahead(j, par):
                load(j, par)
                for s in range(2):
                    b, t = RW_S[par][s], RW_T[s]
                    pool.wait_ge(sem("rw_t"), j * 2 + (s + 1))
                    settled(pool)
                    pool.tensor_tensor(t["in"][:, 1, :], t["in"][:, 1, :], t["t"], ALU.mult).then_inc(sem("rw_k1"), 1)
                for s in range(2):
                    b, t = RW_S[par][s], RW_T[s]
                    pool.wait_ge(sem("rw_exp"), j * 2 + (s + 1))
                    settled(pool)
                    pool.tensor_tensor(b["rt"], t["in"][:, 0, :], t["ex"][:, 0, :], ALU.mult).then_inc(sem("rw_rt"), 1)
                    pool.wait_ge(sem("rw_k1"), j * 2 + (s + 1))
                    settled(pool)
                    pool.tensor_tensor(b["kt"], t["in"][:, 1, :], t["ex"][:, 1, :], ALU.mult).then_inc(sem("rw_kt"), 1)

            def reset(i):
                for s in range(2):
                    pool.wait_ge(sem("rw_y"), i * 2 + (s + 1))
                    settled(pool)
                    pool.tensor_tensor(touched[:, s:s + 1], ones[:, 0:1], ones[:, 0:1], ALU.mult)
                    pool.tensor_copy(RW_C[s]["T"], bc4(ident[:, :])).then_inc(sem("rw_start"), 1)
                    pool.tensor_copy(RW_C[s]["U"], bc4(ident[:, :])).then_inc(sem("rw_start"), 1)

            def turn(i, par, j):
                reset(i)
                if j is not None:
                    ahead(j, 1 - par)

            turns(pool, ahead, turn)

        def rw_scalar(act):
            def exps(j, par):
                for s in range(2):
                    t = RW_T[s]
                    act.wait_ge(sem(f"rw_in{s}"), j * 48 + 48)
                    for x in range(2):
                        e = act.activation(t["in"][:, 2 + x, :], t["in"][:, 2 + x, :], ACT.Exp, scale=-1.0, bias=ncol(j * 2 + (s + 16 * x)))
                    e.then_inc(sem("rw_e"), 1)

            def rate(j, par):
                for s in range(2):
                    t = RW_T[s]
                    act.wait_ge(sem("rw_sig"), j * 2 + (s + 1))
                    act.activation(t["t"], t["in"][:, 3, :], ACT.Identity, scale=col("k_a", j * 2 + s),
                                   bias=omka(j * 2 + s)).then_inc(sem("rw_t"), 1)
                    act.activation(t["sq"], t["kk"], ACT.Square).then_inc(sem("rw_sq"), 1)

            def decays(j, par):
                for s in range(2):
                    t, b = RW_T[s], RW_S[par][s]
                    act.wait_ge(sem("rw_cm"), j * 2 + (s + 1))
                    act.activation(t["ex"][:, 0, :], t["cm"], ACT.Exp)
                    act.activation(t["ex"][:, 1, :], t["cm"], ACT.Exp, scale=-1.0)
                    act.activation(t["ex"][:, 2, :], t["ld"], ACT.Exp)
                    act.activation(b["s1"][:, 64:65], t["c"][:, 191:192], ACT.Exp)
                    act.activation(b["s1"][:, 65:66], t["cm"][:, P - 1:P], ACT.Exp).then_inc(sem("rw_exp"), 1)

            def lengths(j, par):
                for s in range(2):
                    act.wait_ge(sem("rw_ss"), j * 2 + (s + 1))
                    act.activation(RW_T[s]["sq"], ps[s][:, 0:S], ACT.Sqrt).then_inc(sem("rw_nrm"), 1)

            def start(j, par):
                exps(j, par)
                rate(j, par)
                decays(j, par)
                lengths(j, par)

            def turn(i, par, j):
                v = lambda s: i * 2 + (s + 1)
                if j is not None:
                    exps(j, 1 - par)
                for s in range(2):
                    act.wait_ge(sem("rw_m2"), v(s))
                    act.activation(RW_C[s]["tok"], bank4(3 * s + 2), ACT.Copy).then_inc(sem("rw_tok"), 1)
                for lv in range(6):
                    for s in range(2):
                        act.wait_ge(sem("rw_p"), i * 12 + (2 * lv + s + 1))
                        act.activation(RW_C[s]["PP"], bank4(3 * s + 1), ACT.Copy).then_inc(sem("rw_pc"), 1)
                    if lv < 5:
                        for s in range(2):
                            act.wait_ge(sem("rw_tt"), i * 10 + (2 * lv + s + 1))
                            act.activation(RW_C[s]["T"], bank4(3 * s + 2), ACT.Copy).then_inc(sem("rw_tc"), 1)
                    if j is not None and 0 < lv < 4:
                        (rate, decays, lengths)[lv - 1](j, 1 - par)
                for c in range(2):
                    for s in range(2):
                        act.wait_ge(sem("rw_x"), i * 4 + (2 * c + s + 1))
                        act.activation(RW_C[s]["xsa"][:, 0:P], q[3 * s + 1 - c][:, 0:P], ACT.Copy).then_inc(sem("rw_xc"), 1)
                    for s in range(2):
                        act.wait_ge(sem("rw_sa"), i * 4 + (2 * c + s + 1))
                        act.activation(RW_C[s]["xsa"][:, P:S], q[3 * s + 1 - c][:, P:S], ACT.Copy).then_inc(sem("rw_sac"), 1)
                for s in range(2):
                    act.wait_ge(sem("rw_y"), i * 2 + (s + 3))
                    act.activation(RW_C[s]["y"], q[3 * s + 2][:, 0:S], ACT.Copy).then_inc(sem("rw_yc"), 1)
                for s in range(2):
                    act.wait_ge(sem("rw_yd"), v(s))
                    act.activation(RW_C[s]["ysq"], RW_C[s]["yc"], ACT.Square).then_inc(sem("rw_ysq"), 1)
                for s in range(2):
                    act.wait_ge(sem("rw_var"), v(s))
                    act.activation(RW_C[s]["ysq"], q[3 * s + 1][:, S:2 * S], ACT.Sqrt, scale=1.0 / 64, bias=eps_ln[:, 0:1])\
                       .then_inc(sem("rw_sd"), 1)
                for s in range(2):
                    act.wait_ge(sem("rw_val"), v(s))
                    act.activation(tile(AH, i * 2 + s), RW_C[s]["yc"], ACT.Copy).then_inc(sem("rw_hi"), 1)

            turns(act, start, turn)

        def rw_tensor(pe):
            def squares(j, par):
                for s in range(2):
                    pe.wait_ge(sem("rw_sq"), j * 2 + (s + 1))
                    pe.matmul(ps[s][:, 0:S], bones[:], RW_T[s]["sq"], start=True, stop=True).then_inc(sem("rw_ss"), 1)

            def bonus(j, par):
                for s in range(2):
                    pe.wait_ge(sem("rw_rk"), j * 2 + (s + 1))
                    pe.matmul(ps[s][:, S:2 * S], bones[:], RW_T[s]["t"], start=True, stop=True).then_inc(sem("rw_bs"), 1)

            def start(j, par):
                squares(j, par)
                bonus(j, par)

            def turn(i, par, j):
                v = lambda s: i * 2 + (s + 1)
                halves = LoopChain(pe, "rw_rows", i, 6)

                def pairs(s, *products):
                    b = RW_S[par][s]
                    for h in range(2):
                        for bank, l, r in products:
                            for c in range(2):
                                mm = pe.matmul(q[bank][:, P * (2 * h + c):P * (2 * h + c) + P], b[l][rng(h), P * c:P * c + P],
                                               b[r][rng(h), P * c:P * c + P], start=True, stop=True)
                        if h == 0:
                            halves.need(halves.do(mm))
                    return mm

                for s in range(2):
                    pe.wait_ge(sem("rw_bt"), v(s))
                    pe.wait_ge(sem("rw_kt"), v(s))
                    pe.wait_ge(sem("rw_rt"), v(s))
                    pe.wait_ge(sem("rw_sd"), i * 2 + (s + 1))
                    pairs(s, (3 * s, "at", "bt"), (3 * s + 1, "bt", "at"), (3 * s + 2, "kt", "at")).then_inc(sem("rw_m1"), 1)
                for s in range(2):
                    b = RW_S[par][s]
                    pe.wait_ge(sem("rw_m1e"), v(s))
                    pairs(s, (3 * s, "bt", "rt"), (3 * s + 1, "kt", "rt"))
                    for x, src in enumerate((b["bt"][:, 0:P], b["kt"][:, 0:P], b["vg"][:, 0, 0:P], b["vg"][:, 0, P:S])):
                        mm = pe.transpose(q[3 * s + 2][:, P * x:P * x + P], src, ident[:])
                    mm.then_inc(sem("rw_m2"), 1)
                pe.wait_ge(sem("rw_m2e"), v(1))
                pe.wait_ge(sem("rw_tok"), v(1))
                for lv in range(6):
                    for s in range(2):
                        b = RW_C[s]
                        if lv:
                            pe.wait_ge(sem("rw_tc"), i * 10 + (2 * lv - 2 + s + 1))
                        for x in range(4):
                            mm = pe.matmul(q[3 * s + 1][:, P * x:P * x + P], b["M"][:, x, :], b["U"][:, x, :], start=True, stop=True)
                        mm.then_inc(sem("rw_p"), 1)
                    for s in range(2):
                        b = RW_C[s]
                        pe.wait_ge(sem("rw_pc"), i * 12 + (2 * lv + s + 1))
                        for x in range(4):
                            mm = pe.matmul(q[3 * s][:, P * x:P * x + P], b["T"][:, x, :], b["PP"][:, x, :], start=True, stop=True)
                        mm.then_inc(sem("rw_g"), 1)
                    if lv < 5:
                        for s in range(2):
                            b = RW_C[s]
                            pe.wait_ge(sem("rw_u"), i * 12 + (2 * lv + s + 1))
                            for x in range(4):
                                mm = pe.transpose(q[3 * s + 2][:, P * x:P * x + P], b["U"][:, x, :], ident[:])
                            mm.then_inc(sem("rw_tt"), 1)
                    if lv == 2 and j is not None:
                        squares(j, 1 - par)
                for c in range(2):
                    for s in range(2):
                        b, t = RW_C[s], RW_S[par][s]
                        bank = 3 * s + 1 - c
                        pe.wait_ge(sem("rw_u"), i * 12 + (10 + s + 1))
                        if c:
                            pe.wait_ge(sem("rw_s1c"), v(s))
                        for h in range(2):
                            o = q[bank][:, 64 * h:64 * h + 64]
                            mm = pe.matmul(o, b["AK"][:, 2 * h + c, :], b["tok"][:, 2 + c, rng(h)], start=True, stop=c == 0)
                            if c:
                                mm = pe.matmul(o, t["at"][rng(h), P:S], t["s1"][rng(h), 0:64], start=False, stop=True)
                            if c and h == 0:
                                halves.need(halves.do(mm))
                        mm.then_inc(sem("rw_x"), 1)
                    for s in range(2):
                        b = RW_C[s]
                        bank = 3 * s + 1 - c
                        pe.wait_ge(sem("rw_xc"), i * 4 + (2 * c + s + 1))
                        for h in range(2):
                            mm = pe.matmul(q[bank][:, P + 64 * h:P + 64 * h + 64], b["U"][:, 2 * h + c, :], b["xsa"][:, rng(h)],
                                           start=True, stop=True)
                        mm.then_inc(sem("rw_sa"), 1)
                    for s in range(2):
                        b, t = RW_C[s], RW_S[par][s]
                        pe.wait_ge(sem("rw_sac"), i * 4 + (2 * c + s + 1))
                        for h in range(2):
                            sa = b["xsa"][:, P + 64 * h:P + 64 * h + 64]
                            vt = b["tok"][:, 2 + c, rng(h)]
                            if c == 0:
                                o = q[3 * s + 1][rng(h), S:S + 64]
                                pe.matmul(o, b["tok"][:, 0, rng(h)], sa, start=True, stop=False)
                                mm = pe.matmul(o, b["tok"][:, 1, rng(h)], vt, start=False, stop=True)
                        if c == 0:
                            mm.then_inc(sem("rw_s1"), 1)
                        for h in range(2):
                            sa = b["xsa"][:, P + 64 * h:P + 64 * h + 64]
                            vt = b["tok"][:, 2 + c, rng(h)]
                            o = q[3 * s + 2][rng(h), P * c:P * c + P]
                            pe.matmul(o, sa, b["RB"][:, 2 * h + c, :], start=True, stop=False)
                            mm = pe.matmul(o, vt, b["RK"][:, 2 * h + c, :], start=False, stop=c == 0)
                            if c:
                                mm = pe.matmul(o, t["s1"][rng(h), 0:64], t["rt"][rng(h), P:S], start=False, stop=True)
                        if c:
                            mm.then_inc(sem("rw_y"), 1)
                if j is not None:
                    bonus(j, 1 - par)
                for s in range(2):
                    pe.wait_ge(sem("rw_yc"), v(s))
                    pe.matmul(q[3 * s + 1][:, 0:S], bones[:], RW_C[s]["y"], start=True, stop=True).then_inc(sem("rw_mu"), 1)
                for s in range(2):
                    pe.wait_ge(sem("rw_ysq"), v(s))
                    pe.matmul(q[3 * s + 1][:, S:2 * S], bones[:], RW_C[s]["ysq"], start=True, stop=True).then_inc(sem("rw_var"), 1)
                halves.end()

            turns(pe, start, turn)

        def touch(dve, k):
            dve.tensor_copy(touched[:, 2 + k:3 + k], eps[:, 0:1])

        def pred(dve, out_, mask, data):
            return dve.copy_predicated(out_, bc4(mask), data)

        def rw_vector(dve):
            for s in range(2):
                for key in ("M", "AK", "RB", "RK"):
                    o = dve.memset(RW_C[s][key], 0.0)
            o.then_inc(*once("rw_zero"))
            dve.wait_ge(*after("rw_zero"))

            def two(ch, f, needs=None):
                done = []
                for s in range(2):
                    if needs:
                        ch.need(needs[s])
                    done.append(ch.do(f(s, RW_T[s])))
                return done

            class Ahead:

                def __init__(self, j, par):
                    self.j, self.par, self.ch = j, par, LoopChain(dve, "rw_ahead", j, 20)
                    self.v = lambda s: j * 2 + (s + 1)

                def part0(self):
                    for s in range(2):
                        t = RW_T[s]
                        dve.wait_ge(sem(f"rw_in{s}"), self.j * 48 + 48)
                        dve.tensor_scalar(t["kk"], t["in"][:, 1, :], col("k_k", self.j * 2 + s), None, ALU.mult).then_inc(sem("rw_kk0"), 1)
                    for s in range(2):
                        dve.wait_ge(sem("rw_e"), self.v(s))
                        self.ch.do(dve.tensor_scalar(RW_T[s]["in"][:, 2:4, :], RW_T[s]["in"][:, 2:4, :], 1.0, None, ALU.add))
                    for s in range(2):
                        self.ch.need(s + 1)
                        dve.reciprocal(RW_T[s]["in"][:, 2:4, :], RW_T[s]["in"][:, 2:4, :]).then_inc(sem("rw_sig"), 1)

                def part1(self):
                    for s in range(2):
                        dve.wait_ge(sem("rw_sig"), self.v(s))
                        self.ch.do(dve.tensor_scalar(RW_T[s]["ld"], RW_T[s]["in"][:, 2, :], -EXP_HALF, None, ALU.mult))

                def part2(self):
                    def scan(s, t):
                        for c in range(2):
                            o = dve.tensor_tensor_scan(t["c"][:, P * c:P * c + P], ones[:, :], t["ld"][:, P * c:P * c + P], 0.0, ALU.mult, ALU.add)
                        return o
                    k = two(self.ch, scan, [3, 4])
                    self.k = two(self.ch, lambda s, t: dve.tensor_tensor(chunks(t["cm"]), chunks(t["c"]),
                                 chunks(t["c"])[:, :, 63:64].broadcast_to([P, 2, P]), ALU.subtract), k)

                def part3(self):
                    for s in range(2):
                        self.ch.need(self.k[s])
                        dve.tensor_tensor(RW_T[s]["ld"], RW_T[s]["cm"], RW_T[s]["ld"], ALU.subtract).then_inc(sem("rw_cm"), 1)

                def part4(self):
                    for s in range(2):
                        dve.wait_ge(sem("rw_nrm"), self.v(s))
                        self.ch.do(dve.tensor_scalar(RW_T[s]["sq"], RW_T[s]["sq"], 1e-12, None, ALU.max))
                    k = two(self.ch, lambda s, t: dve.reciprocal(t["sq"], t["sq"]), [self.ch.k - 1, self.ch.k])
                    self.k = two(self.ch, lambda s, t: dve.tensor_tensor(t["kk"], t["kk"], t["sq"], ALU.mult), k)

                def part5(self):
                    st = RW_S[self.par]
                    k = two(self.ch, lambda s, t: dve.tensor_tensor(st[s]["bt"], t["kk"], t["in"][:, 3, :], ALU.mult), self.k)
                    for s in range(2):
                        dve.wait_ge(sem("rw_exp"), self.v(s))
                        self.ch.do(dve.scalar_tensor_tensor(out=st[s]["at"], in0=RW_T[s]["kk"], scalar=-1.0, in1=RW_T[s]["ex"][:, 2, :],
                                                            op0=ALU.mult, op1=ALU.mult))
                    self.k = k

                def part6(self):
                    st = RW_S[self.par]
                    for s in range(2):
                        self.ch.need(self.k[s])
                        dve.tensor_tensor(st[s]["bt"], st[s]["bt"], RW_T[s]["ex"][:, 1, :], ALU.mult).then_inc(sem("rw_bt"), 1)
                    for s in range(2):
                        t = RW_T[s]
                        dve.wait_ge(sem("rw_k1"), self.v(s))
                        dve.scalar_tensor_tensor(out=t["t"], in0=t["in"][:, 0, :], scalar=col("r_k", self.j * 2 + s), in1=t["in"][:, 1, :],
                                                 op0=ALU.mult, op1=ALU.mult).then_inc(sem("rw_rk"), 1)

                def part7(self):
                    st = RW_S[self.par]
                    for s in range(2):
                        dve.wait_ge(sem("rw_bs"), self.v(s))
                        dve.wait_ge(sem("rw_kt"), self.v(s))
                        self.ch.do(dve.tensor_copy(st[s]["bon"], ps[s][:, S:2 * S]))
                    for s in range(2):
                        self.ch.need(self.ch.k - 1 + s)
                        dve.tensor_tensor(st[s]["bon"], st[s]["bon"], st[s]["vg"][:, 0, :], ALU.mult).then_inc(sem("rw_bon"), 1)
                    assert self.ch.k == self.ch.per, self.ch.k

            def start(j, par):
                a_ = Ahead(j, par)
                for part in (a_.part0, a_.part1, a_.part2, a_.part3, a_.part4, a_.part5, a_.part6, a_.part7):
                    part()

            def turn(i, par, j):
                v = lambda s: i * 2 + (s + 1)
                ch = LoopChain(dve, "rw_dve", i, 8)
                nxt = Ahead(j, 1 - par) if j is not None else None
                for s in range(2):
                    b = RW_C[s]
                    dve.wait_ge(sem("rw_start"), i * 4 + (2 * s + 2))
                    dve.wait_ge(sem("rw_m1"), v(s))
                    touch(dve, s)
                    pred(dve, b["M"], m_low[:, :], bank4(3 * s))
                    pred(dve, b["T"], lowmask[:, 0, :], bank4(3 * s))
                    pred(dve, b["U"], upmask[:, 0, :], bank4(3 * s + 1))
                    pred(dve, b["AK"], m_up[:, :], bank4(3 * s + 2)).then_inc(sem("rw_m1e"), 1)
                for s in range(2):
                    b = RW_C[s]
                    dve.wait_ge(sem("rw_m2"), v(s))
                    touch(dve, 2 + s)
                    pred(dve, b["RB"], m_upi[:, :], bank4(3 * s))
                    pred(dve, b["RK"], m_upi[:, :], bank4(3 * s + 1)).then_inc(sem("rw_m2e"), 1)
                if nxt:
                    nxt.part0()
                for lv in range(6):
                    for s in range(2):
                        dve.wait_ge(sem("rw_g"), i * 12 + (2 * lv + s + 1))
                        touch(dve, 4 + 2 * lv + s)
                        pred(dve, RW_C[s]["U"], upmask[:, lv + 1, :], bank4(3 * s)).then_inc(sem("rw_u"), 1)
                    if nxt:
                        if lv == 0:
                            nxt.part1()
                            nxt.part2()
                        elif lv == 1:
                            nxt.part3()
                        elif lv == 4:
                            nxt.part4()
                        elif lv == 5:
                            nxt.part5()
                for s in range(2):
                    t = RW_S[par][s]
                    dve.wait_ge(sem("rw_s1"), v(s))
                    dve.tensor_scalar(t["s1"][:, 0:64], q[3 * s + 1][:, S:S + 64], t["s1"][:, 65:66], t["s1"][:, 64:65],
                                      ALU.mult, ALU.mult).then_inc(sem("rw_s1c"), 1)
                if nxt:
                    nxt.part6()
                    nxt.part7()
                for s in range(2):
                    b = RW_C[s]
                    dve.wait_ge(sem("rw_mu"), v(s))
                    dve.scalar_tensor_tensor(out=b["yc"], in0=q[3 * s + 1][:, 0:S], scalar=-1.0 / 64, in1=b["y"], op0=ALU.mult, op1=ALU.add)\
                       .then_inc(sem("rw_yd"), 1)
                k = []
                for s in range(2):
                    dve.wait_ge(sem("rw_sd"), i * 2 + (s + 3))
                    k.append(ch.do(dve.reciprocal(RW_C[s]["ysq"], RW_C[s]["ysq"])))
                for f in (lambda s, b: dve.tensor_tensor(b["yc"], b["yc"], b["ysq"], ALU.mult),
                          lambda s, b: dve.tensor_scalar(b["yc"], b["yc"], col("lnx_w", i * 2 + s), col("lnx_b", i * 2 + s), ALU.mult, ALU.add),
                          lambda s, b: dve.tensor_tensor(b["yc"], b["yc"], RW_S[par][s]["bon"], ALU.add)):
                    nk = []
                    for s in range(2):
                        ch.need(k[s])
                        nk.append(ch.do(f(s, RW_C[s])))
                    k = nk
                for s in range(2):
                    ch.need(k[s])
                    dve.tensor_tensor(RW_C[s]["yc"], RW_C[s]["yc"], RW_S[par][s]["vg"][:, 1, :], ALU.mult).then_inc(sem("rw_val"), 1)
                for s in range(2):
                    dve.wait_ge(sem("rw_hi"), v(s))
                    dve.tensor_tensor(tile(AL, i * 2 + s), RW_C[s]["yc"], tile(AH, i * 2 + s).bitcast(F32), ALU.subtract)\
                       .then_inc(sem("rw_out"), 1)
                ch.end()

            turns(dve, start, turn)

        def relu_scalar(act, idx):
            def evac(t, n, mh, bank):
                r, sqr = G[:, 16 + bank, :], G[:, 18 + bank, :]
                act.wait_ge(sem("w_used"), n * 2 + 2)
                if not (isinstance(t, int) and t < 2 and idx == 0):
                    act.wait_ge(sem("hid_done"), t + (idx - 1))
                act.activation(r, ps[bank][:, 0:S], ACT.Relu).then_inc(sem(f"proj_out{bank}"), 1)
                act.wait_ge(sem("hid_sq"), t + (idx + 1))
                act.activation(tile(BH, t), sqr, ACT.Copy).then_inc(sem("hid_hi"), 1)
            return evac

        def relu_vector(dve, idx):
            def evac(t, n, mh, bank):
                r, sqr = G[:, 16 + bank, :], G[:, 18 + bank, :]
                dve.wait_ge(sem(f"proj_out{bank}"), mh + 1)
                dve.tensor_tensor(sqr, r, r, ALU.mult).then_inc(sem("hid_sq"), 1)
                dve.wait_ge(sem("hid_hi"), t + (idx + 1))
                dve.tensor_tensor(tile(BL, t), sqr, tile(BH, t).bitcast(F32), ALU.subtract).then_inc(sem("hid_done"), 1)
            return evac

        block = ctx.enter_context(nc.Block())
        done2 = stop >= 2

        xtok = G[:, 0:16, :].rearrange("p (b k) n -> p b (k n)", b=2)
        mtok = G[:, 16:32, :].rearrange("p (b k) n -> p b (k n)", b=2)
        otok = xtok
        m32 = G[:, 50:60, :].rearrange("p a (b n) -> p (a b) n", n=P)
        spill_ap = spill.ap()

        def mlp(layer):
            return [(f"up{layer}_{x}", f"dn{layer}_{x}", 64 * layer + 16 * x) for x in range(4)]

        @block.sync
        def _(sp):
            sp.dma_start(mtok, a["mem"][0].rearrange("(b p) d -> p b d", p=P)).then_inc(sem("mem_in"), 16)
            sp.dma_start(xtok, a["x"][0].rearrange("(b p) d -> p b d", p=P)).then_inc(sem("x_in"), 16)
            for name, _c, special in phases:
                def body(t, n, nh, pair, mh, bank):
                    for j in range(2):
                        slot = 2 * pair + j
                        if not (isinstance(n, int) and n < 2):
                            sp.wait_ge(sem("w_lo"), n * 2 + (j - 3))
                        src, kind = SRC[name](t, j)
                        flat = raw[slot][:, :, :].rearrange("p k n -> p (k n)")
                        if kind == "xo":
                            dst = flat.rearrange("p (k n) -> p k n", k=4)
                        elif kind == "up96":
                            dst = flat[0:96, 0:512]
                        elif kind == "up256":
                            dst = flat.rearrange("p (k n) -> p k n", k=2)
                        else:
                            dst = raw[slot][:, :, 0:kind]
                        sp.dma_start(dst, src).then_inc(sem(f"w_loaded{slot}"), 16)
                if special:
                    for t in range(COUNT[name]):
                        n_ = N0[name] + t
                        body(t, n_, n_ // 2, n_ % 2, 0, 0)
                else:
                    over(sp, name, body, peel=2 if N0[name] == 0 else 0)
            for b in range(2):
                sp.wait_ge(sem("fin_d"), 4)
                sp.wait_ge(sem("fin_a"), 4)
                sp.dma_start(out[0, P * b:P * b + P, :], otok[:, b, :]).then_inc(sem("stored"), 16)
            sp.wait_ge(sem("stored"), 32)

        @block.gpsimd
        def _(pool):
            ch = Chain(pool, "pool_chain")
            pool.memset(prow, 0.0).then_inc(*once("prow_zero"))
            pool.memset(ident[:], 0.0)
            pool.memset(ones[:], 1.0)
            pool.memset(bones[:], 1.0)
            pool.memset(kge[:], 1.0)
            pool.memset(causal[:], 0.0)
            pool.memset(limit[:], 3e38)
            pool.memset(m32[:, 0:14, :], 0.0)
            ch.after(pool.memset(m32[:, 14:17, :], 1.0))
            pool.affine_select(out=ident[:], in_=ident[:], compare_op=ALU.not_equal, fill=1.0, base=0,
                               pattern=[[-1, P]], channel_multiplier=1).then_inc(*once("ident"))
            keep = lambda t, pattern, base, fill=0.0, op=ALU.is_ge, cm=1: pool.affine_select(
                out=t, in_=t, compare_op=op, fill=fill, base=base, pattern=pattern, channel_multiplier=cm)
            bo = bones[:, :].rearrange("p (b n) -> p b n", n=64)
            ch.after(keep(bo, [[-64, 2], [0, 64]], 0))
            keep(bo, [[64, 2], [0, 64]], 63, cm=-1)
            keep(kge[:], [[-1, P]], 0)
            keep(causal[:, 1, :], [[-1, P]], 0, NEG)
            for x, f in enumerate((0.0, NEG)):
                keep(limit[:, x, :], [[1, P]], 0, f, ALU.is_gt, -1)
            keep(m32[:, 14, :], [[-1, P]], 0, op=ALU.is_gt)
            keep(m32[:, 15, :], [[1, P]], 0, op=ALU.is_gt, cm=-1)
            keep(m32[:, 16, :], [[1, P]], 0, cm=-1)
            pool.memset(eps[:], EPS).then_inc(sem("sb_out"), 2)
            pool.memset(eps_ln[:], LNX_EPS).then_inc(sem("rw_out"), 4)
            for x, name in enumerate(("rw_bon", "rw_sd", "rw_y")):
                pool.memset(touched[:, x:x + 1], 0.0).then_inc(sem(name), 2)
            pool.memset(stat[:], 0.0).then_inc(sem("att_out"), 2)
            lows, ups = [], []
            for l in range(1, 8):
                n = 2 ** l
                view = lambda x: m32[:, x, :].rearrange("p (b n) -> p b n", n=n)
                lows.append((view(l - 1)[:, :, 0:n // 2], n))
                ups.append((view(6 + l)[:, :, n // 2:n], n))
            for t, n in lows + ups:
                o = pool.memset(t, 1.0)
            ch.after(o)
            for (t, n), (u, _n) in zip(lows, ups):
                keep(t, [[-n, P // n], [0, n // 2]], -n // 2)
                o = keep(u, [[-n, P // n], [0, n // 2]], 0)
            ch.after(o)
            for (t, n), (u, _n) in zip(lows, ups):
                keep(t, [[n, P // n], [0, n // 2]], n - 1, cm=-1)
                o = keep(u, [[n, P // n], [0, n // 2]], n // 2 - 1, cm=-1)
            o.then_inc(sem("masks32"), 1)
            sb_pool(pool)
            gla_pool(pool)
            sgu_pool(pool)
            if stop >= 2:
                phase_done(pool, "xq")
                att_pool(pool, "xa")
            if stop >= 3:
                for name in SPILL:
                    spill_pool(pool, name)
                up_pool(pool)
                rw_pool(pool)
            if stop >= 5:
                phase_done(pool, "fq")
                pool.wait_ge(*after("f_ready"))
                att_pool(pool, "fa")

        @block.scalar
        def _(act):
            act.wait_ge(*after("prow_zero"))
            for src, r, cnt in rows:
                v = a[src]
                while len(v.shape) > 1:
                    v = v.rearrange("a b c -> (a b) c") if len(v.shape) == 3 else v.rearrange("a b -> (a b)")
                act.dma_start(prow[r % P:r % P + cnt, r // P, :], v.rearrange("(r c) -> r c", c=P)).then_inc(sem("prow_in"), 16)
            act.dma_start(gup[:], a["w_gla_gate_up"][0]).then_inc(sem("small_in"), 16)
            act.dma_start(bf[:], a["b_f_2"].rearrange("(n o) -> n o", o=1)).then_inc(sem("small_in"), 16)
            ch = Chain(act, "act_chain")
            for u in range(1, 16, 2):
                act.wait_ge(sem("tr"), u + 1)
                dst = G[:, 32 + 2 * u:34 + 2 * u, :] if u < 8 else X[:, 2 * u - 16:2 * u - 14, :]
                act.activation(dst, q[u % 4][:, :].rearrange("p (a n) -> p a n", a=2), ACT.Copy).then_inc(sem("tr_a"), 1)
            act.wait_ge(*after("prm_t"))
            act.activation(prm[:], q[4][:, :], ACT.Copy).then_inc(*once("prm"))
            for h in range(4):
                act.wait_ge(sem(f"w_loaded{h}"), 16)
                act.activation(wh[h][:], raw[h][:], ACT.Copy).then_inc(sem("w_hi"), 1)
            act.wait_ge(sem("masks32"), 1)
            act.wait_ge(sem("tr_a"), 8)
            act.wait_ge(sem("tr_d"), 8)
            norm_scalar(act, "mem")
            norm_scalar(act, "mix")
            for name in ("xkv", "in_a", "in_r", "in_b"):
                stream(act, name, peel=2 if name == "xkv" else 0)
            sb_scalar(act)
            gla_scalar(act, ch)
            sgu_scalar(act, ch)
            mix_scalar(act)
            stream(act, "out")
            phase_done(act, "out")
            if stop >= 2:
                norm_scalar(act, "xattn")
                stream(act, "xq")
                att_scalar(act, "xa")
                for t in range(4):
                    split_next(act, N0["xo"] + t, (N0["xo"] + t) // 2, (N0["xo"] + t) % 2, N0["xo"] + t >= TOTAL - 2)
                act.wait_ge(sem("xo_out"), 8)
            if stop >= 3:
                norm_scalar(act, "final1")
                act.wait_ge(sem("norm_done"), 4 * NIDX["final1"] + 4)
                norm_scalar(act, "rwkv")
                act.wait_ge(sem("norm_done"), 4 * NIDX["rwkv"] + 4)
                xs_bulk(act, "r", xs_scalar_part, xs_scalar_high)
                for name, nxt in (("rw_r", "k"), ("rw_k", "v"), ("rw_v", "w")):
                    stream(act, name, spill_scalar(act, name, nxt), peel=2 if name == "rw_r" else 0)
                stream(act, "rw_w1", lora_scalar(act, "rw_w1"))
                xs_bulk(act, "a", xs_scalar_part, xs_scalar_high)
                stream(act, "rw_a1", lora_scalar(act, "rw_a1"))
                xs_bulk(act, "g", xs_scalar_part, xs_scalar_high)
                stream(act, "rw_g1", lora_scalar(act, "rw_g1"))
                for t in range(6):
                    n = N0["rw_up"] + t
                    split_next(act, n, n // 2, n % 2, False)
                rw_scalar(act)
                stream(act, "rw_o")
                phase_done(act, "rw_o")
            for layer, lim in ((0, 4), (1, 6)):
                if layer == 1 and stop >= 5:
                    norm_scalar(act, "kv")
                    norm_scalar(act, "fox")
                    for name in ("fk", "fv", "ff"):
                        stream(act, name)
                    act.wait_ge(*after("f_in"))
                    ch.after(act.activation(fscr[0:16, 6, :], fscr[0:16, 5, :], ACT.Abs))
                    ch.after(act.activation(fscr[0:16, 6, :], fscr[0:16, 6, :], ACT.Exp, scale=-1.0))
                    act.activation(fscr[0:16, 6, :], fscr[0:16, 6, :], ACT.Ln, bias=1.0).then_inc(*once("f_ln"))
                    stream(act, "fq")
                    att_scalar(act, "fa")
                    stream(act, "fo")
                    phase_done(act, "fo")
                if stop >= lim:
                    norm_scalar(act, f"ffn{layer}")
                    for up, dn, idx in mlp(layer):
                        stream(act, up, relu_scalar(act, idx), peel=2 if idx == 0 else 0)
                        stream(act, dn)
                    phase_done(act, f"dn{layer}_3")
            norm_scalar(act, "final2")
            for u in range(1, 8, 2):
                act.wait_ge(sem("fin_t"), u + 1)
                act.activation(otok[:, u // 4, 512 * (u % 4):512 * (u % 4) + 512], q[u % 4][:, :], ACT.Copy).then_inc(sem("fin_a"), 1)

        @block.vector
        def _(dve):
            ch = Chain(dve, "dve_chain")
            for u in range(0, 16, 2):
                dve.wait_ge(sem("tr"), u + 1)
                dst = G[:, 32 + 2 * u:34 + 2 * u, :] if u < 8 else X[:, 2 * u - 16:2 * u - 14, :]
                dve.tensor_copy(dst, q[u % 4][:, :].rearrange("p (a n) -> p a n", a=2)).then_inc(sem("tr_d"), 1)
            dve.wait_ge(sem("masks32"), 1)
            dve.wait_ge(*after("ident"))
            dve.tensor_copy(lowmask[:], m32[:, 0:7, :])
            dve.tensor_copy(upmask[:], m32[:, 7:14, :])
            dve.tensor_copy(m_low[:], m32[:, 14, :])
            dve.tensor_copy(m_up[:], m32[:, 15, :])
            dve.tensor_copy(m_upi[:], m32[:, 16, :])
            dve.tensor_copy(m_id[:], ident[:]).then_inc(sem("masks"), 1)
            dve.wait_ge(sem("masks"), 1)
            dve.wait_ge(*after("prm"))
            pc = lambda key, n: prm[:, COL[key]:COL[key] + n]
            dve.tensor_scalar(omm[:], pc("x_mix", 96), -1.0, 1.0, ALU.mult, ALU.add)
            dve.tensor_scalar(neg[:, 0:16], pc("w0", 16), -1.0, None, ALU.mult)
            dve.tensor_scalar(neg[:, 16:32], pc("a0", 16), -1.0, None, ALU.mult)
            dve.tensor_scalar(neg[:, 32:48], pc("k_a", 16), -1.0, 1.0, ALU.mult, ALU.add).then_inc(*once("prm2"))
            for h in range(4):
                dve.wait_ge(sem("w_hi"), h + 1)
                dve.tensor_tensor(wl[h][:], raw[h][:], wh[h][:].bitcast(F32), ALU.subtract).then_inc(sem("w_lo"), 1)
            norm_vector(dve, "mem")
            norm_vector(dve, "mix")
            stream(dve, "xkv", out_copy(dve, G, 56), peel=2)
            stream(dve, "in_a", out_copy(dve, G, 0))
            stream(dve, "in_r", lambda t, n, mh, bank: (
                dve.wait_ge(sem("w_used"), n * 2 + 2),
                dve.tensor_copy(rT[:], ps[bank][0:16, 0:S]).then_inc(sem(f"proj_out{bank}"), 1)))
            stream(dve, "in_b", out_copy(dve, G, 40))
            sb_vector(dve)
            gla_vector(dve, ch)
            sgu_vector(dve, ch)
            mix_vector(dve, ch)
            stream(dve, "out", out_resid(dve))
            if stop >= 2:
                norm_vector(dve, "xattn")
                stream(dve, "xq", out_copy(dve, G, 16, SCALE))
                att_vector(dve, "xa")
                for t in range(4):
                    n = N0["xo"] + t
                    split_next(dve, n, n // 2, n % 2, n >= TOTAL - 2)
                    for j in range(2):
                        hc = 2 * t + j
                        dve.wait_ge(sem("w_used"), 2 * n + j + 1)
                        x = X[:, 2 * hc:2 * hc + 2, :]
                        dve.tensor_tensor(x, q[hc % 2][:, :].rearrange("p (a n) -> p a n", a=2), x, ALU.add).then_inc(sem("xo_out"), 1)
            if stop >= 3:
                norm_vector(dve, "final1")
                norm_vector(dve, "rwkv")
                xs_bulk(dve, "r", xs_vector_add, xs_vector_low)
                for name, nxt in (("rw_r", "k"), ("rw_k", "v"), ("rw_v", "w")):
                    stream(dve, name, spill_vector(dve, nxt))
                stream(dve, "rw_w1", lora_vector(dve, "rw_w1"))
                xs_bulk(dve, "a", xs_vector_add, xs_vector_low)
                stream(dve, "rw_a1", lora_vector(dve, "rw_a1"))
                xs_bulk(dve, "g", xs_vector_add, xs_vector_low)
                stream(dve, "rw_g1", lora_vector(dve, "rw_g1"))
                up_vector(dve)
                for b in range(2):
                    dve.wait_ge(sem(f"up_spilled{b}"), 16 * 6)
                rw_vector(dve)
                stream(dve, "rw_o", out_resid(dve))
            for layer, lim in ((0, 4), (1, 6)):
                if layer == 1 and stop >= 5:
                    norm_vector(dve, "kv")
                    norm_vector(dve, "fox")
                    stream(dve, "fk", out_copy(dve, G, 0))
                    stream(dve, "fv", out_copy(dve, G, 16))
                    stream(dve, "ff", lambda t, n, mh, bank: (
                        dve.wait_ge(sem("w_used"), n * 2 + 2),
                        dve.tensor_scalar(fscr[0:16, 5, :], ps[bank][0:16, 0:S], bf[:, 0:1], None, ALU.add).then_inc(sem(f"proj_out{bank}"), 1)))
                    phase_done(dve, "ff")
                    ch.after(dve.tensor_scalar(fscr[0:16, 7, :], fscr[0:16, 5, :], -1.0, 0.0, ALU.mult, ALU.max))
                    dve.tensor_copy(fscr[0:16, 8, :], fscr[0:16, 7, :]).then_inc(*once("f_in"))
                    dve.wait_ge(*after("f_ln"))
                    ch.after(dve.tensor_tensor(fscr[0:16, 7, :], fscr[0:16, 7, :], fscr[0:16, 6, :], ALU.add))
                    ch.after(dve.tensor_tensor_scan(cneg, ones[0:16, 0:1].broadcast_to([16, S]), fscr[0:16, 7, :], 0.0, ALU.mult, ALU.add))
                    dve.tensor_scalar(cpos, cneg, -1.0, None, ALU.mult).then_inc(*once("f_c"))
                    stream(dve, "fq", out_copy(dve, G, 32, SCALE))
                    dve.wait_ge(*after("f_t"))
                    dve.tensor_copy(fscr[:, 2, 0:32], q[0][:, 0:32]).then_inc(*once("f_ready"))
                    dve.wait_ge(*after("f_ready"))
                    att_vector(dve, "fa")
                    stream(dve, "fo", out_resid(dve))
                if stop >= lim:
                    norm_vector(dve, f"ffn{layer}")
                    for up, dn, idx in mlp(layer):
                        stream(dve, up, relu_vector(dve, idx))
                        stream(dve, dn, out_resid(dve))
            norm_vector(dve, "final2")
            for u in range(0, 8, 2):
                dve.wait_ge(sem("fin_t"), u + 1)
                dve.tensor_copy(otok[:, u // 4, 512 * (u % 4):512 * (u % 4) + 512], q[u % 4][:, :]).then_inc(sem("fin_d"), 1)

        @block.tensor
        def _(pe):
            pe.wait_ge(*after("ident"))
            for u in range(16):
                pe.wait_ge(sem("mem_in" if u < 8 else "x_in"), 16)
                if u > 3:
                    pe.wait_ge(sem("tr_a" if u % 2 else "tr_d"), (u - 4) // 2 + 1)
                tok = mtok if u < 8 else xtok
                for x in range(4):
                    k, b = 2 * (u % 8) + x // 2, x % 2
                    mm = pe.transpose(q[u % 4][:, P * x:P * x + P], tok[:, b, P * k:P * k + P], ident[:])
                mm.then_inc(sem("tr"), 1)
            pe.wait_ge(sem("prow_in"), 16 * len(rows))
            for x in range(NROW):
                mm = pe.transpose(q[4][:, P * x:P * x + P], prow[:, x, :], ident[:])
            mm.then_inc(*once("prm_t"))
            norm_tensor(pe, "mem")
            norm_tensor(pe, "mix")
            project(pe, "xkv", AH, AL, norm_ready("mem"))
            for name in ("in_a", "in_r", "in_b"):
                project(pe, name, BH, BL, norm_ready("mix"))
            pe.wait_ge(sem("small_in"), 32)
            sb_tensor(pe)
            gla_tensor(pe)
            sgu_tensor(pe)
            mix_tensor(pe)
            project(pe, "out", BH, BL, ("mix_done", lambda g: g + 1))
            if stop >= 2:
                norm_tensor(pe, "xattn")
                project(pe, "xq", AH, AL, norm_ready("xattn"))
                phase_done(pe, "xq")
                att_tensor(pe, "xa")
                pe.wait_ge(sem("att_out"), 6)
                for hc in range(8):
                    n = N0["xo"] + hc // 2
                    slot = 2 * (n % 2) + hc % 2
                    pe.wait_ge(sem("w_lo"), 2 * N0["xo"] + hc + 1)
                    if hc > 1:
                        pe.wait_ge(sem("xo_out"), hc - 1)
                    for o in range(2):
                        dst = q[hc % 2][:, S * o:S * o + S]
                        for k in range(4):
                            h_, l_ = (w[slot][:, :, :].rearrange("p k n -> p (k n)")[:, S * k + P * o:S * k + P * o + P] for w in (wh, wl))
                            pe.matmul(dst, h_, BH[:, k, :], start=k == 0, stop=False)
                            pe.matmul(dst, h_, BL[:, k, :], start=False, stop=False)
                            mm = pe.matmul(dst, l_, BH[:, k, :], start=False, stop=k == 3)
                    mm.then_inc(sem("w_used"), 1)
                pe.wait_ge(sem("xo_out"), 8)
            if stop >= 3:
                norm_tensor(pe, "final1")
                norm_tensor(pe, "rwkv")
                for name, mix in (("rw_r", "r"), ("rw_k", "k"), ("rw_v", "v"), ("rw_w1", "w"), ("rw_a1", "a"), ("rw_g1", "g")):
                    d = MIXES[mix][2]
                    project(pe, name, d[0], d[1], xs_ready(mix))
                up_tensor(pe)
                pe.wait_ge(sem("up_out"), 12)
                rw_tensor(pe)
                pe.wait_ge(sem("rw_out"), 20)
                project(pe, "rw_o", AH, AL)
            for layer, lim in ((0, 4), (1, 6)):
                if layer == 1 and stop >= 5:
                    norm_tensor(pe, "kv")
                    norm_tensor(pe, "fox")
                    for name in ("fk", "fv", "ff"):
                        project(pe, name, AH, AL, norm_ready("kv"))
                    project(pe, "fq", BH, BL, norm_ready("fox"))
                    pe.wait_ge(*after("f_c"))
                    for b in range(2):
                        mm = pe.transpose(q[0][:, 16 * b:16 * b + 16], cpos[:, P * b:P * b + P], ident[0:16, 0:16])
                    mm.then_inc(*once("f_t"))
                    pe.wait_ge(*after("f_ready"))
                    phase_done(pe, "fq")
                    att_tensor(pe, "fa")
                    pe.wait_ge(sem("att_out"), 22)
                    project(pe, "fo", AH, AL)
                if stop >= lim:
                    norm_tensor(pe, f"ffn{layer}")
                    for up, dn, idx in mlp(layer):
                        project(pe, up, AH, AL, norm_ready(f"ffn{layer}"))
                        project(pe, dn, BH, BL, ("hid_done", lambda g, idx=idx: idx + 4 * g + 4))
            norm_tensor(pe, "final2")
            norm_all(pe, "final2")
            for u in range(8):
                if u > 3:
                    pe.wait_ge(sem("fin_a" if u % 2 else "fin_d"), (u - 4) // 2 + 1)
                for x in range(4):
                    mm = pe.transpose(q[u % 4][:, P * x:P * x + P], X[:, 4 * (u % 4) + x, P * (u // 4):P * (u // 4) + P], ident[:])
                mm.then_inc(sem("fin_t"), 1)


def kernel(**inputs):
    import numpy as _np
    import concourse.bacc as _bacc
    from concourse import mybir as _mybir
    from concourse.bass_utils import run_bass_kernel_spmd as _run

    nc = _bacc.Bacc("TRN2", target_bir_lowering=False, num_devices=1)
    arrays, args = {}, {}
    for name, value in inputs.items():
        value = _np.ascontiguousarray(value)
        if value.size == 0:
            continue
        arrays[f"in_{name}_dram"] = value
        args[name] = nc.dram_tensor(f"in_{name}_dram", value.shape, _mybir.dt.from_np(value.dtype), kind="ExternalInput").ap()
    out = nc.dram_tensor("out_0_dram", (1, S, D), F32, kind="ExternalOutput").ap()
    two_block_kernel(nc, args, out, 6)
    r = _run(nc, [arrays], core_ids=[0])
    return r.results[0]["out_0_dram"]
```

```python
from contextlib import ExitStack

import concourse.bass as bass
from concourse import mybir

F32 = mybir.dt.float32
F32R = mybir.dt.float32r
U8 = mybir.dt.uint8
ACT = mybir.ActivationFunctionType
ALU = mybir.AluOpType
AXX = mybir.AxisListType.X

P = 128
D = 2048
KT = D // P
S = 256
HALF = KT // 2
EPS = 1e-6
LNX_EPS = 64e-5
NEG = -1e30
GELU = 1.5957691216057308
EXP_HALF = 0.6065306597126334

PHASES = [
    ("in_a", 40, False), ("in_r", 1, False), ("in_b", 16, False), ("xkv", 8, False),
    ("out", 16, False), ("xq", 4, False), ("xo", 4, True),
    ("rw_r", 16, False), ("rw_k", 16, False), ("rw_v", 16, False), ("rw_w1", 1, False),
    ("rw_a1", 1, False), ("rw_g1", 2, False), ("rw_up", 6, True), ("rw_o", 16, False),
    ("up0", 64, False), ("mlp0", 64, False),
    ("fk", 16, False), ("fv", 16, False), ("ff", 1, False), ("fq", 16, False), ("fo", 16, False),
    ("mlp1", 128, False),
]


def mlp_phases(layer):
    return [(f"{w}{layer}_{q}", 16, False) for q in range(4) for w in ("up", "dn")]


PHASES = [p for p in PHASES if p[0] not in ("up0", "mlp0", "mlp1")]
_at = [p[0] for p in PHASES].index("rw_o") + 1
PHASES = PHASES[:_at] + mlp_phases(0) + PHASES[_at:] + mlp_phases(1)
STOPS = {1: "out", 2: "xo", 3: "rw_o", 4: "dn0_3", 5: "fo", 6: "dn1_3"}


def two_block_kernel(nc, a, out, stop=6):
    phases = PHASES[:[p[0] for p in PHASES].index(STOPS[stop]) + 1]
    N0, M0, COUNT, n, m = {}, {}, {}, 0, 0
    for name, count, special in phases:
        N0[name], M0[name], COUNT[name] = n, m, count
        n += count
        m += 0 if special else count
    TOTAL = n

    with ExitStack() as ctx:
        TILE = S * 4
        arena = ctx.enter_context(nc.sbuf_tensor("arena", [P, 192 * 256], F32))
        base = BASE = 16512

        def at(name, tiles_at, shape, dt=F32):
            return nc.alloc_sbuf_tensor_at(name, shape, dt, offset=BASE + tiles_at * TILE)

        X = at("x_resid", 0, [P, KT, S])
        raw = [at(f"w_raw{i}", 16 + 4 * i, [P, HALF, P]) for i in range(4)]
        wh = [at(f"w_high{i}", 32 + 4 * i, [P, HALF, P], F32R) for i in range(4)]
        wl = [at(f"w_low{i}", 48 + 4 * i, [P, HALF, P], F32R) for i in range(4)]
        AH, AL = at("a_high", 64, [P, KT, S], F32R), at("a_low", 80, [P, KT, S], F32R)
        BH, BL = at("b_high", 96, [P, KT, S], F32R), at("b_low", 112, [P, KT, S], F32R)
        AF, BF = at("a_scratch", 64, [P, 32, S]), at("b_scratch", 96, [P, 32, S])
        G = at("g", 128, [P, 64, S])
        LH, LL = at("lora_high", 184, [P, 4, S], F32R), at("lora_low", 188, [P, 4, S], F32R)

        def sb(name, shape, dt=F32):
            return ctx.enter_context(nc.sbuf_tensor(name, shape, dt))

        ident, ones, bones, kge = (sb(x, [P, P]) for x in ("ident", "ones", "bones", "kge"))
        lowmask, upmask = sb("lowmask", [P, 7, P], U8), sb("upmask", [P, 7, P], U8)
        m_low, m_up, m_upi, m_id = (sb(x, [P, P], U8) for x in ("m_low", "m_up", "m_upi", "m_id"))
        causal = sb("causal", [P, 2, P])
        limit = sb("limit", [P, 2, P])
        NROW = 4
        prm = sb("prm", [P, NROW * P])
        omm = sb("one_minus_mix", [P, 6 * KT])
        neg = sb("negated", [P, 3 * KT])
        eps, eps_ln = sb("eps", [P, 1]), sb("eps_ln", [P, 1])
        rT, gup = sb("gla_r", [16, S]), sb("gate_up", [16, S])
        w_s = G[:, 8:10, :].rearrange("p a (b n) -> p (a b) n", n=P)
        b_s = G[0:1, 10:12, :].rearrange("p a (b n) -> p (a b) n", n=P)
        bf = sb("b_f_sb", [16, 1])
        rstd = sb("rstd", [P, 2, S])
        touched = sb("touched", [P, 30])
        s1_all = sb("rw_states", [P, 4, 66])
        stat = sb("stat", [P, 2, 8])
        ps = [ctx.enter_context(nc.psum_tensor(f"proj{i}", [P, 512], F32)) for i in range(2)]
        q = [ctx.enter_context(nc.psum_tensor(f"side{i}", [P, 512], F32)) for i in range(6)]
        spill = nc.dram_tensor("rwkv_spill", [6, KT, P, S], F32)

        names = {}

        def sem(name):
            if name not in names:
                names[name] = ctx.enter_context(nc.semaphore(name))
            return names[name]

        ONCE = {"tensor": ["prm_t", "gl_z", "gl_vt", "gl_o", "sg_wt", "sg_ss", "sg_vt", "sg_mixed", "f_t"],
                "vector": ["prm2", "gl_x", "gl_vtc", "gl_out", "sg_v", "sg_vtc", "sg_out", "rw_zero", "f_in", "f_c", "f_ready"],
                "scalar": ["prm", "gl_ln", "sg_sq", "sg_std", "sg_wtc", "f_ln"],
                "gpsimd": ["prow_zero", "ident", "gl_zero", "sg_wm"]}
        POSITION = {event: (f"{engine}_once", k + 1) for engine, events in ONCE.items() for k, event in enumerate(events)}

        def once(event):
            return sem(POSITION[event][0]), 1

        def after(event):
            return sem(POSITION[event][0]), POSITION[event][1]

        vec = [("norm_mix", "norm_mix", 16), ("out_norm", "out_norm", 16), ("norm_xattn", "norm_xattn", 16),
               ("norm_mem", "norm_mem", 16), ("final_norm", "final_norm", 16), ("mix_norm", "mix_norm_2", 32),
               ("w0", "rwkv_w0_2", 16),
               ("ffn_norm", "ffn_norm_2", 32), ("final2", "final_norm_2", 16), ("a0", "rwkv_a0_2", 16),
               ("k_k", "rwkv_k_k_2", 16), ("k_a", "rwkv_k_a_2", 16), ("r_k", "rwkv_r_k_2", 16), ("lnx_w", "rwkv_lnx_w_2", 16),
               ("x_mix", "rwkv_x_mix_2", 96), ("lnx_b", "rwkv_lnx_b_2", 16), ("kv_norm", "kv_norm_2", 16),
               ("sgu_norm", "sgu_norm", 4), ("b_gla", "b_gla_gate", 2)]
        COL, row = {}, 0
        rows = []
        for key, src, cnt in vec:
            assert row // P == (row + cnt - 1) // P, key
            COL[key] = row
            rows.append((src, row, cnt))
            row += cnt
        assert row <= NROW * P
        prow = G[:, 48:50, :].rearrange("p a (b c) -> p (a b) c", c=P)

        def col(key, k=0):
            return prm[:, bass.ds(COL[key] + k, 1)] if not isinstance(k, int) else prm[:, COL[key] + k:COL[key] + k + 1]

        def tile(t, k):
            return t[:, bass.ds(k, 1), :].rearrange("p a n -> p (a n)") if not isinstance(k, int) else t[:, k, :]

        def rows_of(w):
            return w.rearrange("(k p) n -> p k n", p=P)

        def cols(w, c0, width=P):
            view = rows_of(w)
            return lambda t, j: (view[:, HALF * j:HALF * j + HALF, bass.ds(t * P + c0, width)], width)

        def xo_src(t, j):
            return rows_of(a["w_xo"][0])[:, :, bass.ds(t * 512 + j * 256, 256)], "xo"

        win = a["w_in"][0]
        SRC = {"xkv": cols(a["w_xkv"][0], 0), "in_a": cols(win, 0), "in_r": cols(win, 5120, 16),
               "in_b": cols(win, 5136), "out": cols(a["w_out"][0], 0), "xq": cols(a["w_xq"][0], 0),
               "xo": xo_src, "rw_r": cols(a["rwkv_w_rkv_2"][0, 0], 0), "rw_k": cols(a["rwkv_w_rkv_2"][0, 1], 0),
               "rw_v": cols(a["rwkv_w_rkv_2"][0, 2], 0), "rw_w1": cols(a["rwkv_w1_2"][0], 0, 96),
               "rw_a1": cols(a["rwkv_a1_2"][0], 0, 96), "rw_g1": cols(a["rwkv_g1_2"][0], 0),
               "rw_o": cols(a["rwkv_w_o_2"][0], 0),
               "fk": cols(a["w_kvf_2"], 0), "fv": cols(a["w_kvf_2"], D), "ff": cols(a["w_kvf_2"], 2 * D, 16),
               "fq": cols(a["fox_w_q_2"][0], 0), "fo": cols(a["fox_w_o_2"][0], 0)}
        for layer in range(2):
            for qq in range(4):
                SRC[f"up{layer}_{qq}"] = cols(a["mlp_w_up_2"][layer], qq * D)
                SRC[f"dn{layer}_{qq}"] = cols(a["mlp_w_down_2"][layer][qq * D:(qq + 1) * D], 0)

        def up_src(t, j):
            which, part = divmod(2 * t + j, 4)
            if which < 2:
                w = a["rwkv_w2_2" if which == 0 else "rwkv_a2_2"][0]
                return w[:, part * 512:part * 512 + 512], "up96"
            return rows_of(a["rwkv_g2_2"][0])[:, :, part * 512:part * 512 + 512], "up256"

        SRC["rw_up"] = up_src

        def over(eng, name, body, peel=0, tail=0, between=None):
            cnt, n0, m0 = COUNT[name], N0[name], M0[name]

            def one(t0, i, u):
                t = t0 + 2 * i + u
                nb, mb = n0 + t0 + u, m0 + t0 + u
                body(t, nb + 2 * i, nb // 2 + i, nb % 2, mb // 2 + i, mb % 2)

            for t in range(min(peel, cnt)):
                one(t, 0, 0)
            if between:
                between()
            start, end = min(peel, cnt), cnt - tail
            pairs = max(0, end - start) // 2
            if pairs >= 2:
                with eng.Fori(0, pairs) as i:
                    one(start, i, 0)
                    one(start, i, 1)
                start += 2 * pairs
            for t in range(start, cnt):
                one(t, 0, 0)

        def single(name, t, body):
            n_, m_ = N0[name] + t, M0[name] + t
            body(t, n_, n_ // 2, n_ % 2, m_ // 2, m_ % 2)

        def phase_done(eng, name):
            m_end = M0[name] + COUNT[name]
            eng.wait_ge(sem("proj_out0"), (m_end + 1) // 2)
            eng.wait_ge(sem("proj_out1"), m_end // 2)

        def split_next(eng, n, nh, pair, last):
            if last:
                return
            for j in range(2):
                slot = 2 * pair + j
                if eng is nc.scalar:
                    eng.wait_ge(sem("w_used"), n * 2 + j + 1)
                    eng.wait_ge(sem(f"w_loaded{slot}"), nh * 16 + 32)
                    eng.activation(wh[slot][:], raw[slot][:], ACT.Copy).then_inc(sem("w_hi"), 1)
                else:
                    eng.wait_ge(sem("w_hi"), n * 2 + j + 5)
                    eng.tensor_tensor(wl[slot][:], raw[slot][:], wh[slot][:].bitcast(F32), ALU.subtract)\
                       .then_inc(sem("w_lo"), 1)

        last_phase = phases[-1][0]

        def stream(eng, name, evac=None, peel=0):
            def run(tail_only):
                def body(t, n, nh, pair, mh, bank):
                    split_next(eng, n, nh, pair, tail_only and isinstance(n, int) and n >= TOTAL - 2)
                    if evac:
                        evac(t, n, mh, bank)
                return body
            over(eng, name, run(name == last_phase), peel=peel, tail=2 if name == last_phase else 0)

        def project(pe, name, hi, lo, groups=None, between=None):
            def body(t, n, nh, pair, mh, bank):
                if not (isinstance(mh, int) and mh == 0):
                    pe.wait_ge(sem(f"proj_out{bank}"), mh)
                for j in range(2):
                    slot = 2 * pair + j
                    pe.wait_ge(sem("w_lo"), n * 2 + j + 1)
                    for k in range(HALF):
                        kk = HALF * j + k
                        if groups and kk % 4 == 0:
                            pe.wait_ge(sem(groups[0]), groups[1](kk // 4))
                        o = ps[bank][:, 0:S]
                        pe.matmul(o, wh[slot][:, k, :], hi[:, kk, :], start=kk == 0, stop=False)
                        pe.matmul(o, wh[slot][:, k, :], lo[:, kk, :], start=False, stop=False)
                        mm = pe.matmul(o, wl[slot][:, k, :], hi[:, kk, :], start=False, stop=kk == KT - 1)
                    mm.then_inc(sem("w_used"), 1)
            if name in ("fq", "xkv"):
                return body
            over(pe, name, body, peel=2 if M0[name] == 0 else 0, between=between)

        def out_copy(eng, dst, k0, scale=None):
            def evac(t, n, mh, bank):
                eng.wait_ge(sem("w_used"), n * 2 + 2)
                if scale:
                    o = eng.tensor_scalar(tile(dst, k0 + t), ps[bank][:, 0:S], scale, None, ALU.mult)
                else:
                    o = eng.tensor_copy(tile(dst, k0 + t), ps[bank][:, 0:S])
                o.then_inc(sem(f"proj_out{bank}"), 1)
            return evac

        def out_resid(eng):
            def evac(t, n, mh, bank):
                eng.wait_ge(sem("w_used"), n * 2 + 2)
                eng.tensor_tensor(tile(X, t), ps[bank][:, 0:S], tile(X, t), ALU.add).then_inc(sem(f"proj_out{bank}"), 1)
            return evac

        NORMS = {
            "mem": (0, G, 32, "norm_mem", (AH, AL), G, 16),
            "mix": (1, X, 0, "norm_mix", (BH, BL), G, 0),
            "xattn": (2, X, 0, "norm_xattn", (AH, AL), G, 0),
            "final1": (3, X, 0, "final_norm", None, G, 0),
            "rwkv": (4, X, 0, "mix_norm", G, G, 16),
            "ffn0": (5, X, 0, "ffn_norm", (AH, AL), G, 0),
            "kv": (6, X, 0, "kv_norm", (AH, AL), G, 48),
            "fox": (7, X, 0, ("mix_norm", 16), (BH, BL), G, 48),
            "ffn1": (8, X, 0, ("ffn_norm", 16), (AH, AL), G, 0),
            "final2": (9, X, 0, "final2", None, G, 0),
        }
        run_norms = ["mix", "mem", "xattn", "final1", "rwkv", "ffn0", "kv", "fox", "ffn1", "final2"]
        if stop == 1:
            run_norms = ["mix", "mem"]
        elif stop == 2:
            run_norms = run_norms[:3]
        else:
            run_norms = run_norms[:{3: 5, 4: 6, 5: 8, 6: 9}[stop]]
        run_norms = run_norms + ["final2"]
        NIDX = {x: i for i, x in enumerate(run_norms)}

        SUMMED = {"xattn": "out", "ffn0": "rw_o", "kv": "dn0_3", "ffn1": "fo", "final2": phases[-1][0]}
        SUMMED = {x: y for x, y in SUMMED.items() if x in run_norms and y not in ("xo",)}
        SAME = {"fox": "kv"}

        def before(name, cost):
            return sum(cost(x) for x in run_norms[:NIDX[name]])

        squares_of = lambda x: 0 if x in SUMMED or x in SAME else 4
        sums_of = lambda x: 0 if x in SAME else 1

        def squares_pool(pool, name):
            _, src, k0, gain, dst, scr, s0 = NORMS[name]
            base = 17 * list(SUMMED).index(name)
            acc = scr[:, s0, :]

            def body(t, n, nh, pair, mh, bank):
                sq = scr[:, s0 + 1 + bank, :]
                pool.wait_ge(sem(f"proj_out{bank}"), mh + 1)
                settled(pool)
                if isinstance(t, int) and t == 0:
                    pool.memset(acc, 0.0).then_inc(sem("sum_acc"), 1)
                pool.tensor_tensor(sq, tile(X, t), tile(X, t), ALU.mult).then_inc(sem("sum_sq"), 1)
                pool.wait_ge(sem("sum_acc"), t + (base + 1))
                pool.wait_ge(sem("sum_sq"), t + (base // 17 * 16 + 1))
                settled(pool)
                pool.tensor_tensor(acc, acc, sq, ALU.add).then_inc(sem("sum_acc"), 1)

            over(pool, SUMMED[name], body, peel=2)

        def norm_scalar(act, name):
            _, src, k0, gain, dst, scr, s0 = NORMS[name]
            i = NIDX[name]
            if i:
                act.wait_ge(sem("norm_done"), 4 * i)
            if squares_of(name):
                for g in range(4):
                    act.activation(scr[:, s0 + 4 * g:s0 + 4 * g + 4, :], src[:, k0 + 4 * g:k0 + 4 * g + 4, :], ACT.Square)\
                       .then_inc(sem("norm_sq"), 1)
            if sums_of(name):
                act.wait_ge(sem("norm_sum"), before(name, sums_of) + 1)
                act.activation(rstd[:, 0, :], q[0][:, 0:S], ACT.Sqrt, scale=1.0 / D, bias=eps[:, 0:1]).then_inc(sem("norm_std"), 1)
            if isinstance(dst, tuple):
                for g in range(4):
                    act.wait_ge(sem("norm_val"), 4 * norm_hl(name) + g + 1)
                    act.activation(dst[0][:, 4 * g:4 * g + 4, :], scr[:, s0 + 4 * g:s0 + 4 * g + 4, :], ACT.Copy)\
                       .then_inc(sem("norm_hi"), 1)

        def norm_hl(name):
            return sum(isinstance(NORMS[x][4], tuple) for x in run_norms[:NIDX[name]])

        def norm_tensor(pe, name):
            _, src, k0, gain, dst, scr, s0 = NORMS[name]
            if name in SAME:
                return
            if name in SUMMED:
                pe.wait_ge(sem("sum_acc"), 17 * list(SUMMED).index(name) + 17)
                pe.matmul(q[0][:, 0:S], ones[:], scr[:, s0, :], start=True, stop=True).then_inc(sem("norm_sum"), 1)
                return
            for g in range(4):
                pe.wait_ge(sem("norm_sq"), before(name, squares_of) + g + 1)
                for k in range(4):
                    mm = pe.matmul(q[0][:, 0:S], ones[:], scr[:, s0 + 4 * g + k, :], start=g + k == 0, stop=g + k == 6)
            mm.then_inc(sem("norm_sum"), 1)

        def norm_vector(dve, name):
            _, src, k0, gain, dst, scr, s0 = NORMS[name]
            i = NIDX[name]
            gkey, goff = gain if isinstance(gain, tuple) else (gain, 0)
            split = isinstance(dst, tuple)
            to, t0 = (scr, s0) if split else ((X, 0) if dst is None else (dst, 0))
            if sums_of(name):
                stds = before(name, sums_of) + 1
                dve.wait_ge(sem("norm_std"), stds)
                dve.reciprocal(rstd[:, 1, :], rstd[:, 0, :]).then_inc(sem("norm_rec"), 1)
                dve.wait_ge(sem("norm_rec"), stds)

            def low(g):
                dve.wait_ge(sem("norm_hi"), 4 * norm_hl(name) + g + 1)
                dve.tensor_tensor(dst[1][:, 4 * g:4 * g + 4, :], scr[:, s0 + 4 * g:s0 + 4 * g + 4, :],
                                  dst[0][:, 4 * g:4 * g + 4, :].bitcast(F32), ALU.subtract).then_inc(sem("norm_done"), 1)

            for g in range(4):
                for k in range(4 * g, 4 * g + 4):
                    o = dve.scalar_tensor_tensor(out=to[:, t0 + k, :], in0=src[:, k0 + k, :], scalar=col(gkey, goff + k),
                                                 in1=rstd[:, 1, :], op0=ALU.mult, op1=ALU.mult)
                o.then_inc(sem("norm_val" if split else "norm_done"), 1)
                if split and g:
                    low(g - 1)
            if split:
                low(3)

        def norm_ready(name):
            return ("norm_done", lambda g: 4 * NIDX[name] + g + 1)

        def norm_all(eng, name):
            eng.wait_ge(sem("norm_done"), 4 * NIDX[name] + 4)

        ATT = {"xa": dict(heads=4, hb=0, q0=16, k0=56, v0=60, causal=False, scr=(G, 20), dst=(BH, BL)),
               "fa": dict(heads=16, hb=4, q0=32, k0=0, v0=16, causal=True, scr=(G, 32), dst=(AH, AL))}
        SCALE = float(P) ** -0.5

        def att_bufs(name, s):
            t, o = ATT[name]["scr"]
            o += 9 * s
            flat = lambda b, k: t[:, o + b:o + b + k, :].rearrange("p a n -> p (a n)")
            return dict(qS=flat(0, 1), vS=flat(1, 1), S=flat(2, 2), P=flat(4, 2), PT=flat(6, 2), vt=flat(8, 1))

        fscr = G[:, 52:64, :]
        cneg, cpos = fscr[0:16, 0, :], fscr[0:16, 1, :]
        cT = fscr[:, 2, 0:32].rearrange("p (a h) -> p a h", a=2)
        selS = [fscr[0:16, 3 + s, 0:P] for s in range(2)]

        def settled(pool):
            pool.wait_ge(sem("masks32"), 1)

        def att_pool(pool, name):
            c = ATT[name]
            with pool.Fori(0, c["heads"] // 2) as i:
                for s in range(2):
                    b = att_bufs(name, s)
                    pool.wait_ge(sem("att_out"), i * 2 + (s + 1 + c["hb"]))
                    settled(pool)
                    pool.tensor_copy(b["qS"], tile(G, i * 2 + (c["q0"] + s))).then_inc(sem("att_staged"), 1)
                    pool.tensor_copy(b["vS"], tile(G, i * 2 + (c["v0"] + s))).then_inc(sem("att_staged"), 1)
                    if c["causal"]:
                        pool.tensor_copy(selS[s], ident[0:16, bass.ds(i * 2 + s, 1)].broadcast_to([16, P]))\
                            .then_inc(sem("att_staged"), 1)

        def att_tensor(pe, name):
            c = ATT[name]
            per = 3 if c["causal"] else 2
            W = (P, S) if c["causal"] else (S, S)
            with pe.Fori(0, c["heads"] // 2) as i:
                for s in range(2):
                    b = att_bufs(name, s)
                    pe.wait_ge(sem("att_staged"), i * (2 * per) + ((s + 1) * per + 2 * c["hb"]))
                    for t in range(2):
                        o = q[s][:, S * t:S * t + W[t]]
                        mm = pe.matmul(o, b["qS"][:, P * t:P * t + P], tile(G, i * 2 + (c["k0"] + s))[:, 0:W[t]],
                                       start=True, stop=not c["causal"])
                        if c["causal"]:
                            mm = pe.matmul(o, selS[s], cneg[:, 0:W[t]], start=False, stop=True)
                    mm.then_inc(sem("att_score"), 1)
                    for t in range(2):
                        mm = pe.transpose(q[4 + s][:, P * t:P * t + P], b["vS"][:, P * t:P * t + P], ident[:])
                    mm.then_inc(sem("att_vt"), 1)
                for s in range(2):
                    b = att_bufs(name, s)
                    pe.wait_ge(sem("att_prob"), i * 2 + (s + 1 + c["hb"]))
                    o = 0
                    for k in range(2):
                        for t in range(2):
                            if P * k < W[t]:
                                mm = pe.transpose(q[2 + s][:, o:o + P], b["P"][:, S * t + P * k:S * t + P * k + P], ident[:])
                                o += P
                    mm.then_inc(sem("att_pt"), 1)
                for s in range(2):
                    b = att_bufs(name, s)
                    pe.wait_ge(sem("att_ptc"), i * 2 + (s + 1 + c["hb"]))
                    pe.wait_ge(sem("att_vtc"), i * 2 + (s + 1 + c["hb"]))
                    pe.matmul(q[4 + s][:, S:2 * S], b["vt"][:, 0:P], b["PT"][:, 0:S], start=True, stop=False)
                    lo = P if c["causal"] else 0
                    pe.matmul(q[4 + s][:, S + lo:2 * S], b["vt"][:, P:2 * P], b["PT"][:, S:2 * S - lo], start=False, stop=True)\
                        .then_inc(sem("att_o"), 1)

        def att_scalar(act, name):
            c = ATT[name]
            W = (P, S) if c["causal"] else (S, S)
            n = 3 * P if c["causal"] else 4 * P
            with act.Fori(0, c["heads"] // 2) as i:
                for s in range(2):
                    b = att_bufs(name, s)
                    act.wait_ge(sem("att_max"), i * 2 + (s + 1 + c["hb"]))
                    src = b["S"] if c["causal"] else q[s]
                    for t in range(2):
                        e = act.activation(b["P"][:, S * t:S * t + W[t]], src[:, S * t:S * t + W[t]], ACT.Exp,
                                           bias=stat[:, s, t:t + 1], accum_out=stat[:, s, 2 + t:3 + t])
                    e.then_inc(sem("att_exp"), 1)
                for s in range(2):
                    b = att_bufs(name, s)
                    act.wait_ge(sem("att_pt"), i * 2 + (s + 1 + c["hb"]))
                    act.activation(b["PT"][:, 0:n], q[2 + s][:, 0:n], ACT.Copy).then_inc(sem("att_ptc"), 1)
                for s in range(2):
                    act.wait_ge(sem("att_o"), i * 2 + (s + 1 + c["hb"]))
                    act.activation(tile(c["dst"][0], i * 2 + s), q[4 + s][:, S:2 * S], ACT.Copy).then_inc(sem("att_ohi"), 1)

        def att_vector(dve, name):
            c = ATT[name]
            W = (P, S) if c["causal"] else (S, S)
            with dve.Fori(0, c["heads"] // 2) as i:
                for s in range(2):
                    b = att_bufs(name, s)
                    dve.wait_ge(sem("att_score"), i * 2 + (s + 1 + c["hb"]))
                    src = q[s]
                    if c["causal"]:
                        cm = causal[:, :, :].rearrange("p a n -> p (a n)")
                        for t in range(2):
                            o = dve.scalar_tensor_tensor(out=b["S"][:, S * t:S * t + W[t]], in0=q[s][:, S * t:S * t + W[t]],
                                                         scalar=cT[:, t, bass.ds(i * 2 + s, 1)], in1=cm[:, S - W[t]:S],
                                                         op0=ALU.add, op1=ALU.add)
                        o.then_inc(sem("att_masked"), 1)
                        dve.wait_ge(sem("att_masked"), i * 2 + (s + 1))
                        src = b["S"]
                    for t in range(2):
                        o = dve.tensor_reduce(stat[:, s, t:t + 1], src[:, S * t:S * t + W[t]], AXX, ALU.max, negate=True)
                    o.then_inc(sem("att_max"), 1)
                    dve.wait_ge(sem("att_vt"), i * 2 + (s + 1 + c["hb"]))
                    dve.tensor_copy(b["vt"], q[4 + s][:, 0:S]).then_inc(sem("att_vtc"), 1)
                for s in range(2):
                    b = att_bufs(name, s)
                    dve.wait_ge(sem("att_exp"), i * 2 + (s + 1 + c["hb"]))
                    dve.reciprocal(stat[:, s, 4:6], stat[:, s, 2:4]).then_inc(sem("att_rec"), 1)
                    dve.wait_ge(sem("att_rec"), i * 2 + (s + 1 + c["hb"]))
                    for t in range(2):
                        p_ = b["P"][:, S * t:S * t + W[t]]
                        o = dve.tensor_scalar(p_, p_, stat[:, s, 4 + t:5 + t], None, ALU.mult)
                    o.then_inc(sem("att_prob"), 1)
                for s in range(2):
                    dve.wait_ge(sem("att_ohi"), i * 2 + (s + 1 + c["hb"]))
                    dve.tensor_tensor(tile(c["dst"][1], i * 2 + s), q[4 + s][:, S:2 * S],
                                      tile(c["dst"][0], i * 2 + s).bitcast(F32), ALU.subtract).then_inc(sem("att_out"), 1)

        FB = [att_bufs("fa", s) for s in range(2)]
        HB = ATT["fa"]["hb"]
        FW = (P, S)

        def fused(eng, body, first, steps, after_first=None):
            n0, m0 = N0["fq"], M0["fq"]

            def chunk(i, t0):
                nb, mb = n0 + t0, m0 + t0
                body(i * 2 + t0, i * 2 + nb, i + nb // 2, nb % 2, i + mb // 2, mb % 2)

            chunk(0, 0)
            chunk(0, 1)
            if after_first:
                after_first()
            with eng.Fori(0, 7) as i:
                first(i)
                chunk(i, 2)
                steps[0](i)
                chunk(i, 3)
                steps[1](i)
            first(7)
            steps[0](7)
            steps[1](7)

        def fused_pool(pool):
            with pool.Fori(0, 8) as i:
                for s in range(2):
                    pool.wait_ge(sem("att_vt"), i * 2 + (HB + s - 1))
                    settled(pool)
                    pool.tensor_copy(FB[s]["vS"], tile(G, i * 2 + (16 + s))).then_inc(sem("att_staged"), 1)
                    pool.tensor_copy(selS[s], ident[0:16, bass.ds(i * 2 + s, 1)].broadcast_to([16, P]))\
                        .then_inc(sem("att_staged"), 1)

        def fused_tensor(pe, project_chunk, forget):
            v = lambda i, s: i * 2 + (s + 1 + HB)

            def scores(i):
                for s in range(2):
                    b = FB[s]
                    pe.wait_ge(sem("att_staged"), i * 4 + (2 * s + 2 + 2 * HB))
                    bank = (M0["fq"] + s) % 2
                    pe.wait_ge(sem(f"proj_out{bank}"), i + ((M0["fq"] + s) // 2 + 1))
                    for t in range(2):
                        o = q[s][:, S * t:S * t + FW[t]]
                        pe.matmul(o, b["qS"][:, P * t:P * t + P], tile(G, i * 2 + s)[:, 0:FW[t]], start=True, stop=False)
                        mm = pe.matmul(o, selS[s], cneg[:, 0:FW[t]], start=False, stop=True)
                    mm.then_inc(sem("att_score"), 1)

            def turned(i):
                for s in range(2):
                    b = FB[s]
                    pe.wait_ge(sem("att_out"), v(i, s))
                    for t in range(2):
                        mm = pe.transpose(q[4 + s][:, P * t:P * t + P], b["vS"][:, P * t:P * t + P], ident[:])
                    mm.then_inc(sem("att_vt"), 1)
                for s in range(2):
                    b = FB[s]
                    pe.wait_ge(sem("att_prob"), v(i, s))
                    for x, at_ in enumerate((0, S, S + P)):
                        mm = pe.transpose(q[2 + s][:, P * x:P * x + P], b["P"][:, at_:at_ + P], ident[:])
                    mm.then_inc(sem("att_pt"), 1)

            def output(i):
                for s in range(2):
                    b = FB[s]
                    pe.wait_ge(sem("att_ptc"), v(i, s))
                    pe.wait_ge(sem("att_vtc"), v(i, s))
                    pe.matmul(q[4 + s][:, S:2 * S], b["vt"][:, 0:P], b["PT"][:, 0:S], start=True, stop=False)
                    pe.matmul(q[4 + s][:, S + P:2 * S], b["vt"][:, P:2 * P], b["PT"][:, S:S + P], start=False, stop=True)\
                        .then_inc(sem("att_o"), 1)

            fused(pe, project_chunk, scores, (turned, output), forget)

        def fused_scalar(act):
            v = lambda i, s: i * 2 + (s + 1 + HB)

            def exps(i):
                for s in range(2):
                    b = FB[s]
                    act.wait_ge(sem("att_max"), v(i, s))
                    for t in range(2):
                        e = act.activation(b["P"][:, S * t:S * t + FW[t]], b["S"][:, S * t:S * t + FW[t]], ACT.Exp,
                                           bias=stat[:, s, t:t + 1], accum_out=stat[:, s, 2 + t:3 + t])
                    e.then_inc(sem("att_exp"), 1)

            def turned(i):
                for s in range(2):
                    act.wait_ge(sem("att_pt"), v(i, s))
                    act.activation(FB[s]["PT"][:, 0:3 * P], q[2 + s][:, 0:3 * P], ACT.Copy).then_inc(sem("att_ptc"), 1)

            def output(i):
                for s in range(2):
                    act.wait_ge(sem("att_o"), v(i, s))
                    act.activation(tile(AH, i * 2 + s), q[4 + s][:, S:2 * S], ACT.Copy).then_inc(sem("att_ohi"), 1)

            fused(act, lambda t, n, nh, pair, mh, bank: split_next(act, n, nh, pair, False), exps, (turned, output))

        def fused_vector(dve, ready):
            v = lambda i, s: i * 2 + (s + 1 + HB)

            def chunk(t, n, nh, pair, mh, bank):
                split_next(dve, n, nh, pair, False)
                dve.wait_ge(sem("w_used"), n * 2 + 2)
                s = (bank - M0["fq"]) % 2
                dve.tensor_scalar(FB[s]["qS"], ps[bank][:, 0:S], SCALE, None, ALU.mult).then_inc(sem(f"proj_out{bank}"), 1)

            def probs(i):
                for s in range(2):
                    b = FB[s]
                    dve.wait_ge(sem("att_score"), v(i, s))
                    cm = causal[:, :, :].rearrange("p a n -> p (a n)")
                    for t in range(2):
                        row = cT[:, t, bass.ds(i * 2 + s, 1)] if not isinstance(i, int) else cT[:, t, i * 2 + s:i * 2 + s + 1]
                        o = dve.scalar_tensor_tensor(out=b["S"][:, S * t:S * t + FW[t]], in0=q[s][:, S * t:S * t + FW[t]],
                                                     scalar=row, in1=cm[:, S - FW[t]:S], op0=ALU.add, op1=ALU.add)
                    o.then_inc(sem("att_masked"), 1)
                for s in range(2):
                    b = FB[s]
                    dve.wait_ge(sem("att_masked"), i * 2 + (s + 1))
                    for t in range(2):
                        o = dve.tensor_reduce(stat[:, s, t:t + 1], b["S"][:, S * t:S * t + FW[t]], AXX, ALU.max, negate=True)
                    o.then_inc(sem("att_max"), 1)
                for s in range(2):
                    dve.wait_ge(sem("att_exp"), v(i, s))
                    dve.reciprocal(stat[:, s, 4:6], stat[:, s, 2:4]).then_inc(sem("att_rec"), 1)
                for s in range(2):
                    dve.wait_ge(sem("att_rec"), v(i, s))
                    for t in range(2):
                        p_ = FB[s]["P"][:, S * t:S * t + FW[t]]
                        o = dve.tensor_scalar(p_, p_, stat[:, s, 4 + t:5 + t], None, ALU.mult)
                    o.then_inc(sem("att_prob"), 1)

            def values(i):
                for s in range(2):
                    dve.wait_ge(sem("att_vt"), v(i, s))
                    dve.tensor_copy(FB[s]["vt"], q[4 + s][:, 0:S]).then_inc(sem("att_vtc"), 1)

            def output(i):
                for s in range(2):
                    dve.wait_ge(sem("att_ohi"), v(i, s))
                    dve.tensor_tensor(tile(AL, i * 2 + s), q[4 + s][:, S:2 * S],
                                      tile(AH, i * 2 + s).bitcast(F32), ALU.subtract).then_inc(sem("att_out"), 1)

            fused(dve, chunk, probs, (values, output), ready)

        class Chain:

            def __init__(self, eng, name):
                self.eng, self.sem, self.n = eng, sem(name), 0

            def after(self, ins):
                self.n += 1
                ins.then_inc(self.sem, 1)
                self.eng.wait_ge(self.sem, self.n)

        def sb_bufs(s):
            flat = lambda b, n=1: BF[:, 10 * s + b:10 * s + b + n, :].rearrange("p a n -> p (a n)")
            return dict(kS=flat(0), vS=flat(1), qS=flat(2), z=flat(3, 2)[:, 0:384], e=flat(5, 2)[:, 0:384],
                        a=flat(7, 2)[:, 0:384], vt=flat(9))

        def diag(t):
            return t.rearrange("p (b n) -> p b n", n=P)[:, 0:3:2, :]

        def sb_pool(pool):
            phase_done(pool, "in_b")
            with pool.Fori(0, 4) as i:
                for s in range(2):
                    b = sb_bufs(s)
                    pool.wait_ge(sem("sb_out"), i * 2 + (s + 1))
                    settled(pool)
                    pool.tensor_copy(b["kS"], tile(G, i * 2 + (8 + s))).then_inc(sem("sb_staged"), 1)
                    pool.tensor_copy(b["vS"], tile(G, i * 2 + (16 + s))).then_inc(sem("sb_staged"), 1)

        def sb_tensor(pe):
            phase_done(pe, "in_b")
            with pe.Fori(0, 4) as i:
                for s in range(2):
                    b = sb_bufs(s)
                    pe.wait_ge(sem("sb_staged"), i * 4 + 2 * (s + 1))
                    query = tile(G, i * 2 + s)
                    pe.matmul(q[s][:, 0:S], b["kS"][:, 0:P], query, start=True, stop=True)
                    pe.matmul(q[s][:, S:384], b["kS"][:, P:S], query[:, P:S], start=True, stop=True).then_inc(sem("sb_z"), 1)
                    pe.transpose(q[2 + s][:, 0:P], b["vS"][:, 0:P], ident[:])
                    pe.transpose(q[2 + s][:, P:S], b["vS"][:, P:S], ident[:]).then_inc(sem("sb_vt"), 1)
                for s in range(2):
                    b = sb_bufs(s)
                    pe.wait_ge(sem("sb_spm"), i * 2 + (s + 1))
                    pe.matmul(q[4 + s][:, 0:S], kge[:], b["e"][:, 0:S], start=True, stop=False)
                    pe.matmul(q[4 + s][:, P:S], ones[:], b["e"][:, S:384], start=False, stop=True)
                    pe.matmul(q[4 + s][:, S:384], kge[:], b["e"][:, S:384], start=True, stop=True).then_inc(sem("sb_sum"), 1)
                for s in range(2):
                    b = sb_bufs(s)
                    pe.wait_ge(sem("sb_vtc"), i * 2 + (s + 1))
                    pe.wait_ge(sem("sb_exp"), i * 2 + (s + 1))
                    pe.matmul(q[s][:, 0:S], b["vt"][:, 0:P], b["a"][:, 0:S], start=True, stop=False)
                    pe.matmul(q[s][:, P:S], b["vt"][:, P:S], b["a"][:, S:384], start=False, stop=True).then_inc(sem("sb_o"), 1)

        def sb_scalar(act):
            with act.Fori(0, 4) as i:
                for s in range(2):
                    b = sb_bufs(s)
                    act.wait_ge(sem("sb_z"), i * 2 + (s + 1))
                    act.activation(b["z"], q[s][:, 0:384], ACT.Copy, scale=SCALE).then_inc(sem("sb_zc"), 1)
                    act.activation(b["e"], q[s][:, 0:384], ACT.Abs, scale=SCALE).then_inc(sem("sb_abs"), 1)
                for s in range(2):
                    b = sb_bufs(s)
                    act.wait_ge(sem("sb_abs"), i * 2 + (s + 1))
                    act.activation(b["e"], b["e"], ACT.Exp, scale=-1.0).then_inc(sem("sb_e"), 1)
                for s in range(2):
                    b = sb_bufs(s)
                    act.wait_ge(sem("sb_e"), i * 2 + (s + 1))
                    act.activation(b["e"], b["e"], ACT.Ln, bias=1.0).then_inc(sem("sb_ln"), 1)
                for s in range(2):
                    b = sb_bufs(s)
                    act.wait_ge(sem("sb_dm"), i * 2 + (s + 1))
                    act.activation(b["a"], b["a"], ACT.Exp).then_inc(sem("sb_exp"), 1)

        def sb_vector(dve):
            with dve.Fori(0, 4) as i:
                for s in range(2):
                    b = sb_bufs(s)
                    dve.wait_ge(sem("sb_vt"), i * 2 + (s + 1))
                    dve.tensor_copy(b["vt"], q[2 + s][:, 0:S]).then_inc(sem("sb_vtc"), 1)
                for s in range(2):
                    b = sb_bufs(s)
                    dve.wait_ge(sem("sb_ln"), i * 2 + (s + 1))
                    dve.scalar_tensor_tensor(out=b["e"], in0=b["z"], scalar=0.0, in1=b["e"], op0=ALU.max, op1=ALU.add)\
                       .then_inc(sem("sb_sp"), 1)
                for s in range(2):
                    b = sb_bufs(s)
                    dve.wait_ge(sem("sb_sp"), i * 2 + (s + 1))
                    dve.tensor_tensor(diag(b["e"]), diag(b["e"]), limit[:, 0, :].unsqueeze(1).broadcast_to([P, 2, P]), ALU.min)\
                       .then_inc(sem("sb_spm"), 1)
                for s in range(2):
                    b = sb_bufs(s)
                    dve.wait_ge(sem("sb_sum"), i * 2 + (s + 1))
                    dve.scalar_tensor_tensor(out=b["a"], in0=q[4 + s][:, 0:384], scalar=-1.0, in1=b["z"], op0=ALU.mult, op1=ALU.add)\
                       .then_inc(sem("sb_d"), 1)
                for s in range(2):
                    b = sb_bufs(s)
                    dve.wait_ge(sem("sb_d"), i * 2 + (s + 1))
                    dve.tensor_tensor(diag(b["a"]), diag(b["a"]), limit[:, 1, :].unsqueeze(1).broadcast_to([P, 2, P]), ALU.min)\
                       .then_inc(sem("sb_dm"), 1)
                for s in range(2):
                    dve.wait_ge(sem("sb_o"), i * 2 + (s + 1))
                    dve.tensor_copy(tile(G, i * 2 + s), q[s][:, 0:S]).then_inc(sem("sb_out"), 1)

        bf_ = lambda o, n: BF[:, o:o + n, :]
        gl_c, gl_x, gl_l = bf_(0, 2), bf_(2, 2), bf_(4, 2)
        gl_E, gl_Q, gl_K = [bf_(6, 2), bf_(8, 2)], [bf_(10, 2), bf_(12, 2)], [bf_(14, 2), bf_(16, 2)]
        gl_AT = bf_(18, 6).rearrange("p a (b n) -> p (a b) n", n=P).rearrange("p (x h) n -> p x h n", x=3)
        gl_vt = bf_(24, 4).rearrange("p a (b n) -> p (a b) n", n=P).rearrange("p (x h) n -> p x h n", x=2)
        gl_d, gl_nd = bf_(28, 2), bf_(30, 2)

        def level(t, l):
            return t.rearrange("p a (b n) -> p (a b) n", n=2 ** l)

        def bank4(b):
            return q[b][:, :].rearrange("p (h n) -> p h n", h=4)

        def gla_pool(pool):
            pool.wait_ge(sem("sb_out"), 10)
            pool.dma_start(w_s, a["w_sgu"][0].rearrange("g t s -> t g s")).then_inc(sem("sgu_in"), 16)
            pool.dma_start(b_s, a["b_sgu"]).then_inc(sem("sgu_in"), 16)
            pool.memset(gl_AT, 0.0).then_inc(*once("gl_zero"))
            for l in range(1, 9):
                pool.wait_ge(sem("gl_E"), l)
                if l > 2:
                    pool.wait_ge(sem("gl_mm"), l - 2)
                pool.tensor_tensor(gl_K[l % 2], G[:, 34:36, :], gl_E[l % 2], ALU.mult).then_inc(sem("gl_K"), 1)

        def keys_scalar(act, t):
            single("xkv", t, lambda t, n, nh, pair, mh, bank: split_next(act, n, nh, pair, False))

        def keys_vector(dve, t):
            def chunk(t, n, nh, pair, mh, bank):
                split_next(dve, n, nh, pair, False)
                out_copy(dve, G, 56)(t, n, mh, bank)
            single("xkv", t, chunk)

        def gla_scalar(act, ch):
            act.wait_ge(*after("gl_x"))
            ch.after(act.activation(gl_l, gl_x, ACT.Abs))
            ch.after(act.activation(gl_l, gl_l, ACT.Exp, scale=-1.0))
            act.activation(gl_l, gl_l, ACT.Ln, bias=1.0).then_inc(*once("gl_ln"))
            for l in range(1, 9):
                act.wait_ge(sem("gl_nd"), l)
                if l > 2:
                    act.wait_ge(sem("gl_K"), l - 2)
                    act.wait_ge(sem("gl_Q"), l - 2)
                act.activation(gl_E[l % 2], gl_nd, ACT.Exp).then_inc(sem("gl_E"), 1)
                if l > 1:
                    keys_scalar(act, l - 2)
            keys_scalar(act, 7)

        def gla_vector(dve, ch):
            dve.wait_ge(*after("gl_z"))
            dve.wait_ge(sem("sb_out"), 10)
            for j in range(2):
                o = dve.tensor_scalar(gl_x[:, j, :], q[0][:, S * j:S * j + S], col("b_gla", j), None, ALU.add)
            o.then_inc(*once("gl_x"))
            dve.wait_ge(*after("gl_x"))
            ch.after(dve.tensor_scalar(gl_d, gl_x, -1.0, 0.0, ALU.mult, ALU.max))
            dve.wait_ge(*after("gl_ln"))
            ch.after(dve.tensor_tensor(gl_d, gl_d, gl_l, ALU.add))
            ch.after(dve.tensor_scalar(gl_d, gl_d, -1.0 / 16.0, None, ALU.mult))
            for j in range(2):
                o = dve.tensor_tensor_scan(gl_c[:, j, :], ones[:, 0:1].broadcast_to([P, S]), gl_d[:, j, :], 0.0, ALU.mult, ALU.add)
            ch.after(o)
            ch.after(dve.tensor_scalar(G[:, 32:34, :], G[:, 32:34, :], 0.125, None, ALU.mult))

            def pick(l, lv):
                dve.wait_ge(sem("gl_mm"), lv)
                b0 = 2 * (lv % 2)
                if l == 8:
                    o = dve.tensor_copy(gl_AT[:, 1], bank4(b0))
                else:
                    mask = m_id[:, :] if l == 0 else upmask[:, l - 1, :]
                    for x, b in ((0, b0), (2, b0 + 1)):
                        o = dve.copy_predicated(gl_AT[:, x], mask.unsqueeze(1).broadcast_to([P, 4, P]), bank4(b))
                o.then_inc(sem("gl_pick"), 1)

            dve.wait_ge(*after("gl_zero"))
            for l in range(1, 9):
                c = level(gl_c, l)
                n = 2 ** l
                if l > 1:
                    dve.wait_ge(sem("gl_E"), l - 1)
                ch.after(dve.tensor_tensor(level(gl_d, l), c, c[:, :, n // 2 - 1:n // 2].broadcast_to([P, 512 // n, n]), ALU.subtract))
                dve.scalar_tensor_tensor(out=gl_nd, in0=gl_d, scalar=-1.0, in1=gl_d, op0=ALU.mult, op1=ALU.min).then_inc(sem("gl_nd"), 1)
                if l > 1:
                    pick(l - 1, l - 1)
                dve.wait_ge(sem("gl_E"), l)
                dve.tensor_tensor(gl_Q[l % 2], G[:, 32:34, :], gl_E[l % 2], ALU.mult).then_inc(sem("gl_Q"), 1)
                if l > 1:
                    keys_vector(dve, l - 2)
            pick(8, 8)
            pick(0, 9)
            keys_vector(dve, 7)
            dve.wait_ge(*after("gl_vt"))
            for x in range(2):
                o = dve.tensor_copy(gl_vt[:, x], bank4(4 + x))
            o.then_inc(*once("gl_vtc"))
            dve.wait_ge(*after("gl_o"))
            for x in range(2):
                o = dve.tensor_copy(G[:, 32 + 2 * x:34 + 2 * x, :], q[x][:, :].rearrange("p (a n) -> p a n", a=2))
            o.then_inc(*once("gl_out"))

        def gla_tensor(pe):
            rows_done = Chain(pe, "rows_done")
            keys = project(pe, "xkv", AH, AL, norm_ready("mem"))
            pe.wait_ge(sem("sb_out"), 10)
            for j in range(2):
                mm = pe.matmul(q[0][:, S * j:S * j + S], gup[:, P * j:P * j + P], rT[:, :], start=True, stop=True)
            mm.then_inc(*once("gl_z"))
            for h in range(4):
                for x in range(2):
                    mm = pe.transpose(q[4 + x][:, P * h:P * h + P], G[:, 36 + h, P * x:P * x + P], ident[:])
            mm.then_inc(*once("gl_vt"))
            pe.wait_ge(*after("gl_x"))
            for lv, l in enumerate([1, 2, 3, 4, 5, 6, 7, 8, 0], 1):
                if l:
                    pe.wait_ge(sem("gl_Q"), l)
                    pe.wait_ge(sem("gl_K"), l)
                if lv > 2:
                    pe.wait_ge(sem("gl_pick"), lv - 2)
                kk, qq = (gl_K[l % 2], gl_Q[l % 2]) if l else (G[:, 34:36, :], G[:, 32:34, :])
                for h in (0, 2, 1, 3):
                    for x, (ts, tt) in enumerate([(0, 1)] if l == 8 else [(0, 0), (1, 1)]):
                        r = slice(64 * (h % 2), 64 * (h % 2) + 64)
                        mm = pe.matmul(q[2 * (lv % 2) + x][:, P * h:P * h + P], kk[r, h // 2, P * ts:P * ts + P],
                                       qq[r, h // 2, P * tt:P * tt + P], start=True, stop=True)
                    if h == 2:
                        rows_done.after(mm)
                mm.then_inc(sem("gl_mm"), 1)
                if lv < 9:
                    single("xkv", lv - 1, keys)
            pe.wait_ge(sem("gl_pick"), 9)
            pe.wait_ge(*after("gl_vtc"))
            for h in range(4):
                o = q[h // 2][:, S * (h % 2):S * (h % 2) + S]
                pe.matmul(o[:, 0:P], gl_vt[:, 0, h, :], gl_AT[:, 0, h, :], start=True, stop=True)
                pe.matmul(o[:, P:S], gl_vt[:, 0, h, :], gl_AT[:, 1, h, :], start=True, stop=False)
                mm = pe.matmul(o[:, P:S], gl_vt[:, 1, h, :], gl_AT[:, 2, h, :], start=False, stop=True)
            mm.then_inc(*once("gl_o"))

        sg_e, sg_sq = bf_(0, 8), bf_(8, 4)
        sg_vt = bf_(12, 4).rearrange("p a (b n) -> p (a b) n", n=P).rearrange("p (x h) n -> p x h n", x=2)
        sg_w = bf_(16, 2).rearrange("p a (b n) -> p (a b) n", n=P)

        def sgu_scalar(act, ch):
            act.wait_ge(*after("gl_out"))
            for h, lo in ((0, 4), (1, 0)):
                x, e = G[:, 44 + lo:48 + lo, :], sg_e[:, lo:lo + 4, :]
                act.activation(e, x, ACT.Square).then_inc(sem("sg_x2"), 1)
                act.wait_ge(sem("sg_arg"), h + 1)
                act.activation(e, e, ACT.Exp, scale=-GELU).then_inc(sem("sg_exp"), 1)
            act.wait_ge(sem("sg_gelu"), 1)
            act.activation(sg_sq, G[:, 48:52, :], ACT.Square).then_inc(*once("sg_sq"))
            act.wait_ge(*after("sg_ss"))
            act.activation(rstd[:, 0, :], q[0][:, 0:S], ACT.Sqrt, scale=1.0 / 512, bias=eps[:, 0:1]).then_inc(*once("sg_std"))
            act.wait_ge(*after("sg_wt"))
            act.activation(sg_w, bank4(3), ACT.Copy).then_inc(*once("sg_wtc"))

        def sgu_vector(dve, ch):
            for h, lo in ((0, 4), (1, 0)):
                x, e = G[:, 44 + lo:48 + lo, :], sg_e[:, lo:lo + 4, :]
                dve.wait_ge(sem("sg_x2"), h + 1)
                ch.after(dve.tensor_scalar(e, e, 0.044715, 1.0, ALU.mult, ALU.add))
                dve.tensor_tensor(e, e, x, ALU.mult).then_inc(sem("sg_arg"), 1)
                dve.wait_ge(sem("sg_exp"), h + 1)
                ch.after(dve.tensor_scalar(e, e, 1.0, None, ALU.add))
                ch.after(dve.reciprocal(e, e))
                dve.tensor_tensor(x, x, e, ALU.mult).then_inc(sem("sg_gelu"), 1)
            dve.wait_ge(*after("sg_std"))
            ch.after(dve.reciprocal(rstd[:, 1, :], rstd[:, 0, :]))
            for g in range(4):
                o = dve.scalar_tensor_tensor(out=G[:, 48 + g, :], in0=G[:, 48 + g, :], scalar=col("sgu_norm", g),
                                             in1=rstd[:, 1, :], op0=ALU.mult, op1=ALU.mult)
            o.then_inc(*once("sg_v"))
            dve.wait_ge(*after("sg_vt"))
            for x in range(2):
                o = dve.tensor_copy(sg_vt[:, x], bank4(1 + x))
            o.then_inc(*once("sg_vtc"))
            dve.wait_ge(*after("sg_mixed"))
            for x in range(2):
                u = G[:, 44 + 2 * x:46 + 2 * x, :]
                o = dve.tensor_tensor(u, q[4 + x][:, :].rearrange("p (a n) -> p a n", a=2), u, ALU.mult)
            o.then_inc(*once("sg_out"))

        def sgu_pool(pool):
            pool.wait_ge(*after("sg_wtc"))
            pool.affine_select(out=sg_w, in_=sg_w, compare_op=ALU.is_ge, fill=0.0, base=0,
                               pattern=[[0, 4], [1, P]], channel_multiplier=-1).then_inc(*once("sg_wm"))

        def sgu_tensor(pe):
            pe.wait_ge(*after("gl_out"))
            pe.wait_ge(sem("sgu_in"), 32)
            for g in range(4):
                mm = pe.transpose(q[3][:, P * g:P * g + P], w_s[:, g, :], ident[:])
            mm.then_inc(*once("sg_wt"))
            pe.wait_ge(*after("sg_sq"))
            for g in range(4):
                mm = pe.matmul(q[0][:, 0:S], ones[:], sg_sq[:, g, :], start=g == 0, stop=g == 3)
            mm.then_inc(*once("sg_ss"))
            pe.wait_ge(*after("sg_v"))
            for g in range(4):
                for x in range(2):
                    mm = pe.transpose(q[1 + x][:, P * g:P * g + P], G[:, 48 + g, P * x:P * x + P], ident[:])
            mm.then_inc(*once("sg_vt"))
            pe.wait_ge(*after("sg_vtc"))
            pe.wait_ge(*after("sg_wm"))
            for g in range(4):
                for x in range(2):
                    o = q[4 + g // 2][:, S * (g % 2) + P * x:S * (g % 2) + P * x + P]
                    pe.matmul(o, sg_vt[:, x, g, :], sg_w[:, g, :], start=True, stop=False)
                    mm = pe.matmul(o, ones[0:1, :], b_s[0:1, g, :], start=False, stop=True)
            mm.then_inc(*once("sg_mixed"))

        MIX_O, MIX_G = [0, 4, 32, 44], [24, 28, 40, 52]

        af = lambda o, n: AF[:, o:o + n, :]

        def mix_scalar(act):
            act.wait_ge(*after("sg_out"))
            for g in range(4):
                act.activation(af(4 * g, 4), G[:, MIX_G[g]:MIX_G[g] + 4, :], ACT.Exp, scale=-1.0).then_inc(sem("mix_e"), 1)
            for g in range(4):
                act.activation(af(16 + 4 * g, 4), G[:, MIX_O[g]:MIX_O[g] + 4, :], ACT.Square).then_inc(sem("mix_sq"), 1)
                act.wait_ge(sem("mix_ss"), g + 1)
                for x in range(2):
                    o = act.activation(af(16 + 4 * g + 2 * x, 2), q[2 * (g % 2) + x][:, :].rearrange("p (a n) -> p a n", a=2),
                                       ACT.Sqrt, scale=1.0 / P, bias=eps[:, 0:1])
                o.then_inc(sem("mix_std"), 1)
                if g:
                    act.wait_ge(sem("mix_val"), g)
                    act.activation(BH[:, 4 * g - 4:4 * g, :], af(4 * g - 4, 4), ACT.Copy).then_inc(sem("mix_hi"), 1)
            act.wait_ge(sem("mix_val"), 4)
            act.activation(BH[:, 12:16, :], af(12, 4), ACT.Copy).then_inc(sem("mix_hi"), 1)

        def mix_tensor(pe):
            for g in range(4):
                pe.wait_ge(sem("mix_sq"), g + 1)
                if g > 1:
                    pe.wait_ge(sem("mix_std"), g - 1)
                for k in range(4):
                    mm = pe.matmul(q[2 * (g % 2) + k // 2][:, S * (k % 2):S * (k % 2) + S], ones[:], AF[:, 16 + 4 * g + k, :],
                                   start=True, stop=True)
                mm.then_inc(sem("mix_ss"), 1)

        def mix_vector(dve, ch):
            def low(g):
                dve.wait_ge(sem("mix_hi"), g + 1)
                dve.tensor_tensor(BL[:, 4 * g:4 * g + 4, :], af(4 * g, 4), BH[:, 4 * g:4 * g + 4, :].bitcast(F32), ALU.subtract)\
                   .then_inc(sem("mix_done"), 1)

            for g in range(4):
                e, r, o = af(4 * g, 4), af(16 + 4 * g, 4), MIX_O[g]
                dve.wait_ge(sem("mix_e"), g + 1)
                ch.after(dve.tensor_scalar(e, e, 1.0, None, ALU.add))
                ch.after(dve.reciprocal(e, e))
                ch.after(dve.tensor_tensor(e, e, G[:, MIX_G[g]:MIX_G[g] + 4, :], ALU.mult))
                dve.wait_ge(sem("mix_std"), g + 1)
                ch.after(dve.reciprocal(r, r))
                for k in range(4):
                    i = dve.scalar_tensor_tensor(out=AF[:, 16 + 4 * g + k, :], in0=G[:, o + k, :], scalar=col("out_norm", 4 * g + k),
                                                 in1=AF[:, 16 + 4 * g + k, :], op0=ALU.mult, op1=ALU.mult)
                ch.after(i)
                dve.tensor_tensor(e, e, r, ALU.mult).then_inc(sem("mix_val"), 1)
                if g:
                    low(g - 1)
            low(3)

        class LoopChain:

            def __init__(self, eng, name, i, per):
                self.eng, self.sem, self.i, self.per, self.k = eng, sem(name), i, per, 0

            def do(self, ins):
                ins.then_inc(self.sem, 1)
                self.k += 1
                return self.k

            def need(self, k):
                self.eng.wait_ge(self.sem, self.i * self.per + k)

            def end(self):
                assert self.k == self.per, self.k

        H, XT = G, G[:, 16:32, :]
        MIXES = {"r": (0, 0, (AH, AL)), "k": (1, 1, (BH, BL)), "v": (2, 2, (AH, AL)), "w": (3, 3, (BH, BL)),
                 "a": (4, 4, (AH, AL)), "g": (5, 5, (BH, BL))}

        def xs_scalar_part(act, mix, t):
            m, c, dst = MIXES[mix]
            if m:
                act.wait_ge(sem("xs_done"), t + (16 * m - 15))
            src = omm[:, bass.ds(t + 16 * c, 1)] if not isinstance(t, int) else omm[:, 16 * c + t:16 * c + t + 1]
            act.activation(tile(XT, t), tile(H, t), ACT.Copy, scale=src).then_inc(sem("xs_here"), 1)

        def xs_scalar_high(act, mix, t):
            m, c, dst = MIXES[mix]
            act.wait_ge(sem("xs_val"), t + (16 * m + 1))
            act.activation(tile(dst[0], t), tile(XT, t), ACT.Copy).then_inc(sem("xs_hi"), 1)

        def xs_vector_add(dve, mix, t):
            m, c, dst = MIXES[mix]
            dve.wait_ge(sem("xs_here"), t + (16 * m + 1))
            x = tile(XT, t)
            dve.scalar_tensor_tensor(out=x[:, 1:S], in0=tile(H, t)[:, 0:S - 1], scalar=col("x_mix", t + 16 * c),
                                     in1=x[:, 1:S], op0=ALU.mult, op1=ALU.add).then_inc(sem("xs_val"), 1)

        def xs_vector_low(dve, mix, t):
            m, c, dst = MIXES[mix]
            dve.wait_ge(sem("xs_hi"), t + (16 * m + 1))
            dve.tensor_tensor(tile(dst[1], t), tile(XT, t), tile(dst[0], t).bitcast(F32), ALU.subtract).then_inc(sem("xs_done"), 1)

        def xs_bulk(eng, mix, first, second):
            with eng.Fori(0, 4) as i:
                for u in range(4):
                    first(eng, mix, i * 4 + u)
                for u in range(4):
                    second(eng, mix, i * 4 + u)

        def xs_ready(mix):
            return ("xs_done", lambda g: 16 * MIXES[mix][0] + 4 * g + 4)

        SPILL = {"rw_r": 0, "rw_k": 1, "rw_v": 2}

        def spill_before(name, mh, bank):
            m0 = M0["rw_r"]
            return mh - (m0 // 2 if m0 % 2 == bank else (m0 + 1) // 2)

        def spill_scalar(act, name, nxt):
            def evac(t, n, mh, bank):
                act.wait_ge(sem("w_used"), n * 2 + 2)
                before = spill_before(name, mh, bank)
                if not (isinstance(before, int) and before == 0):
                    act.wait_ge(sem(f"spilled{bank}"), before * 16)
                act.activation(G[:, 40 + bank, :], ps[bank][:, 0:S], ACT.Copy).then_inc(sem(f"proj_out{bank}"), 1)
                xs_scalar_part(act, nxt, t)
                xs_scalar_high(act, nxt, t)
            return evac

        def spill_vector(dve, nxt):
            def evac(t, n, mh, bank):
                xs_vector_add(dve, nxt, t)
                xs_vector_low(dve, nxt, t)
            return evac

        def spill_pool(pool, name):
            def body(t, n, nh, pair, mh, bank):
                pool.wait_ge(sem(f"proj_out{bank}"), mh + 1)
                settled(pool)
                pool.dma_start(spill_ap[SPILL[name], bass.ds(t, 1)].rearrange("a p n -> p (a n)"), G[:, 40 + bank, :])\
                    .then_inc(sem(f"spilled{bank}"), 16)
            over(pool, name, body)

        LORA = {"rw_w1": (0, 96, ACT.Tanh), "rw_a1": (1, 96, ACT.Copy), "rw_g1": (2, P, ACT.Sigmoid)}

        def lora_scalar(act, name):
            k0, parts, func = LORA[name]

            def evac(t, n, mh, bank):
                f = G[0:parts, 36 + k0 + t, :]
                act.wait_ge(sem("w_used"), n * 2 + 2)
                act.activation(f, ps[bank][0:parts, 0:S], func).then_inc(sem(f"proj_out{bank}"), 1)
                act.wait_ge(sem(f"proj_out{bank}"), mh + 1)
                act.activation(LH[0:parts, k0 + t, :], f, ACT.Copy).then_inc(sem("lora_hi"), 1)
            return evac

        def lora_vector(dve, name):
            k0, parts, func = LORA[name]

            def evac(t, n, mh, bank):
                dve.wait_ge(sem("lora_hi"), k0 + t + 1)
                dve.tensor_tensor(LL[0:parts, k0 + t, :], G[0:parts, 36 + k0 + t, :], LH[0:parts, k0 + t, :].bitcast(F32), ALU.subtract)\
                   .then_inc(sem("lora_done"), 1)
            return evac

        def up_tensor(pe):
            n0 = N0["rw_up"]
            for hc in range(12):
                which, part = divmod(hc, 4)
                slot = 2 * ((n0 + hc // 2) % 2) + hc % 2
                pe.wait_ge(sem("w_lo"), 2 * n0 + hc + 1)
                pe.wait_ge(sem("lora_done"), (1, 2, 4)[which])
                if hc > 1:
                    pe.wait_ge(sem("up_out"), hc - 1)
                kn, parts = ((1, 96), (1, 96), (2, P))[which]
                flat = lambda w: w[slot][:, :, :].rearrange("p k n -> p (k n)")
                for o in range(4):
                    dst = q[2 * (hc % 2) + o // 2][:, S * (o % 2):S * (o % 2) + S]
                    for k in range(kn):
                        c = slice(512 * k + P * o, 512 * k + P * o + P)
                        x = which + k
                        pe.matmul(dst, flat(wh)[0:parts, c], LH[0:parts, x, :], start=k == 0, stop=False)
                        pe.matmul(dst, flat(wh)[0:parts, c], LL[0:parts, x, :], start=False, stop=False)
                        mm = pe.matmul(dst, flat(wl)[0:parts, c], LH[0:parts, x, :], start=False, stop=k == kn - 1)
                mm.then_inc(sem("w_used"), 1)

        def up_vector(dve):
            n0 = N0["rw_up"]
            for t in range(6):
                split_next(dve, n0 + t, (n0 + t) // 2, (n0 + t) % 2, n0 + t >= TOTAL - 2)
                for j in range(2):
                    hc = 2 * t + j
                    dve.wait_ge(sem("w_used"), 2 * n0 + hc + 1)
                    if hc > 1:
                        dve.wait_ge(sem(f"up_spilled{hc % 2}"), 16 * (hc // 2))
                    for x in range(2):
                        g = 44 + 4 * (hc % 2) + 2 * x
                        o = dve.tensor_copy(G[:, g:g + 2, :], q[2 * (hc % 2) + x][:, :].rearrange("p (a n) -> p a n", a=2))
                    o.then_inc(sem("up_out"), 1)

        def up_pool(pool):
            for hc in range(12):
                which, part = divmod(hc, 4)
                pool.wait_ge(sem("up_out"), hc + 1)
                pool.dma_start(spill_ap[3 + which, 4 * part:4 * part + 4].rearrange("a p n -> p a n"),
                               G[:, 44 + 4 * (hc % 2):48 + 4 * (hc % 2), :]).then_inc(sem(f"up_spilled{hc % 2}"), 16)

        def rw_layout():
            left = [[G, 0, 64], [BF, 0, 32]]

            def take(cnt, blocks=False):
                for piece in left:
                    if piece[2] >= cnt:
                        view = piece[0][:, piece[1]:piece[1] + cnt, :]
                        piece[1] += cnt
                        piece[2] -= cnt
                        if blocks:
                            return view.rearrange("p a (b n) -> p (a b) n", n=P)
                        return view.rearrange("p a n -> p (a n)") if cnt == 1 else view
                raise AssertionError(cnt)

            temps, cores = [], []
            for s in range(2):
                t = dict(zip(("in", "ex"), (take(4), take(3))))
                t.update((key, take(1)) for key in ("ld", "c", "cm", "kk", "sq", "t"))
                temps.append(t)
                b = {key: take(2, True) for key in ("M", "AK", "RB", "RK", "U", "T", "PP", "tok")}
                b.update((key, take(1)) for key in ("xsa", "y", "yc", "ysq"))
                cores.append(b)
            sets = []
            for par in range(2):
                sets.append([])
                for s in range(2):
                    t = {key: take(1) for key in ("at", "bt", "kt", "rt", "bon")}
                    t["vg"] = take(2)
                    sets[par].append(t)
            for par in range(2):
                for s in range(2):
                    sets[par][s]["s1"] = s1_all[:, 2 * par + s, :]
            return temps, cores, sets

        RW_T, RW_C, RW_S = rw_layout()
        chunks = lambda t: t.rearrange("p (c n) -> p c n", n=P)
        rng = lambda h: slice(64 * h, 64 * h + 64)

        def bc4(m):
            return m.unsqueeze(1).broadcast_to([P, 4, P])

        def omka(j):
            return neg[:, bass.ds(j + 32, 1)] if not isinstance(j, int) else neg[:, j + 32:j + 33]

        def ncol(j):
            return neg[:, bass.ds(j, 1)] if not isinstance(j, int) else neg[:, j:j + 1]

        def turns(eng, start, turn, finish=None):
            start(0, 0)
            turn(0, 0, 1, None)
            with eng.Fori(0, 3) as ii:
                turn(ii * 2 + 1, 1, ii * 2 + 2, ii * 2)
                turn(ii * 2 + 2, 0, ii * 2 + 3, ii * 2 + 1)
            turn(7, 1, None, 6)
            if finish:
                finish(7, 1)

        def rw_pool(pool):
            for b in range(2):
                pool.wait_ge(sem(f"spilled{b}"), 16 * 24)
                pool.wait_ge(sem(f"up_spilled{b}"), 16 * 6)
            phase_done(pool, "rw_g1")
            pool.wait_ge(*after("rw_zero"))

            def load(j, par):
                for s in range(2):
                    pool.wait_ge(sem("rw_bon"), j * 2 + (s + 1))
                    settled(pool)
                    pair = bass.ds(j * 2 + s, 1) if not isinstance(j, int) else slice(j * 2 + s, j * 2 + s + 1)
                    part = lambda x: spill_ap[x, pair].rearrange("x a p n -> p x (a n)")
                    pool.dma_start(RW_T[s]["in"][:, 2:4, :], part(slice(3, 5))).then_inc(sem(f"rw_in{s}"), 16)
                    pool.dma_start(RW_T[s]["in"][:, 0:2, :], part(slice(0, 2))).then_inc(sem(f"rw_in{s}"), 16)

            def load_values(j, par):
                for s in range(2):
                    pool.wait_ge(sem("rw_out"), j * 2 + (s + 1))
                    settled(pool)
                    pair = bass.ds(j * 2 + s, 1) if not isinstance(j, int) else slice(j * 2 + s, j * 2 + s + 1)
                    pool.dma_start(RW_S[par][s]["vg"], spill_ap[slice(2, 6, 3), pair].rearrange("x a p n -> p x (a n)"))\
                        .then_inc(sem(f"rw_vg{s}"), 16)

            def ahead(j, par):
                load(j, par)
                for s in range(2):
                    b, t = RW_S[par][s], RW_T[s]
                    pool.wait_ge(sem("rw_t"), j * 2 + (s + 1))
                    settled(pool)
                    pool.tensor_tensor(t["in"][:, 1, :], t["in"][:, 1, :], t["t"], ALU.mult).then_inc(sem("rw_k1"), 1)
                for s in range(2):
                    b, t = RW_S[par][s], RW_T[s]
                    pool.wait_ge(sem("rw_exp"), j * 2 + (s + 1))
                    settled(pool)
                    pool.tensor_tensor(b["rt"], t["in"][:, 0, :], t["ex"][:, 0, :], ALU.mult).then_inc(sem("rw_rt"), 1)
                    pool.wait_ge(sem("rw_k1"), j * 2 + (s + 1))
                    settled(pool)
                    pool.tensor_tensor(b["kt"], t["in"][:, 1, :], t["ex"][:, 1, :], ALU.mult).then_inc(sem("rw_kt"), 1)
                load_values(j, par)

            def reset(i):
                for s in range(2):
                    pool.wait_ge(sem("rw_y"), i * 2 + (s + 1))
                    settled(pool)
                    pool.tensor_tensor(touched[:, s:s + 1], ones[:, 0:1], ones[:, 0:1], ALU.mult)
                    pool.tensor_copy(RW_C[s]["T"], bc4(ident[:, :])).then_inc(sem("rw_start"), 1)
                    pool.tensor_copy(RW_C[s]["U"], bc4(ident[:, :])).then_inc(sem("rw_start"), 1)

            def turn(i, par, j, last):
                reset(i)
                if j is not None:
                    ahead(j, 1 - par)

            turns(pool, ahead, turn)

        def rw_scalar(act):
            def gates(j, par):
                for s in range(2):
                    t = RW_T[s]
                    act.wait_ge(sem(f"rw_in{s}"), j * 32 + 32)
                    for x in range(2):
                        e = act.activation(t["in"][:, 2 + x, :], t["in"][:, 2 + x, :], ACT.Sigmoid, bias=col(("w0", "a0")[x], j * 2 + s))
                    e.then_inc(sem("rw_sig"), 1)

            def rate(j, par):
                for s in range(2):
                    t = RW_T[s]
                    act.wait_ge(sem("rw_sig"), j * 2 + (s + 1))
                    act.wait_ge(sem("rw_kk0"), j * 2 + (s + 1))
                    act.activation(t["t"], t["in"][:, 3, :], ACT.Identity, scale=col("k_a", j * 2 + s),
                                   bias=omka(j * 2 + s)).then_inc(sem("rw_t"), 1)
                    act.activation(t["sq"], t["kk"], ACT.Square).then_inc(sem("rw_sq"), 1)

            def decays(j, par):
                for s in range(2):
                    t, b = RW_T[s], RW_S[par][s]
                    act.wait_ge(sem("rw_cm"), j * 2 + (s + 1))
                    act.activation(t["ex"][:, 0, :], t["cm"], ACT.Exp)
                    act.activation(t["ex"][:, 1, :], t["cm"], ACT.Exp, scale=-1.0)
                    act.activation(t["ex"][:, 2, :], t["ld"], ACT.Exp)
                    act.activation(b["s1"][:, 64:65], t["c"][:, 191:192], ACT.Exp)
                    act.activation(b["s1"][:, 65:66], t["cm"][:, P - 1:P], ACT.Exp).then_inc(sem("rw_exp"), 1)

            def lengths(j, par):
                for s in range(2):
                    act.wait_ge(sem("rw_ss"), j * 2 + (s + 1))
                    act.activation(RW_T[s]["sq"], ps[s][:, 0:S], ACT.Sqrt).then_inc(sem("rw_nrm"), 1)

            def start(j, par):
                gates(j, par)
                rate(j, par)
                decays(j, par)
                lengths(j, par)

            def turn(i, par, j, last):
                for s in range(2):
                    act.wait_ge(sem("rw_m2"), i * 2 + (s + 1))
                    act.activation(RW_C[s]["tok"], bank4(3 * s + 2), ACT.Copy).then_inc(sem("rw_tok"), 1)
                if last is not None:
                    deviations(last)
                if j is not None:
                    gates(j, 1 - par)
                for lv in range(6):
                    for s in range(2):
                        act.wait_ge(sem("rw_p"), i * 12 + (2 * lv + s + 1))
                        act.activation(RW_C[s]["PP"], bank4(3 * s + 1), ACT.Copy).then_inc(sem("rw_pc"), 1)
                    if lv < 5:
                        for s in range(2):
                            act.wait_ge(sem("rw_tt"), i * 10 + (2 * lv + s + 1))
                            act.activation(RW_C[s]["T"], bank4(3 * s + 2), ACT.Copy).then_inc(sem("rw_tc"), 1)
                    if j is not None and 0 < lv < 4:
                        (rate, decays, lengths)[lv - 1](j, 1 - par)
                    if last is not None and lv == 0:
                        spreads(last)
                    if last is not None and lv == 4:
                        high(last)
                for c in range(2):
                    for s in range(2):
                        act.wait_ge(sem("rw_x"), i * 4 + (2 * c + s + 1))
                        act.activation(RW_C[s]["xsa"][:, 0:P], q[3 * s + 1 - c][:, 0:P], ACT.Copy).then_inc(sem("rw_xc"), 1)
                    for s in range(2):
                        act.wait_ge(sem("rw_sa"), i * 4 + (2 * c + s + 1))
                        act.activation(RW_C[s]["xsa"][:, P:S], q[3 * s + 1 - c][:, P:S], ACT.Copy).then_inc(sem("rw_sac"), 1)
                for s in range(2):
                    act.wait_ge(sem("rw_y"), i * 2 + (s + 3))
                    act.activation(RW_C[s]["y"], q[3 * s + 2][:, 0:S], ACT.Copy).then_inc(sem("rw_yc"), 1)

            def deviations(i):
                for s in range(2):
                    act.wait_ge(sem("rw_yd"), i * 2 + (s + 1))
                    act.activation(RW_C[s]["ysq"], RW_C[s]["yc"], ACT.Square).then_inc(sem("rw_ysq"), 1)

            def spreads(i):
                for s in range(2):
                    act.wait_ge(sem("rw_var"), i * 2 + (s + 1))
                    act.activation(RW_C[s]["ysq"], ps[s][:, S:2 * S], ACT.Sqrt, scale=1.0 / 64, bias=eps_ln[:, 0:1])\
                       .then_inc(sem("rw_sd"), 1)

            def high(i):
                for s in range(2):
                    act.wait_ge(sem("rw_val"), i * 2 + (s + 1))
                    act.activation(tile(AH, i * 2 + s), RW_C[s]["yc"], ACT.Copy).then_inc(sem("rw_hi"), 1)

            def finish(i, par):
                deviations(i)
                spreads(i)
                high(i)

            turns(act, start, turn, finish)

        def rw_tensor(pe):
            def squares(j, par):
                for s in range(2):
                    pe.wait_ge(sem("rw_sq"), j * 2 + (s + 1))
                    pe.matmul(ps[s][:, 0:S], bones[:], RW_T[s]["sq"], start=True, stop=True).then_inc(sem("rw_ss"), 1)

            def bonus(j, par):
                for s in range(2):
                    pe.wait_ge(sem("rw_rk"), j * 2 + (s + 1))
                    pe.matmul(ps[s][:, S:2 * S], bones[:], RW_T[s]["t"], start=True, stop=True).then_inc(sem("rw_bs"), 1)

            def start(j, par):
                squares(j, par)
                bonus(j, par)

            def turn(i, par, j, last):
                v = lambda s: i * 2 + (s + 1)
                halves = LoopChain(pe, "rw_rows", i, 6)

                def pairs(s, *products):
                    b = RW_S[par][s]
                    for h in range(2):
                        for bank, l, r in products:
                            for c in range(2):
                                mm = pe.matmul(q[bank][:, P * (2 * h + c):P * (2 * h + c) + P], b[l][rng(h), P * c:P * c + P],
                                               b[r][rng(h), P * c:P * c + P], start=True, stop=True)
                        if h == 0:
                            halves.need(halves.do(mm))
                    return mm

                for s in range(2):
                    pe.wait_ge(sem("rw_bt"), v(s))
                    pe.wait_ge(sem("rw_kt"), v(s))
                    pe.wait_ge(sem("rw_rt"), v(s))
                    pe.wait_ge(sem("rw_yc"), i * 2 + (s + 1))
                    pairs(s, (3 * s, "at", "bt"), (3 * s + 1, "bt", "at"), (3 * s + 2, "kt", "at")).then_inc(sem("rw_m1"), 1)
                for s in range(2):
                    b = RW_S[par][s]
                    pe.wait_ge(sem("rw_m1e"), v(s))
                    pe.wait_ge(sem(f"rw_vg{s}"), i * 16 + 16)
                    pairs(s, (3 * s, "bt", "rt"), (3 * s + 1, "kt", "rt"))
                    for x, src in enumerate((b["bt"][:, 0:P], b["kt"][:, 0:P], b["vg"][:, 0, 0:P], b["vg"][:, 0, P:S])):
                        mm = pe.transpose(q[3 * s + 2][:, P * x:P * x + P], src, ident[:])
                    mm.then_inc(sem("rw_m2"), 1)
                if last is not None:
                    means(last)
                pe.wait_ge(sem("rw_m2e"), v(1))
                pe.wait_ge(sem("rw_tok"), v(1))
                for lv in range(6):
                    for s in range(2):
                        b = RW_C[s]
                        if lv:
                            pe.wait_ge(sem("rw_tc"), i * 10 + (2 * lv - 2 + s + 1))
                        for x in range(4):
                            mm = pe.matmul(q[3 * s + 1][:, P * x:P * x + P], b["M"][:, x, :], b["U"][:, x, :], start=True, stop=True)
                        mm.then_inc(sem("rw_p"), 1)
                    for s in range(2):
                        b = RW_C[s]
                        pe.wait_ge(sem("rw_pc"), i * 12 + (2 * lv + s + 1))
                        for x in range(4):
                            mm = pe.matmul(q[3 * s][:, P * x:P * x + P], b["T"][:, x, :], b["PP"][:, x, :], start=True, stop=True)
                        mm.then_inc(sem("rw_g"), 1)
                    if lv < 5:
                        for s in range(2):
                            b = RW_C[s]
                            pe.wait_ge(sem("rw_u"), i * 12 + (2 * lv + s + 1))
                            for x in range(4):
                                mm = pe.transpose(q[3 * s + 2][:, P * x:P * x + P], b["U"][:, x, :], ident[:])
                            mm.then_inc(sem("rw_tt"), 1)
                    if lv == 0 and last is not None:
                        spreads(last)
                    if lv == 2 and j is not None:
                        squares(j, 1 - par)
                for c in range(2):
                    for s in range(2):
                        b, t = RW_C[s], RW_S[par][s]
                        bank = 3 * s + 1 - c
                        pe.wait_ge(sem("rw_u"), i * 12 + (10 + s + 1))
                        if c:
                            pe.wait_ge(sem("rw_s1c"), v(s))
                        for h in range(2):
                            o = q[bank][:, 64 * h:64 * h + 64]
                            mm = pe.matmul(o, b["AK"][:, 2 * h + c, :], b["tok"][:, 2 + c, rng(h)], start=True, stop=c == 0)
                            if c:
                                mm = pe.matmul(o, t["at"][rng(h), P:S], t["s1"][rng(h), 0:64], start=False, stop=True)
                            if c and h == 0:
                                halves.need(halves.do(mm))
                        mm.then_inc(sem("rw_x"), 1)
                    for s in range(2):
                        b = RW_C[s]
                        bank = 3 * s + 1 - c
                        pe.wait_ge(sem("rw_xc"), i * 4 + (2 * c + s + 1))
                        for h in range(2):
                            mm = pe.matmul(q[bank][:, P + 64 * h:P + 64 * h + 64], b["U"][:, 2 * h + c, :], b["xsa"][:, rng(h)],
                                           start=True, stop=True)
                        mm.then_inc(sem("rw_sa"), 1)
                    for s in range(2):
                        b, t = RW_C[s], RW_S[par][s]
                        pe.wait_ge(sem("rw_sac"), i * 4 + (2 * c + s + 1))
                        for h in range(2):
                            sa = b["xsa"][:, P + 64 * h:P + 64 * h + 64]
                            vt = b["tok"][:, 2 + c, rng(h)]
                            if c == 0:
                                o = q[3 * s + 1][rng(h), S:S + 64]
                                pe.matmul(o, b["tok"][:, 0, rng(h)], sa, start=True, stop=False)
                                mm = pe.matmul(o, b["tok"][:, 1, rng(h)], vt, start=False, stop=True)
                        if c == 0:
                            mm.then_inc(sem("rw_s1"), 1)
                        for h in range(2):
                            sa = b["xsa"][:, P + 64 * h:P + 64 * h + 64]
                            vt = b["tok"][:, 2 + c, rng(h)]
                            o = q[3 * s + 2][rng(h), P * c:P * c + P]
                            pe.matmul(o, sa, b["RB"][:, 2 * h + c, :], start=True, stop=False)
                            mm = pe.matmul(o, vt, b["RK"][:, 2 * h + c, :], start=False, stop=c == 0)
                            if c:
                                mm = pe.matmul(o, t["s1"][rng(h), 0:64], t["rt"][rng(h), P:S], start=False, stop=True)
                        if c:
                            mm.then_inc(sem("rw_y"), 1)
                if j is not None:
                    bonus(j, 1 - par)
                halves.end()

            def means(i):
                for s in range(2):
                    pe.wait_ge(sem("rw_bon"), i * 2 + (s + 3) if isinstance(i, int) and i == 7 else i * 2 + (s + 5))
                    pe.wait_ge(sem("rw_yc"), i * 2 + (s + 3))
                    pe.matmul(ps[s][:, 0:S], bones[:], RW_C[s]["y"], start=True, stop=True).then_inc(sem("rw_mu"), 1)

            def spreads(i):
                for s in range(2):
                    pe.wait_ge(sem("rw_ysq"), i * 2 + (s + 1))
                    pe.matmul(ps[s][:, S:2 * S], bones[:], RW_C[s]["ysq"], start=True, stop=True).then_inc(sem("rw_var"), 1)

            def finish(i, par):
                means(i)
                spreads(i)

            turns(pe, start, turn, finish)

        def touch(dve, k):
            dve.tensor_copy(touched[:, 2 + k:3 + k], eps[:, 0:1])

        def pred(dve, out_, mask, data):
            return dve.copy_predicated(out_, bc4(mask), data)

        def rw_vector(dve):
            for s in range(2):
                for key in ("M", "AK", "RB", "RK"):
                    o = dve.memset(RW_C[s][key], 0.0)
            o.then_inc(*once("rw_zero"))
            dve.wait_ge(*after("rw_zero"))

            def two(ch, f, needs=None):
                done = []
                for s in range(2):
                    if needs:
                        ch.need(needs[s])
                    done.append(ch.do(f(s, RW_T[s])))
                return done

            class Ahead:

                def __init__(self, j, par):
                    self.j, self.par, self.ch = j, par, LoopChain(dve, "rw_ahead", j, 18)
                    self.v = lambda s: j * 2 + (s + 1)

                def part0(self):
                    for s in range(2):
                        t = RW_T[s]
                        dve.wait_ge(sem(f"rw_in{s}"), self.j * 32 + 32)
                        dve.tensor_scalar(t["kk"], t["in"][:, 1, :], col("k_k", self.j * 2 + s), None, ALU.mult).then_inc(sem("rw_kk0"), 1)

                def part1(self):
                    for s in range(2):
                        dve.wait_ge(sem("rw_sig"), self.v(s))
                        self.ch.do(dve.tensor_scalar(RW_T[s]["ld"], RW_T[s]["in"][:, 2, :], -EXP_HALF, None, ALU.mult))

                def part2(self):
                    def scan(s, t):
                        for c in range(2):
                            o = dve.tensor_tensor_scan(t["c"][:, P * c:P * c + P], ones[:, :], t["ld"][:, P * c:P * c + P], 0.0, ALU.mult, ALU.add)
                        return o
                    k = two(self.ch, scan, [1, 2])
                    self.k = two(self.ch, lambda s, t: dve.tensor_tensor(chunks(t["cm"]), chunks(t["c"]),
                                 chunks(t["c"])[:, :, 63:64].broadcast_to([P, 2, P]), ALU.subtract), k)

                def part3(self):
                    for s in range(2):
                        self.ch.need(self.k[s])
                        dve.tensor_tensor(RW_T[s]["ld"], RW_T[s]["cm"], RW_T[s]["ld"], ALU.subtract).then_inc(sem("rw_cm"), 1)

                def part4(self):
                    for s in range(2):
                        dve.wait_ge(sem("rw_nrm"), self.v(s))
                        self.ch.do(dve.tensor_scalar(RW_T[s]["sq"], RW_T[s]["sq"], 1e-12, None, ALU.max))
                    k = two(self.ch, lambda s, t: dve.reciprocal(t["sq"], t["sq"]), [self.ch.k - 1, self.ch.k])
                    self.k = two(self.ch, lambda s, t: dve.tensor_tensor(t["kk"], t["kk"], t["sq"], ALU.mult), k)

                def part5(self):
                    st = RW_S[self.par]
                    k = two(self.ch, lambda s, t: dve.tensor_tensor(st[s]["bt"], t["kk"], t["in"][:, 3, :], ALU.mult), self.k)
                    for s in range(2):
                        dve.wait_ge(sem("rw_exp"), self.v(s))
                        self.ch.do(dve.scalar_tensor_tensor(out=st[s]["at"], in0=RW_T[s]["kk"], scalar=-1.0, in1=RW_T[s]["ex"][:, 2, :],
                                                            op0=ALU.mult, op1=ALU.mult))
                    self.k = k

                def part6(self):
                    st = RW_S[self.par]
                    for s in range(2):
                        self.ch.need(self.k[s])
                        dve.tensor_tensor(st[s]["bt"], st[s]["bt"], RW_T[s]["ex"][:, 1, :], ALU.mult).then_inc(sem("rw_bt"), 1)
                    for s in range(2):
                        t = RW_T[s]
                        dve.wait_ge(sem("rw_k1"), self.v(s))
                        dve.scalar_tensor_tensor(out=t["t"], in0=t["in"][:, 0, :], scalar=col("r_k", self.j * 2 + s), in1=t["in"][:, 1, :],
                                                 op0=ALU.mult, op1=ALU.mult).then_inc(sem("rw_rk"), 1)

                def part7(self):
                    st = RW_S[self.par]
                    for s in range(2):
                        dve.wait_ge(sem("rw_bs"), self.v(s))
                        dve.wait_ge(sem("rw_kt"), self.v(s))
                        dve.wait_ge(sem(f"rw_vg{s}"), self.j * 16 + 16)
                        self.ch.do(dve.tensor_copy(st[s]["bon"], ps[s][:, S:2 * S]))
                    for s in range(2):
                        self.ch.need(self.ch.k - 1 + s)
                        dve.tensor_tensor(st[s]["bon"], st[s]["bon"], st[s]["vg"][:, 0, :], ALU.mult).then_inc(sem("rw_bon"), 1)
                    assert self.ch.k == self.ch.per, self.ch.k

            def start(j, par):
                a_ = Ahead(j, par)
                for part in (a_.part0, a_.part1, a_.part2, a_.part3, a_.part4, a_.part5, a_.part6, a_.part7):
                    part()

            def turn(i, par, j, last):
                v = lambda s: i * 2 + (s + 1)
                fin = Finish(last, 1 - par) if last is not None else None
                nxt = Ahead(j, 1 - par) if j is not None else None
                for s in range(2):
                    b = RW_C[s]
                    dve.wait_ge(sem("rw_start"), i * 4 + (2 * s + 2))
                    dve.wait_ge(sem("rw_m1"), v(s))
                    touch(dve, s)
                    pred(dve, b["M"], m_low[:, :], bank4(3 * s))
                    pred(dve, b["T"], lowmask[:, 0, :], bank4(3 * s))
                    pred(dve, b["U"], upmask[:, 0, :], bank4(3 * s + 1))
                    pred(dve, b["AK"], m_up[:, :], bank4(3 * s + 2)).then_inc(sem("rw_m1e"), 1)
                for s in range(2):
                    b = RW_C[s]
                    dve.wait_ge(sem("rw_m2"), v(s))
                    touch(dve, 2 + s)
                    pred(dve, b["RB"], m_upi[:, :], bank4(3 * s))
                    pred(dve, b["RK"], m_upi[:, :], bank4(3 * s + 1)).then_inc(sem("rw_m2e"), 1)
                if fin:
                    fin.centre()
                for lv in range(6):
                    for s in range(2):
                        dve.wait_ge(sem("rw_g"), i * 12 + (2 * lv + s + 1))
                        touch(dve, 4 + 2 * lv + s)
                        pred(dve, RW_C[s]["U"], upmask[:, lv + 1, :], bank4(3 * s)).then_inc(sem("rw_u"), 1)
                    if nxt:
                        if lv == 0:
                            nxt.part0()
                        elif lv == 1:
                            nxt.part1()
                            nxt.part2()
                        elif lv == 2:
                            nxt.part3()
                        elif lv == 4:
                            nxt.part4()
                        elif lv == 5:
                            nxt.part5()
                    if fin:
                        if lv == 2:
                            fin.scale()
                        elif lv == 3:
                            fin.gate()
                        elif lv == 4:
                            fin.low()
                for s in range(2):
                    t = RW_S[par][s]
                    dve.wait_ge(sem("rw_s1"), v(s))
                    dve.tensor_scalar(t["s1"][:, 0:64], q[3 * s + 1][:, S:S + 64], t["s1"][:, 65:66], t["s1"][:, 64:65],
                                      ALU.mult, ALU.mult).then_inc(sem("rw_s1c"), 1)
                if nxt:
                    nxt.part6()
                    nxt.part7()

            class Finish:

                def __init__(self, i, par):
                    self.i, self.par, self.ch = i, par, LoopChain(dve, "rw_dve", i, 8)
                    self.v = lambda s: i * 2 + (s + 1)

                def centre(self):
                    for s in range(2):
                        b = RW_C[s]
                        dve.wait_ge(sem("rw_mu"), self.v(s))
                        dve.scalar_tensor_tensor(out=b["yc"], in0=ps[s][:, 0:S], scalar=-1.0 / 64, in1=b["y"], op0=ALU.mult, op1=ALU.add)\
                           .then_inc(sem("rw_yd"), 1)

                def each(self, f):
                    self.k = two(self.ch, lambda s, t: f(s, RW_C[s]), self.k)

                def scale(self):
                    self.k = []
                    for s in range(2):
                        dve.wait_ge(sem("rw_sd"), self.v(s))
                        self.k.append(self.ch.do(dve.reciprocal(RW_C[s]["ysq"], RW_C[s]["ysq"])))
                    self.each(lambda s, b: dve.tensor_tensor(b["yc"], b["yc"], b["ysq"], ALU.mult))

                def gate(self):
                    i, st = self.i, RW_S[self.par]
                    self.each(lambda s, b: dve.tensor_scalar(b["yc"], b["yc"], col("lnx_w", i * 2 + s), col("lnx_b", i * 2 + s), ALU.mult, ALU.add))
                    self.each(lambda s, b: dve.tensor_tensor(b["yc"], b["yc"], st[s]["bon"], ALU.add))
                    for s in range(2):
                        self.ch.need(self.k[s])
                        dve.tensor_tensor(RW_C[s]["yc"], RW_C[s]["yc"], st[s]["vg"][:, 1, :], ALU.mult).then_inc(sem("rw_val"), 1)
                    self.ch.end()

                def low(self):
                    i = self.i
                    for s in range(2):
                        dve.wait_ge(sem("rw_hi"), self.v(s))
                        dve.tensor_tensor(tile(AL, i * 2 + s), RW_C[s]["yc"], tile(AH, i * 2 + s).bitcast(F32), ALU.subtract)\
                           .then_inc(sem("rw_out"), 1)

            def finish(i, par):
                f = Finish(i, par)
                f.centre()
                f.scale()
                f.gate()
                f.low()

            turns(dve, start, turn, finish)

        def relu_scalar(act, idx):
            def evac(t, n, mh, bank):
                r, sqr = G[:, 16 + bank, :], G[:, 18 + bank, :]
                act.wait_ge(sem("w_used"), n * 2 + 2)
                if not (isinstance(t, int) and t < 2 and idx == 0):
                    act.wait_ge(sem("hid_done"), t + (idx - 1))
                act.activation(r, ps[bank][:, 0:S], ACT.Relu).then_inc(sem(f"proj_out{bank}"), 1)
                act.wait_ge(sem("hid_sq"), t + (idx + 1))
                act.activation(tile(BH, t), sqr, ACT.Copy).then_inc(sem("hid_hi"), 1)
            return evac

        def relu_vector(dve, idx):
            def evac(t, n, mh, bank):
                r, sqr = G[:, 16 + bank, :], G[:, 18 + bank, :]
                dve.wait_ge(sem(f"proj_out{bank}"), mh + 1)
                dve.tensor_tensor(sqr, r, r, ALU.mult).then_inc(sem("hid_sq"), 1)
                dve.wait_ge(sem("hid_hi"), t + (idx + 1))
                dve.tensor_tensor(tile(BL, t), sqr, tile(BH, t).bitcast(F32), ALU.subtract).then_inc(sem("hid_done"), 1)
            return evac

        block = ctx.enter_context(nc.Block())
        done2 = stop >= 2

        xtok = G[:, 0:16, :].rearrange("p (b k) n -> p b (k n)", b=2)
        mtok = G[:, 16:32, :].rearrange("p (b k) n -> p b (k n)", b=2)
        otok = xtok
        m32 = G[:, 50:60, :].rearrange("p a (b n) -> p (a b) n", n=P)
        spill_ap = spill.ap()

        def mlp(layer):
            return [(f"up{layer}_{x}", f"dn{layer}_{x}", 64 * layer + 16 * x) for x in range(4)]

        @block.sync
        def _(sp):
            sp.dma_start(mtok, a["mem"][0].rearrange("(b p) d -> p b d", p=P)).then_inc(sem("mem_in"), 16)
            sp.dma_start(xtok, a["x"][0].rearrange("(b p) d -> p b d", p=P)).then_inc(sem("x_in"), 16)
            for name, _c, special in phases:
                def body(t, n, nh, pair, mh, bank):
                    for j in range(2):
                        slot = 2 * pair + j
                        if not (isinstance(n, int) and n < 2):
                            sp.wait_ge(sem("w_lo"), n * 2 + (j - 3))
                        src, kind = SRC[name](t, j)
                        flat = raw[slot][:, :, :].rearrange("p k n -> p (k n)")
                        if kind == "xo":
                            dst = flat.rearrange("p (k n) -> p k n", k=4)
                        elif kind == "up96":
                            dst = flat[0:96, 0:512]
                        elif kind == "up256":
                            dst = flat.rearrange("p (k n) -> p k n", k=2)
                        else:
                            dst = raw[slot][:, :, 0:kind]
                        sp.dma_start(dst, src).then_inc(sem(f"w_loaded{slot}"), 16)
                if special:
                    for t in range(COUNT[name]):
                        n_ = N0[name] + t
                        body(t, n_, n_ // 2, n_ % 2, 0, 0)
                else:
                    over(sp, name, body, peel=2 if N0[name] == 0 else 0)
            for b in range(2):
                sp.wait_ge(sem("fin_d"), 4)
                sp.wait_ge(sem("fin_a"), 4)
                sp.dma_start(out[0, P * b:P * b + P, :], otok[:, b, :]).then_inc(sem("stored"), 16)
            sp.wait_ge(sem("stored"), 32)

        @block.gpsimd
        def _(pool):
            ch = Chain(pool, "pool_chain")
            pool.memset(prow, 0.0).then_inc(*once("prow_zero"))
            pool.memset(ident[:], 0.0)
            pool.memset(ones[:], 1.0)
            pool.memset(bones[:], 1.0)
            pool.memset(kge[:], 1.0)
            pool.memset(causal[:], 0.0)
            pool.memset(limit[:], 3e38)
            pool.memset(m32[:, 0:14, :], 0.0)
            ch.after(pool.memset(m32[:, 14:17, :], 1.0))
            pool.affine_select(out=ident[:], in_=ident[:], compare_op=ALU.not_equal, fill=1.0, base=0,
                               pattern=[[-1, P]], channel_multiplier=1).then_inc(*once("ident"))
            keep = lambda t, pattern, base, fill=0.0, op=ALU.is_ge, cm=1: pool.affine_select(
                out=t, in_=t, compare_op=op, fill=fill, base=base, pattern=pattern, channel_multiplier=cm)
            bo = bones[:, :].rearrange("p (b n) -> p b n", n=64)
            ch.after(keep(bo, [[-64, 2], [0, 64]], 0))
            keep(bo, [[64, 2], [0, 64]], 63, cm=-1)
            keep(kge[:], [[-1, P]], 0)
            keep(causal[:, 1, :], [[-1, P]], 0, NEG)
            for x, f in enumerate((0.0, NEG)):
                keep(limit[:, x, :], [[1, P]], 0, f, ALU.is_gt, -1)
            keep(m32[:, 14, :], [[-1, P]], 0, op=ALU.is_gt)
            keep(m32[:, 15, :], [[1, P]], 0, op=ALU.is_gt, cm=-1)
            keep(m32[:, 16, :], [[1, P]], 0, cm=-1)
            pool.memset(eps[:], EPS).then_inc(sem("sb_out"), 2)
            pool.memset(eps_ln[:], LNX_EPS).then_inc(sem("rw_out"), 4)
            for x, name in enumerate(("rw_bon", "rw_yc", "rw_y")):
                pool.memset(touched[:, x:x + 1], 0.0).then_inc(sem(name), 2)
            pool.memset(stat[:], 0.0).then_inc(sem("att_out"), 2)
            lows, ups = [], []
            for l in range(1, 8):
                n = 2 ** l
                view = lambda x: m32[:, x, :].rearrange("p (b n) -> p b n", n=n)
                lows.append((view(l - 1)[:, :, 0:n // 2], n))
                ups.append((view(6 + l)[:, :, n // 2:n], n))
            for t, n in lows + ups:
                o = pool.memset(t, 1.0)
            ch.after(o)
            for (t, n), (u, _n) in zip(lows, ups):
                keep(t, [[-n, P // n], [0, n // 2]], -n // 2)
                o = keep(u, [[-n, P // n], [0, n // 2]], 0)
            ch.after(o)
            for (t, n), (u, _n) in zip(lows, ups):
                keep(t, [[n, P // n], [0, n // 2]], n - 1, cm=-1)
                o = keep(u, [[n, P // n], [0, n // 2]], n // 2 - 1, cm=-1)
            o.then_inc(sem("masks32"), 1)
            sb_pool(pool)
            gla_pool(pool)
            sgu_pool(pool)
            if stop >= 2:
                squares_pool(pool, "xattn")
                phase_done(pool, "xq")
                att_pool(pool, "xa")
            if stop >= 3:
                for name in SPILL:
                    spill_pool(pool, name)
                up_pool(pool)
                rw_pool(pool)
            if stop >= 4:
                squares_pool(pool, "ffn0")
            if stop >= 5:
                squares_pool(pool, "kv")
                pool.wait_ge(*after("f_ready"))
                fused_pool(pool)
            if stop >= 6:
                squares_pool(pool, "ffn1")
            squares_pool(pool, "final2")

        @block.scalar
        def _(act):
            act.wait_ge(*after("prow_zero"))
            for src, r, cnt in rows:
                v = a[src]
                while len(v.shape) > 1:
                    v = v.rearrange("a b c -> (a b) c") if len(v.shape) == 3 else v.rearrange("a b -> (a b)")
                act.dma_start(prow[r % P:r % P + cnt, r // P, :], v.rearrange("(r c) -> r c", c=P)).then_inc(sem("prow_in"), 16)
            act.dma_start(gup[:], a["w_gla_gate_up"][0]).then_inc(sem("small_in"), 16)
            act.dma_start(bf[:], a["b_f_2"].rearrange("(n o) -> n o", o=1)).then_inc(sem("small_in"), 16)
            ch = Chain(act, "act_chain")
            for u in range(1, 16, 2):
                act.wait_ge(sem("tr"), u + 1)
                dst = G[:, 32 + 2 * u:34 + 2 * u, :] if u < 8 else X[:, 2 * u - 16:2 * u - 14, :]
                act.activation(dst, q[u % 4][:, :].rearrange("p (a n) -> p a n", a=2), ACT.Copy).then_inc(sem("tr_a"), 1)
            act.wait_ge(*after("prm_t"))
            act.activation(prm[:], q[4][:, :], ACT.Copy).then_inc(*once("prm"))
            for h in range(4):
                act.wait_ge(sem(f"w_loaded{h}"), 16)
                act.activation(wh[h][:], raw[h][:], ACT.Copy).then_inc(sem("w_hi"), 1)
            act.wait_ge(sem("masks32"), 1)
            act.wait_ge(sem("tr_a"), 8)
            act.wait_ge(sem("tr_d"), 8)
            norm_scalar(act, "mix")
            norm_scalar(act, "mem")
            for name in ("in_a", "in_r", "in_b"):
                stream(act, name, peel=2 if name == "in_a" else 0)
            sb_scalar(act)
            gla_scalar(act, ch)
            sgu_scalar(act, ch)
            mix_scalar(act)
            stream(act, "out")
            phase_done(act, "out")
            if stop >= 2:
                norm_scalar(act, "xattn")
                stream(act, "xq")
                att_scalar(act, "xa")
                for t in range(4):
                    split_next(act, N0["xo"] + t, (N0["xo"] + t) // 2, (N0["xo"] + t) % 2, N0["xo"] + t >= TOTAL - 2)
                act.wait_ge(sem("xo_out"), 8)
            if stop >= 3:
                norm_scalar(act, "final1")
                act.wait_ge(sem("norm_done"), 4 * NIDX["final1"] + 4)
                norm_scalar(act, "rwkv")
                act.wait_ge(sem("norm_done"), 4 * NIDX["rwkv"] + 4)
                xs_bulk(act, "r", xs_scalar_part, xs_scalar_high)
                for name, nxt in (("rw_r", "k"), ("rw_k", "v"), ("rw_v", "w")):
                    stream(act, name, spill_scalar(act, name, nxt), peel=2 if name == "rw_r" else 0)
                stream(act, "rw_w1", lora_scalar(act, "rw_w1"))
                xs_bulk(act, "a", xs_scalar_part, xs_scalar_high)
                stream(act, "rw_a1", lora_scalar(act, "rw_a1"))
                xs_bulk(act, "g", xs_scalar_part, xs_scalar_high)
                stream(act, "rw_g1", lora_scalar(act, "rw_g1"))
                for t in range(6):
                    n = N0["rw_up"] + t
                    split_next(act, n, n // 2, n % 2, False)
                rw_scalar(act)
                stream(act, "rw_o")
                phase_done(act, "rw_o")
            for layer, lim in ((0, 4), (1, 6)):
                if layer == 1 and stop >= 5:
                    norm_scalar(act, "kv")
                    norm_scalar(act, "fox")
                    for name in ("fk", "fv", "ff"):
                        stream(act, name)
                    act.wait_ge(*after("f_in"))
                    ch.after(act.activation(fscr[0:16, 6, :], fscr[0:16, 5, :], ACT.Abs))
                    ch.after(act.activation(fscr[0:16, 6, :], fscr[0:16, 6, :], ACT.Exp, scale=-1.0))
                    act.activation(fscr[0:16, 6, :], fscr[0:16, 6, :], ACT.Ln, bias=1.0).then_inc(*once("f_ln"))
                    fused_scalar(act)
                    stream(act, "fo")
                    phase_done(act, "fo")
                if stop >= lim:
                    norm_scalar(act, f"ffn{layer}")
                    for up, dn, idx in mlp(layer):
                        stream(act, up, relu_scalar(act, idx), peel=2 if idx == 0 else 0)
                        stream(act, dn)
                    phase_done(act, f"dn{layer}_3")
            norm_scalar(act, "final2")
            for u in range(1, 8, 2):
                act.wait_ge(sem("fin_t"), u + 1)
                act.activation(otok[:, u // 4, 512 * (u % 4):512 * (u % 4) + 512], q[u % 4][:, :], ACT.Copy).then_inc(sem("fin_a"), 1)

        @block.vector
        def _(dve):
            ch = Chain(dve, "dve_chain")
            for u in range(0, 16, 2):
                dve.wait_ge(sem("tr"), u + 1)
                dst = G[:, 32 + 2 * u:34 + 2 * u, :] if u < 8 else X[:, 2 * u - 16:2 * u - 14, :]
                dve.tensor_copy(dst, q[u % 4][:, :].rearrange("p (a n) -> p a n", a=2)).then_inc(sem("tr_d"), 1)
            dve.wait_ge(sem("masks32"), 1)
            dve.wait_ge(*after("ident"))
            dve.tensor_copy(lowmask[:], m32[:, 0:7, :])
            dve.tensor_copy(upmask[:], m32[:, 7:14, :])
            dve.tensor_copy(m_low[:], m32[:, 14, :])
            dve.tensor_copy(m_up[:], m32[:, 15, :])
            dve.tensor_copy(m_upi[:], m32[:, 16, :])
            dve.tensor_copy(m_id[:], ident[:]).then_inc(sem("masks"), 1)
            dve.wait_ge(sem("masks"), 1)
            dve.wait_ge(*after("prm"))
            pc = lambda key, n: prm[:, COL[key]:COL[key] + n]
            dve.tensor_scalar(omm[:], pc("x_mix", 96), -1.0, 1.0, ALU.mult, ALU.add)
            dve.tensor_scalar(neg[:, 0:16], pc("w0", 16), -1.0, None, ALU.mult)
            dve.tensor_scalar(neg[:, 16:32], pc("a0", 16), -1.0, None, ALU.mult)
            dve.tensor_scalar(neg[:, 32:48], pc("k_a", 16), -1.0, 1.0, ALU.mult, ALU.add).then_inc(*once("prm2"))
            for h in range(4):
                dve.wait_ge(sem("w_hi"), h + 1)
                dve.tensor_tensor(wl[h][:], raw[h][:], wh[h][:].bitcast(F32), ALU.subtract).then_inc(sem("w_lo"), 1)
            norm_vector(dve, "mix")
            norm_vector(dve, "mem")
            stream(dve, "in_a", out_copy(dve, G, 0), peel=2)
            stream(dve, "in_r", lambda t, n, mh, bank: (
                dve.wait_ge(sem("w_used"), n * 2 + 2),
                dve.tensor_copy(rT[:], ps[bank][0:16, 0:S]).then_inc(sem(f"proj_out{bank}"), 1)))
            stream(dve, "in_b", out_copy(dve, G, 40))
            sb_vector(dve)
            gla_vector(dve, ch)
            sgu_vector(dve, ch)
            mix_vector(dve, ch)
            stream(dve, "out", out_resid(dve))
            if stop >= 2:
                norm_vector(dve, "xattn")
                stream(dve, "xq", out_copy(dve, G, 16, SCALE))
                att_vector(dve, "xa")
                for t in range(4):
                    n = N0["xo"] + t
                    split_next(dve, n, n // 2, n % 2, n >= TOTAL - 2)
                    for j in range(2):
                        hc = 2 * t + j
                        dve.wait_ge(sem("w_used"), 2 * n + j + 1)
                        x = X[:, 2 * hc:2 * hc + 2, :]
                        dve.tensor_tensor(x, q[hc % 2][:, :].rearrange("p (a n) -> p a n", a=2), x, ALU.add).then_inc(sem("xo_out"), 1)
            if stop >= 3:
                norm_vector(dve, "final1")
                norm_vector(dve, "rwkv")
                xs_bulk(dve, "r", xs_vector_add, xs_vector_low)
                for name, nxt in (("rw_r", "k"), ("rw_k", "v"), ("rw_v", "w")):
                    stream(dve, name, spill_vector(dve, nxt))
                stream(dve, "rw_w1", lora_vector(dve, "rw_w1"))
                xs_bulk(dve, "a", xs_vector_add, xs_vector_low)
                stream(dve, "rw_a1", lora_vector(dve, "rw_a1"))
                xs_bulk(dve, "g", xs_vector_add, xs_vector_low)
                stream(dve, "rw_g1", lora_vector(dve, "rw_g1"))
                up_vector(dve)
                for b in range(2):
                    dve.wait_ge(sem(f"up_spilled{b}"), 16 * 6)
                rw_vector(dve)
                stream(dve, "rw_o", out_resid(dve))
            for layer, lim in ((0, 4), (1, 6)):
                if layer == 1 and stop >= 5:
                    norm_vector(dve, "kv")
                    norm_vector(dve, "fox")
                    stream(dve, "fk", out_copy(dve, G, 0))
                    stream(dve, "fv", out_copy(dve, G, 16))
                    stream(dve, "ff", lambda t, n, mh, bank: (
                        dve.wait_ge(sem("w_used"), n * 2 + 2),
                        dve.tensor_scalar(fscr[0:16, 5, :], ps[bank][0:16, 0:S], bf[:, 0:1], None, ALU.add).then_inc(sem(f"proj_out{bank}"), 1)))
                    phase_done(dve, "ff")
                    ch.after(dve.tensor_scalar(fscr[0:16, 7, :], fscr[0:16, 5, :], -1.0, 0.0, ALU.mult, ALU.max))
                    dve.tensor_copy(fscr[0:16, 8, :], fscr[0:16, 7, :]).then_inc(*once("f_in"))
                    dve.wait_ge(*after("f_ln"))
                    ch.after(dve.tensor_tensor(fscr[0:16, 7, :], fscr[0:16, 7, :], fscr[0:16, 6, :], ALU.add))
                    ch.after(dve.tensor_tensor_scan(cneg, ones[0:16, 0:1].broadcast_to([16, S]), fscr[0:16, 7, :], 0.0, ALU.mult, ALU.add))
                    dve.tensor_scalar(cpos, cneg, -1.0, None, ALU.mult).then_inc(*once("f_c"))

                    def turned():
                        dve.wait_ge(*after("f_t"))
                        dve.tensor_copy(fscr[:, 2, 0:32], q[0][:, 0:32]).then_inc(*once("f_ready"))
                        dve.wait_ge(*after("f_ready"))

                    fused_vector(dve, turned)
                    stream(dve, "fo", out_resid(dve))
                if stop >= lim:
                    norm_vector(dve, f"ffn{layer}")
                    for up, dn, idx in mlp(layer):
                        stream(dve, up, relu_vector(dve, idx))
                        stream(dve, dn, out_resid(dve))
            norm_vector(dve, "final2")
            for u in range(0, 8, 2):
                dve.wait_ge(sem("fin_t"), u + 1)
                dve.tensor_copy(otok[:, u // 4, 512 * (u % 4):512 * (u % 4) + 512], q[u % 4][:, :]).then_inc(sem("fin_d"), 1)

        @block.tensor
        def _(pe):
            pe.wait_ge(*after("ident"))
            for u in range(16):
                pe.wait_ge(sem("mem_in" if u < 8 else "x_in"), 16)
                if u > 3:
                    pe.wait_ge(sem("tr_a" if u % 2 else "tr_d"), (u - 4) // 2 + 1)
                tok = mtok if u < 8 else xtok
                for x in range(4):
                    k, b = 2 * (u % 8) + x // 2, x % 2
                    mm = pe.transpose(q[u % 4][:, P * x:P * x + P], tok[:, b, P * k:P * k + P], ident[:])
                mm.then_inc(sem("tr"), 1)
            pe.wait_ge(sem("prow_in"), 16 * len(rows))
            for x in range(NROW):
                mm = pe.transpose(q[4][:, P * x:P * x + P], prow[:, x, :], ident[:])
            mm.then_inc(*once("prm_t"))
            norm_tensor(pe, "mix")
            project(pe, "in_a", BH, BL, norm_ready("mix"), lambda: norm_tensor(pe, "mem"))
            for name in ("in_r", "in_b"):
                project(pe, name, BH, BL, norm_ready("mix"))
            pe.wait_ge(sem("small_in"), 32)
            sb_tensor(pe)
            gla_tensor(pe)
            sgu_tensor(pe)
            mix_tensor(pe)
            project(pe, "out", BH, BL, ("mix_done", lambda g: g + 1))
            if stop >= 2:
                norm_tensor(pe, "xattn")
                project(pe, "xq", AH, AL, norm_ready("xattn"))
                phase_done(pe, "xq")
                att_tensor(pe, "xa")
                pe.wait_ge(sem("att_out"), 6)
                for hc in range(8):
                    n = N0["xo"] + hc // 2
                    slot = 2 * (n % 2) + hc % 2
                    pe.wait_ge(sem("w_lo"), 2 * N0["xo"] + hc + 1)
                    if hc > 1:
                        pe.wait_ge(sem("xo_out"), hc - 1)
                    for o in range(2):
                        dst = q[hc % 2][:, S * o:S * o + S]
                        for k in range(4):
                            h_, l_ = (w[slot][:, :, :].rearrange("p k n -> p (k n)")[:, S * k + P * o:S * k + P * o + P] for w in (wh, wl))
                            pe.matmul(dst, h_, BH[:, k, :], start=k == 0, stop=False)
                            pe.matmul(dst, h_, BL[:, k, :], start=False, stop=False)
                            mm = pe.matmul(dst, l_, BH[:, k, :], start=False, stop=k == 3)
                    mm.then_inc(sem("w_used"), 1)
                pe.wait_ge(sem("xo_out"), 8)
            if stop >= 3:
                norm_tensor(pe, "final1")
                norm_tensor(pe, "rwkv")
                for name, mix in (("rw_r", "r"), ("rw_k", "k"), ("rw_v", "v"), ("rw_w1", "w"), ("rw_a1", "a"), ("rw_g1", "g")):
                    d = MIXES[mix][2]
                    project(pe, name, d[0], d[1], xs_ready(mix))
                up_tensor(pe)
                pe.wait_ge(sem("up_out"), 12)
                rw_tensor(pe)
                pe.wait_ge(sem("rw_out"), 20)
                project(pe, "rw_o", AH, AL)
            for layer, lim in ((0, 4), (1, 6)):
                if layer == 1 and stop >= 5:
                    norm_tensor(pe, "kv")
                    norm_tensor(pe, "fox")
                    for name in ("fk", "fv", "ff"):
                        project(pe, name, AH, AL, norm_ready("kv"))

                    def forget():
                        pe.wait_ge(*after("f_c"))
                        for b in range(2):
                            mm = pe.transpose(q[0][:, 16 * b:16 * b + 16], cpos[:, P * b:P * b + P], ident[0:16, 0:16])
                        mm.then_inc(*once("f_t"))
                        pe.wait_ge(*after("f_ready"))

                    fused_tensor(pe, project(pe, "fq", BH, BL, norm_ready("fox")), forget)
                    pe.wait_ge(sem("att_out"), 22)
                    project(pe, "fo", AH, AL)
                if stop >= lim:
                    norm_tensor(pe, f"ffn{layer}")
                    for up, dn, idx in mlp(layer):
                        project(pe, up, AH, AL, norm_ready(f"ffn{layer}"))
                        project(pe, dn, BH, BL, ("hid_done", lambda g, idx=idx: idx + 4 * g + 4))
            norm_tensor(pe, "final2")
            norm_all(pe, "final2")
            for u in range(8):
                if u > 3:
                    pe.wait_ge(sem("fin_a" if u % 2 else "fin_d"), (u - 4) // 2 + 1)
                for x in range(4):
                    mm = pe.transpose(q[u % 4][:, P * x:P * x + P], X[:, 4 * (u % 4) + x, P * (u // 4):P * (u // 4) + P], ident[:])
                mm.then_inc(sem("fin_t"), 1)


def kernel(**inputs):
    import numpy as _np
    import concourse.bacc as _bacc
    from concourse import mybir as _mybir
    from concourse.bass_utils import run_bass_kernel_spmd as _run

    nc = _bacc.Bacc("TRN2", target_bir_lowering=False, num_devices=1)
    arrays, args = {}, {}
    for name, value in inputs.items():
        value = _np.ascontiguousarray(value)
        if value.size == 0:
            continue
        arrays[f"in_{name}_dram"] = value
        args[name] = nc.dram_tensor(f"in_{name}_dram", value.shape, _mybir.dt.from_np(value.dtype), kind="ExternalInput").ap()
    out = nc.dram_tensor("out_0_dram", (1, S, D), F32, kind="ExternalOutput").ap()
    two_block_kernel(nc, args, out, 6)
    r = _run(nc, [arrays], core_ids=[0])
    return r.results[0]["out_0_dram"]
```
